# Optimizing a Trainium2 kernel written in Bass

```python
import math
import jax, jax.numpy as jnp
from jax import lax
import numpy as np

D_MODEL = 1024
BATCH = 1
SEQ = 512
DEPTH = 2

N_A_LAYERS = DEPTH // 2
N_B_LAYERS = DEPTH - N_A_LAYERS
SSM_GROUP = 16
SSM_GROUPS = D_MODEL // SSM_GROUP
SSM_STATE = 64
SSM_CHUNK = 128
DT_MIN = 1e-3
DT_MAX = 1e-1
HEAD_DIM = 64
N_HEADS = D_MODEL // HEAD_DIM
N_KV_HEADS = N_HEADS // 4
GQA_GROUP = N_HEADS // N_KV_HEADS
WINDOW = 128
ATTN_BLOCK = 128
ROPE_THETA = 500000.0
ROT_DIM = HEAD_DIM // 4
D_FF = 4 * D_MODEL
PLE_DIM = 256
RMS_EPS = 1e-6
NEG_INF = -1e30


def rmsnorm(x, g):
    xf = x.astype(jnp.float32)
    y = xf * lax.rsqrt(jnp.mean(xf * xf, axis=-1, keepdims=True) + RMS_EPS)
    return (y * g.astype(jnp.float32)).astype(x.dtype)

def partial_rope(x, pos):
    inv = ROPE_THETA ** (-jnp.arange(0, ROT_DIM, 2, dtype=jnp.float32) / ROT_DIM)
    ang = pos.astype(jnp.float32)[:, None] * inv[None, :]
    cos = jnp.cos(ang)[None, :, None, :]
    sin = jnp.sin(ang)[None, :, None, :]
    xr = x[..., :ROT_DIM].astype(jnp.float32)
    x1, x2 = xr[..., :ROT_DIM // 2], xr[..., ROT_DIM // 2:]
    rot = jnp.concatenate([x1 * cos - x2 * sin, x2 * cos + x1 * sin], axis=-1).astype(x.dtype)
    return jnp.concatenate([rot, x[..., ROT_DIM:]], axis=-1)

def s5_mixer(u, lam_re, lam_im, log_dt, b_re, b_im, c_re, c_im, d, w_glu):
    bsz, seqlen, dm = u.shape
    f32 = jnp.float32
    lam_re = lam_re.astype(f32); lam_im = lam_im.astype(f32)
    b_re = b_re.astype(f32); b_im = b_im.astype(f32)
    c_re = c_re.astype(f32); c_im = c_im.astype(f32)
    dt = jnp.exp(log_dt.astype(f32))[:, None]
    mag = jnp.exp(lam_re * dt)
    a_r = mag * jnp.cos(lam_im * dt)
    a_i = mag * jnp.sin(lam_im * dt)
    den = lam_re * lam_re + lam_im * lam_im
    nr = a_r - 1.0
    coef_r = (nr * lam_re + a_i * lam_im) / den
    coef_i = (a_i * lam_re - nr * lam_im) / den
    bb_r = coef_r[..., None] * b_re - coef_i[..., None] * b_im
    bb_i = coef_r[..., None] * b_im + coef_i[..., None] * b_re

    n_chunks = seqlen // SSM_CHUNK
    ug = u.astype(f32).reshape(bsz, n_chunks, SSM_CHUNK, SSM_GROUPS, SSM_GROUP)
    ug = jnp.transpose(ug, (1, 0, 2, 3, 4))

    def combine(e1, e2):
        a1r, a1i, s1r, s1i = e1
        a2r, a2i, s2r, s2i = e2
        return (a2r * a1r - a2i * a1i,
                a2r * a1i + a2i * a1r,
                a2r * s1r - a2i * s1i + s2r,
                a2r * s1i + a2i * s1r + s2i)

    def chunk_step(carry, uc):
        cr, ci = carry
        bur = jnp.einsum('gnh,btgh->btgn', bb_r, uc)
        bui = jnp.einsum('gnh,btgh->btgn', bb_i, uc)
        ar = jnp.broadcast_to(a_r, bur.shape)
        ai = jnp.broadcast_to(a_i, bui.shape)
        pr, pi, sr, si = lax.associative_scan(combine, (ar, ai, bur, bui), axis=1)
        xr = sr + pr * cr[:, None] - pi * ci[:, None]
        xi = si + pr * ci[:, None] + pi * cr[:, None]
        y = jnp.einsum('ghn,btgn->btgh', c_re, xr) - jnp.einsum('ghn,btgn->btgh', c_im, xi)
        return (xr[:, -1], xi[:, -1]), y

    init = (jnp.zeros((bsz, SSM_GROUPS, SSM_STATE), f32), jnp.zeros((bsz, SSM_GROUPS, SSM_STATE), f32))
    _, ys = lax.scan(chunk_step, init, ug)
    y = jnp.transpose(ys, (1, 0, 2, 3, 4)).reshape(bsz, seqlen, dm)
    y = y + d.astype(f32) * u.astype(f32)
    y = jax.nn.gelu(y).astype(u.dtype)
    ab = y @ w_glu
    a, b = ab[..., :dm], ab[..., dm:]
    return a * jax.nn.sigmoid(b)

def swa_sink_attention(q, k, v, sinks):
    bsz, seqlen = q.shape[0], q.shape[1]
    nb = seqlen // ATTN_BLOCK
    f32 = jnp.float32
    qb = q.astype(f32).reshape(bsz, nb, ATTN_BLOCK, N_KV_HEADS, GQA_GROUP, HEAD_DIM)
    kb = k.astype(f32).reshape(bsz, nb, ATTN_BLOCK, N_KV_HEADS, HEAD_DIM)
    vb = v.astype(f32).reshape(bsz, nb, ATTN_BLOCK, N_KV_HEADS, HEAD_DIM)
    k_prev = jnp.concatenate([jnp.zeros_like(kb[:, :1]), kb[:, :-1]], axis=1)
    v_prev = jnp.concatenate([jnp.zeros_like(vb[:, :1]), vb[:, :-1]], axis=1)
    kk = jnp.concatenate([k_prev, kb], axis=2)
    vv = jnp.concatenate([v_prev, vb], axis=2)
    s = jnp.einsum('bnqkgd,bnjkd->bnkgqj', qb, kk) * (HEAD_DIM ** -0.5)
    qi = jnp.arange(ATTN_BLOCK)[:, None] + ATTN_BLOCK
    kj = jnp.arange(2 * ATTN_BLOCK)[None, :]
    band = (kj <= qi) & (qi - kj < WINDOW)
    has_prev = jnp.arange(nb) > 0
    mask = band[None] & ((kj >= ATTN_BLOCK)[None] | has_prev[:, None, None])
    s = jnp.where(mask[None, :, None, None], s, NEG_INF)
    sink = sinks.astype(f32).reshape(1, 1, N_KV_HEADS, GQA_GROUP, 1, 1)
    m = jnp.maximum(jnp.max(s, axis=-1, keepdims=True), sink)
    pr = jnp.exp(s - m)
    w = pr / (jnp.sum(pr, axis=-1, keepdims=True) + jnp.exp(sink - m))
    o = jnp.einsum('bnkgqj,bnjkd->bnqkgd', w, vv)
    return o.reshape(bsz, seqlen, N_HEADS * HEAD_DIM).astype(q.dtype)

def first_inputs(seed: int = 0) -> dict:
    key = jax.random.key(seed)
    ks = jax.random.split(key, 32)
    f32 = jnp.float32
    nrm = lambda k, shape, scale: jax.random.normal(k, shape, f32) * scale
    x = nrm(ks[0], (BATCH, SEQ, D_MODEL), 1.0)
    p = nrm(ks[1], (DEPTH, BATCH, SEQ, PLE_DIM), 1.0)
    norm_mix = 1.0 + nrm(ks[2], (DEPTH, D_MODEL), 0.02)
    ssm_lambda_re = -0.5 + nrm(ks[3], (N_A_LAYERS, SSM_GROUPS, SSM_STATE), 0.01)
    ssm_lambda_im = (jnp.pi * jnp.arange(SSM_STATE, dtype=f32))[None, None, :] + nrm(ks[4], (N_A_LAYERS, SSM_GROUPS, SSM_STATE), 0.01)
    ssm_log_dt = math.log(DT_MIN) + jax.random.uniform(ks[5], (N_A_LAYERS, SSM_GROUPS), f32) * (math.log(DT_MAX) - math.log(DT_MIN))
    ssm_b_re = nrm(ks[6], (N_A_LAYERS, SSM_GROUPS, SSM_STATE, SSM_GROUP), (2 * SSM_GROUP) ** -0.5)
    ssm_b_im = nrm(ks[7], (N_A_LAYERS, SSM_GROUPS, SSM_STATE, SSM_GROUP), (2 * SSM_GROUP) ** -0.5)
    ssm_c_re = nrm(ks[8], (N_A_LAYERS, SSM_GROUPS, SSM_GROUP, SSM_STATE), (2 * SSM_STATE) ** -0.5)
    ssm_c_im = nrm(ks[9], (N_A_LAYERS, SSM_GROUPS, SSM_GROUP, SSM_STATE), (2 * SSM_STATE) ** -0.5)
    ssm_d = nrm(ks[10], (N_A_LAYERS, D_MODEL), 1.0)
    ssm_w_glu = nrm(ks[11], (N_A_LAYERS, D_MODEL, 2 * D_MODEL), D_MODEL ** -0.5)
    kv_norm = 1.0 + nrm(ks[12], (D_MODEL,), 0.02)
    w_k = nrm(ks[13], (D_MODEL, N_KV_HEADS * HEAD_DIM), D_MODEL ** -0.5)
    w_v = nrm(ks[14], (D_MODEL, N_KV_HEADS * HEAD_DIM), D_MODEL ** -0.5)
    w_q = nrm(ks[15], (N_B_LAYERS, D_MODEL, N_HEADS * HEAD_DIM), D_MODEL ** -0.5)
    attn_sinks = nrm(ks[16], (N_B_LAYERS, N_HEADS), 0.5)
    w_o = nrm(ks[17], (N_B_LAYERS, N_HEADS * HEAD_DIM, D_MODEL), (N_HEADS * HEAD_DIM) ** -0.5)
    norm_mlp = 1.0 + nrm(ks[18], (DEPTH, D_MODEL), 0.02)
    w_up = nrm(ks[19], (DEPTH, D_MODEL, D_FF), D_MODEL ** -0.5)
    w_down = nrm(ks[20], (DEPTH, D_FF, D_MODEL), D_FF ** -0.5)
    norm_ple = 1.0 + nrm(ks[21], (DEPTH, D_MODEL), 0.02)
    w_ple_gate = nrm(ks[22], (DEPTH, D_MODEL, D_MODEL), D_MODEL ** -0.5)
    w_ple_proj = nrm(ks[23], (DEPTH, PLE_DIM, D_MODEL), PLE_DIM ** -0.5)
    norm_final = 1.0 + nrm(ks[24], (D_MODEL,), 0.02)
    return {'x': x, 'p': p, 'norm_mix': norm_mix,
            'ssm_lambda_re': ssm_lambda_re, 'ssm_lambda_im': ssm_lambda_im, 'ssm_log_dt': ssm_log_dt,
            'ssm_b_re': ssm_b_re, 'ssm_b_im': ssm_b_im, 'ssm_c_re': ssm_c_re, 'ssm_c_im': ssm_c_im,
            'ssm_d': ssm_d, 'ssm_w_glu': ssm_w_glu,
            'kv_norm': kv_norm, 'w_k': w_k, 'w_v': w_v, 'w_q': w_q, 'attn_sinks': attn_sinks, 'w_o': w_o,
            'norm_mlp': norm_mlp, 'w_up': w_up, 'w_down': w_down,
            'norm_ple': norm_ple, 'w_ple_gate': w_ple_gate, 'w_ple_proj': w_ple_proj,
            'norm_final': norm_final}

def first_block(x, p, norm_mix, ssm_lambda_re, ssm_lambda_im, ssm_log_dt, ssm_b_re, ssm_b_im,
              ssm_c_re, ssm_c_im, ssm_d, ssm_w_glu, kv_norm, w_k, w_v, w_q, attn_sinks, w_o,
              norm_mlp, w_up, w_down, norm_ple, w_ple_gate, w_ple_proj, norm_final):
    bsz, seqlen, _ = x.shape
    pos = jnp.arange(seqlen, dtype=jnp.int32)
    h = x
    k_shared = None
    v_shared = None
    for i in range(DEPTH):
        hn = rmsnorm(h, norm_mix[i])
        if i < N_A_LAYERS:
            mix = s5_mixer(hn, ssm_lambda_re[i], ssm_lambda_im[i], ssm_log_dt[i], ssm_b_re[i], ssm_b_im[i],
                           ssm_c_re[i], ssm_c_im[i], ssm_d[i], ssm_w_glu[i])
        else:
            j = i - N_A_LAYERS
            q = (hn @ w_q[j]).reshape(bsz, seqlen, N_HEADS, HEAD_DIM)
            q = partial_rope(q, pos)
            mix = swa_sink_attention(q, k_shared, v_shared, attn_sinks[j]) @ w_o[j]
        h = h + mix
        hm = rmsnorm(h, norm_mlp[i])
        h = h + jnp.square(jax.nn.relu(hm @ w_up[i])) @ w_down[i]
        gate = jax.nn.sigmoid(rmsnorm(h, norm_ple[i]) @ w_ple_gate[i])
        h = h + gate * (p[i] @ w_ple_proj[i])
        if i == N_A_LAYERS - 1:
            hk = rmsnorm(h, kv_norm)
            k_shared = partial_rope((hk @ w_k).reshape(bsz, seqlen, N_KV_HEADS, HEAD_DIM), pos)
            v_shared = (hk @ w_v).reshape(bsz, seqlen, N_KV_HEADS, HEAD_DIM)
    return rmsnorm(h, norm_final)


RET_HEADS = 8
RET_DK = 64
RET_DV = 128
RET_CHUNK = 128
CONV_W = 1024
CONV_K = 3
MLA_HEADS = 8
MLA_NOPE = 128
MLA_ROPE = 64
MLA_DV = 128
Q_LORA = 384
KV_LORA = 256
ROPE_BASE = 10000.0
EPS = 1e-6
N_EVEN = (DEPTH + 1) // 2
N_ODD = DEPTH // 2

RET_QK = RET_HEADS * RET_DK
RET_V = RET_HEADS * RET_DV
EVEN_SPLITS = (RET_QK, RET_QK, RET_V, RET_V, CONV_W, CONV_W, CONV_W, CONV_W)
EVEN_IN = sum(EVEN_SPLITS)
EVEN_MIX = RET_V + CONV_W
MLA_QK = MLA_NOPE + MLA_ROPE
MLA_V = MLA_HEADS * MLA_DV
ODD_SPLITS = (Q_LORA, KV_LORA, MLA_ROPE, MLA_V)
ODD_IN = sum(ODD_SPLITS)


def rms_norm(x, g):
    xf = x.astype(jnp.float32)
    y = xf * lax.rsqrt(jnp.mean(xf * xf, axis=-1, keepdims=True) + EPS)
    return (y * g.astype(jnp.float32)).astype(x.dtype)

def rope(x, positions):
    d = x.shape[-1]
    inv = ROPE_BASE ** (-jnp.arange(0, d, 2, dtype=jnp.float32) / d)
    ang = positions.astype(jnp.float32)[..., None] * inv
    cos = jnp.cos(ang)[:, :, None, :]
    sin = jnp.sin(ang)[:, :, None, :]
    xf = x.astype(jnp.float32)
    x1, x2 = xf[..., : d // 2], xf[..., d // 2:]
    out = jnp.concatenate([x1 * cos - x2 * sin, x1 * sin + x2 * cos], axis=-1)
    return out.astype(x.dtype)

def split_cols(h, sizes):
    return jnp.split(h, np.cumsum(sizes)[:-1].tolist(), axis=-1)

def retention(q, k, v):
    b, s, h, dk = q.shape
    dv = v.shape[-1]
    c = RET_CHUNK
    n = s // c
    dt = q.dtype
    log_gamma = jnp.log1p(-jnp.exp2(-5.0 - jnp.arange(h, dtype=jnp.float32)))
    i = jnp.arange(c, dtype=jnp.float32)
    rel = i[:, None] - i[None, :]
    intra = jnp.where(rel >= 0, jnp.exp(log_gamma[:, None, None] * jnp.maximum(rel, 0.0)), 0.0).astype(dt)
    xi = jnp.exp(log_gamma[:, None] * (i + 1.0)).astype(dt)
    zeta = jnp.exp(log_gamma[:, None] * (c - 1.0 - i)).astype(dt)
    gamma_c = jnp.exp(log_gamma * c).astype(dt)
    qc = q.reshape(b, n, c, h, dk)
    kc = k.reshape(b, n, c, h, dk)
    vc = v.reshape(b, n, c, h, dv)
    scores = jnp.einsum('bnihd,bnjhd->bnhij', qc, kc) * intra
    inner = jnp.einsum('bnhij,bnjhe->bnihe', scores, vc)
    kv = jnp.einsum('bnjhd,hj,bnjhe->nbhde', kc, zeta, vc)

    def step(state, kv_i):
        return gamma_c[None, :, None, None] * state + kv_i, state

    _, prev = lax.scan(step, jnp.zeros((b, h, dk, dv), dt), kv)
    cross = jnp.einsum('bnihd,nbhde,hi->bnihe', qc, prev, xi)
    return (inner + cross).reshape(b, s, h, dv)

def short_conv(u, w, bias):
    s = u.shape[1]
    up = jnp.pad(u, ((0, 0), (CONV_K - 1, 0), (0, 0)))
    out = up[:, 0:s] * w[0]
    for tap in range(1, CONV_K):
        out = out + up[:, tap:tap + s] * w[tap]
    return out + bias

def even_layer(h, positions, w_in, conv_w, conv_b, gn, w_out):
    b, s, _ = h.shape
    q, k, v, g_ret, cb, cc, cx, g_conv = split_cols(h @ w_in, EVEN_SPLITS)
    q = rope(q.reshape(b, s, RET_HEADS, RET_DK), positions)
    k = rope(k.reshape(b, s, RET_HEADS, RET_DK), positions) * (RET_DK ** -0.5)
    v = v.reshape(b, s, RET_HEADS, RET_DV)
    r = retention(q, k, v)
    r = rms_norm(r, gn.reshape(RET_HEADS, RET_DV)).reshape(b, s, RET_V)
    y_conv = cb * short_conv(cc * cx, conv_w, conv_b)
    mix = jnp.concatenate([r * jax.nn.silu(g_ret), y_conv * jax.nn.silu(g_conv)], axis=-1)
    return mix @ w_out

def causal_mla_attention(q_nope, q_rope, k_nope, k_rope, v):
    s = q_nope.shape[1]
    scale = MLA_QK ** -0.5
    outs = []
    for blk in range(s // ATTN_BLOCK):
        lo, hi = blk * ATTN_BLOCK, (blk + 1) * ATTN_BLOCK
        sc = (jnp.einsum('bqhd,bkhd->bhqk', q_nope[:, lo:hi].astype(jnp.float32), k_nope[:, :hi].astype(jnp.float32))
              + jnp.einsum('bqhd,bkd->bhqk', q_rope[:, lo:hi].astype(jnp.float32), k_rope[:, :hi].astype(jnp.float32))) * scale
        qpos = lo + jnp.arange(ATTN_BLOCK)
        kpos = jnp.arange(hi)
        sc = jnp.where(kpos[None, :] <= qpos[:, None], sc, -jnp.inf)
        p = jax.nn.softmax(sc, axis=-1).astype(v.dtype)
        outs.append(jnp.einsum('bhqk,bkhd->bqhd', p, v[:, :hi]))
    return jnp.concatenate(outs, axis=1)

def odd_layer(h, positions, w_in, q_a_norm, w_qb, kv_a_norm, w_kvb, w_out):
    b, s, _ = h.shape
    cq, ckv, k_rope, gate = split_cols(h @ w_in, ODD_SPLITS)
    q = (rms_norm(cq, q_a_norm) @ w_qb).reshape(b, s, MLA_HEADS, MLA_QK)
    q_nope = q[..., :MLA_NOPE]
    q_rope = rope(q[..., MLA_NOPE:], positions)
    kv = (rms_norm(ckv, kv_a_norm) @ w_kvb).reshape(b, s, MLA_HEADS, MLA_NOPE + MLA_DV)
    k_nope, v = kv[..., :MLA_NOPE], kv[..., MLA_NOPE:]
    k_rope = rope(k_rope[:, :, None, :], positions)[:, :, 0]
    o = causal_mla_attention(q_nope, q_rope, k_nope, k_rope, v)
    return (o.reshape(b, s, MLA_V) * jax.nn.silu(gate)) @ w_out

def second_inputs(seed: int = 0) -> dict:
    key = jax.random.key(seed)
    ks = jax.random.split(key, 16)
    f32 = jnp.float32
    nrm = lambda k, shape, scale: jax.random.normal(k, shape, f32) * scale
    x = jax.random.normal(ks[0], (BATCH, SEQ, D_MODEL), f32)
    offsets = jax.random.randint(ks[1], (BATCH, 1), 0, 1024, dtype=jnp.int32)
    positions = (offsets + jnp.arange(SEQ, dtype=jnp.int32)[None, :]).astype(jnp.int32)
    pre_norm = 1.0 + nrm(ks[2], (DEPTH, D_MODEL), 0.02)
    post_norm = 1.0 + nrm(ks[3], (DEPTH, D_MODEL), 0.02)
    even_w_in = nrm(ks[4], (N_EVEN, D_MODEL, EVEN_IN), D_MODEL ** -0.5)
    even_conv_w = nrm(ks[5], (N_EVEN, CONV_K, CONV_W), CONV_K ** -0.5)
    even_conv_b = nrm(ks[6], (N_EVEN, CONV_W), 0.01)
    ret_gn = 1.0 + nrm(ks[7], (N_EVEN, RET_V), 0.02)
    even_w_out = nrm(ks[8], (N_EVEN, EVEN_MIX, D_MODEL), EVEN_MIX ** -0.5)
    odd_w_in = nrm(ks[9], (N_ODD, D_MODEL, ODD_IN), D_MODEL ** -0.5)
    q_a_norm = 1.0 + nrm(ks[10], (N_ODD, Q_LORA), 0.02)
    w_qb = nrm(ks[11], (N_ODD, Q_LORA, MLA_HEADS * MLA_QK), Q_LORA ** -0.5)
    kv_a_norm = 1.0 + nrm(ks[12], (N_ODD, KV_LORA), 0.02)
    w_kvb = nrm(ks[13], (N_ODD, KV_LORA, MLA_HEADS * (MLA_NOPE + MLA_DV)), KV_LORA ** -0.5)
    odd_w_out = nrm(ks[14], (N_ODD, MLA_V, D_MODEL), MLA_V ** -0.5)
    return {"x": x, "positions": positions, "pre_norm": pre_norm, "post_norm": post_norm,
            "even_w_in": even_w_in, "even_conv_w": even_conv_w, "even_conv_b": even_conv_b,
            "ret_gn": ret_gn, "even_w_out": even_w_out, "odd_w_in": odd_w_in,
            "q_a_norm": q_a_norm, "w_qb": w_qb, "kv_a_norm": kv_a_norm, "w_kvb": w_kvb,
            "odd_w_out": odd_w_out}

def second_block(x, positions, pre_norm, post_norm, even_w_in, even_conv_w, even_conv_b, ret_gn,
              even_w_out, odd_w_in, q_a_norm, w_qb, kv_a_norm, w_kvb, odd_w_out):
    h = x
    for layer in range(DEPTH):
        u = rms_norm(h, pre_norm[layer])
        if layer % 2 == 0:
            e = layer // 2
            y = even_layer(u, positions, even_w_in[e], even_conv_w[e], even_conv_b[e], ret_gn[e], even_w_out[e])
        else:
            o = layer // 2
            y = odd_layer(u, positions, odd_w_in[o], q_a_norm[o], w_qb[o], kv_a_norm[o], w_kvb[o], odd_w_out[o])
        h = h + rms_norm(y, post_norm[layer])
    return h


def setup_inputs(seed=0):
    out = dict(first_inputs(seed))
    for name, value in second_inputs(seed + 1).items():
        if name != "x":
            out[name + "_2"] = value
    return out


def reference(
    x, p, norm_mix, ssm_lambda_re, ssm_lambda_im, ssm_log_dt, ssm_b_re, ssm_b_im, ssm_c_re,
    ssm_c_im, ssm_d, ssm_w_glu, kv_norm, w_k, w_v, w_q, attn_sinks, w_o, norm_mlp, w_up, w_down,
    norm_ple, w_ple_gate, w_ple_proj, norm_final, positions_2, pre_norm_2, post_norm_2,
    even_w_in_2, even_conv_w_2, even_conv_b_2, ret_gn_2, even_w_out_2, odd_w_in_2, q_a_norm_2,
    w_qb_2, kv_a_norm_2, w_kvb_2, odd_w_out_2,
):
    x = first_block(
        x, p, norm_mix, ssm_lambda_re, ssm_lambda_im, ssm_log_dt, ssm_b_re, ssm_b_im, ssm_c_re,
        ssm_c_im, ssm_d, ssm_w_glu, kv_norm, w_k, w_v, w_q, attn_sinks, w_o, norm_mlp, w_up,
        w_down, norm_ple, w_ple_gate, w_ple_proj, norm_final,
    )
    return second_block(
        x, positions_2, pre_norm_2, post_norm_2, even_w_in_2, even_conv_w_2, even_conv_b_2,
        ret_gn_2, even_w_out_2, odd_w_in_2, q_a_norm_2, w_qb_2, kv_a_norm_2, w_kvb_2,
        odd_w_out_2,
    )


_drawn_inputs = setup_inputs


def setup_inputs(seed=0):
    import zlib

    import numpy as np

    out = dict(_drawn_inputs(seed))
    spreads = {}
    factors = {'norm_mix': 3.442,
     'ssm_lambda_re': 8.0,
     'kv_norm': 5.161,
     'attn_sinks': 3.323,
     'norm_ple': 8.0,
     'post_norm_2': 2.852,
     'even_conv_b_2': 8.0,
     'ret_gn_2': 5.016,
     'q_a_norm_2': 8.0,
     'kv_a_norm_2': 4.708}
    for name, (base, spread) in spreads.items():
        noise = np.random.default_rng([zlib.crc32(name.encode()), seed]).standard_normal(out[name].shape)
        drawn = base * np.exp(spread * noise) if base else spread * noise
        out[name] = __import__('jax').numpy.asarray(drawn.astype(out[name].dtype))
    for name, factor in factors.items():
        out[name] = (out[name] * factor).astype(out[name].dtype)
    return out
```

```python
from contextlib import ExitStack

import numpy as np

import concourse.bass as bass
from concourse import mybir

F32 = mybir.dt.float32
FR = mybir.dt.float32r
I32 = mybir.dt.int32
ALU = mybir.AluOpType
ACT = mybir.ActivationFunctionType
AX_X = mybir.AxisListType.X

P = 128
TOK = 512
D = 1024
KT = D // P
FF = 4 * D
CHUNKS = FF // D
PLE = 256
EPS = 1e-6
NEG = -1e30

GR, GH, NST = 64, 16, 64
ST = P // GH
NC = TOK // ST
SG = 8
NSL = GR // SG
W8 = SG * P

HD, NKV, GQA, WIN = 64, 4, 4, 128
NB = TOK // P
RH, RDK = 8, 64
MH, MN, MR = 8, 128, 64
QL, KL = 384, 256

RING = 4
LEAD = RING - 1

PHASES = [
    ("proj0", 2, 4), ("glu", 16, 1),
    *[(f"{k}0_{c}", 8, 1) for k, c in (("up", 0), ("up", 1), ("down", 0), ("up", 2), ("down", 1), ("up", 3), ("down", 2), ("down", 3))],
    ("gate0", 8, 1), ("kv", 4, 1), ("q", 8, 1), ("wo", 8, 1), ("proj1", 2, 4),
    *[(f"{k}1_{c}", 8, 1) for k, c in (("up", 0), ("up", 1), ("down", 0), ("up", 2), ("down", 1), ("up", 3), ("down", 2), ("down", 3))],
    ("gate1", 8, 1), ("even", 56, 1), ("eout", 16, 1), ("odd", 14, 1), ("qb", 6, 2), ("kvb", 4, 4), ("oout", 8, 1),
]
N_OUT = {"eout": 8}
S0, SEG0, OUT0, NSTR, SEGS = {}, {}, {}, {}, {}
_s = _g = _o = 0
for _name, _n, _k in PHASES:
    S0[_name], SEG0[_name], OUT0[_name], NSTR[_name], SEGS[_name] = _s, _g, _o, _n, _k
    _s, _g, _o = _s + _n, _g + _n * _k, _o + N_OUT.get(_name, _n * _k)
NS = _s
assert NS % RING == 0

XT = {}
_x = 0
for _name, _n in [("p0", 2), ("y", 8), ("mlp0", 8), ("hid0_0", 8), ("hid0_1", 8), ("hid0_2", 8), ("hid0_3", 8), ("gate0", 8),
                  ("kvq", 16), ("o", 8), ("mlp1", 8), ("p1", 2), ("hid1_0", 8), ("hid1_1", 8), ("hid1_2", 8), ("hid1_3", 8),
                  ("gate1", 8), ("even", 8), ("conv", 8), ("ret", 8), ("odd", 8), ("lat", 5), ("oo", 8)]:
    XT[_name] = _x
    _x += _n

CC = {}
_c = 0
for _name, _n in [("ident", P), ("perm1", P), ("perm2", P), ("permz", P), ("ones", P),
                  ("eps", 1), ("halfpi", 1), ("sgn", 1), ("nsgn", 1), ("inv", 1), ("gam", 4), ("zeta", RH)]:
    CC[_name] = slice(_c, _c + _n)
    _c += _n
NCC = _c
GC = {}
_c = 0
for _name, _n in [("mix1", 8), ("kvn", 8), ("mlp0", 8), ("mlp1", 8), ("ple0", 8), ("ple1", 8), ("fin", 8), ("pre0", 8), ("pre1", 8),
                  ("post0", 8), ("post1", 8), ("gn", 8), ("qa", 3), ("kva", 2), ("cw", 24), ("cb", 8), ("sink", 16)]:
    GC[_name] = slice(_c, _c + _n)
    _c += _n
NGC = _c

TWO_PI = 2 * np.pi
ROUND = 12582912.0
PI_A = 6.28125
PI_B = float(np.float32(np.round((TWO_PI - PI_A) * 2**20) / 2**20))
PI_C = float(TWO_PI - PI_A - PI_B)
PI_IN = 3.1415925


class Chain:

    def __init__(self, eng, sem):
        self.eng, self.sem, self.n, self.at = eng, sem, 0, None

    def now(self):
        return self.n if self.at is None else self.n + self.at[0] * self.at[1]

    def link(self, ins):
        ins.then_inc(self.sem, 1)
        self.n += 1
        self.eng.wait_ge(self.sem, self.now())

    def each(self, i, per):
        self.at, self.first = (i, per), self.n

    def done(self, count):
        assert self.n - self.first == self.at[1], (self.n - self.first, self.at[1])
        self.n, self.at = self.first + self.at[1] * count, None


def program(nc, a):
    with ExitStack() as top:
        def sem(name):
            return top.enter_context(nc.semaphore(name))

        def area(stack, name, shape, dt=F32):
            return stack.enter_context(nc.sbuf_tensor(name, shape, dt))

        ps = top.enter_context(nc.psum_tensor("ps", [P, 8, 512], F32))
        NRM, SX, SY, SZ = 4, 5, 6, 7
        raw = area(top, "raw", [P, RING, D])
        cst = area(top, "cst", [P, NCC])
        gp = area(top, "gp", [P, NGC])
        with ExitStack() as s5:
            lam = area(s5, "lam", [P, 3, GR])
            tab = area(s5, "tab", [P, 24, GR])
            pwr = area(s5, "pwr", [P, ST + 1, GR])
            pwi = area(s5, "pwi", [P, ST + 1, GR])
            spi = area(s5, "spi", [P, ST + 1, GR])
            bc = area(s5, "bc", [P, 4, GR * GH])
            bb = area(s5, "bb", [P, 2, GR * GH])
            bt = area(s5, "bt", [P, W8])
            kst = area(s5, "kst", [P, GH, GR])
            d16 = area(s5, "d16", [GH, 2, D])
            blk = area(s5, "blk", [P, P])
            u = area(s5, "u", [P, GR, NC])
            gch = area(s5, "gch", [P, GR])
            ssum = area(s5, "ssum", [P, 3, NC])
            E = area(s5, "E", [P, SG, P])
            ET = area(s5, "ET", [P, SG, P])
            G = area(s5, "G", [P, 2, SG * P])
            Wc = area(s5, "Wc", [P, GR, NC])
            Wsn = area(s5, "Wsn", [P, GR, NC])
            T = area(s5, "T", [P, ST * GH, GR])
            S = area(s5, "S", [P, GR, NC])
            vsb = area(s5, "vsb", [P, 512])
            z1 = area(s5, "z1", [P, 512])
            z2 = area(s5, "z2", [P, 512])
            dec = area(s5, "dec", [P, SG, NC])
            yg = area(s5, "yg", [P, 2, 512])
        main = top.enter_context(ExitStack())
        whi = area(main, "whi", [P, RING, D], FR)
        wlo = area(main, "wlo", [P, RING, D], FR)
        h = area(main, "h", [P, KT, TOK])
        rcos = area(main, "rcos", [P, TOK])
        rsin = area(main, "rsin", [P, TOK])
        ev = area(main, "ev", [P, 2, TOK])
        sg = area(main, "sg", [P, TOK])
        sq = area(main, "sq", [P, TOK])
        acc = area(main, "acc", [P, TOK])
        std = area(main, "std", [P, TOK])
        rstd = area(main, "rstd", [P, TOK])
        cols = area(main, "cols", [P, 64])
        X = {}

        def pair(stack, name, tiles=KT):
            X[name] = (area(stack, name + "h", [P, tiles, TOK], FR), area(stack, name + "l", [P, tiles, TOK], FR))

        pair(main, "A")
        with ExitStack() as st:
            pair(st, "C")
            with ExitStack() as st2:
                pair(st2, "B")
                ple = area(st2, "ple", [P, KT, TOK])
            with ExitStack() as st2:
                yfm = area(st2, "yfm", [P, KT, ST, NC])
            with ExitStack() as st2:
                q1 = area(st2, "q1", [P, 8, TOK])
                k1 = area(st2, "k1", [P, 2, TOK + P])
                kv1 = area(st2, "kv1", [P, 4, TOK])
                v1 = area(st2, "v1", [P, NB, 256])
                rope1 = area(st2, "rope1", [P, 2, TOK])
                msk1 = area(st2, "msk1", [P, 3, 256])
                sm1 = area(st2, "sm1", [P, 2, 2, 256])
                pt1 = area(st2, "pt1", [P, 2, 512])
            with ExitStack() as st2:
                q2 = area(st2, "q2", [P, 4, TOK])
                k2 = area(st2, "k2", [P, 4, TOK])
                v2 = area(st2, "v2", [P, NB, D])
                sgr = area(st2, "sgr", [P, KT, TOK])
            with ExitStack() as st2:
                ybuf = area(st2, "ybuf", [P, KT, TOK])
        with ExitStack() as st2:
            for k in ("C",):
                area(st2, "pad_c", [P, 2 * KT * TOK])
            area(st2, "pad_b", [P, 3 * KT * TOK])
            rmask = area(st2, "rmask", [P, RH, P])
            xi = area(st2, "xi", [P, 4, P])
            cu = area(st2, "cu", [P, TOK + 2])
            cy = area(st2, "cy", [P, TOK])
        with ExitStack() as st:
            qn = area(st, "qn", [P, MH, TOK])
            kn = area(st, "kn", [P, MH, TOK])
            qr = area(st, "qr", [P, 4, TOK])
            kr = area(st, "kr", [P, TOK])
            v3 = area(st, "v3", [P, NB, D])
            sg3 = area(st, "sg3", [P, KT, TOK])
            cm = area(st, "cm", [P, TOK])
            sm3 = area(st, "sm3", [P, 2, TOK])
        with ExitStack() as st:
            ybuf3 = area(st, "ybuf3", [P, KT, TOK])
        ysc = nc.dram_tensor("ysc", [NSL, P, 512], F32, kind="Internal").ap()

        raw_in = [sem(f"raw_in{r}") for r in range(RING)]
        hi_ready = sem("hi_ready")
        lo_ready = sem("lo_ready")
        seg_done = sem("seg_done")
        evac = sem("evac")
        x_hi = sem("x_hi")
        x_lo = sem("x_lo")
        to_act = sem("to_act")
        to_dve = sem("to_dve")
        ssq_ready = sem("ssq_ready")
        nrm_ps = sem("nrm_ps")
        nrm_std = sem("nrm_std")
        acc_add = sem("acc_add")
        rope_ps = sem("rope_ps")
        rope_done = sem("rope_done")
        vt_ps = sem("vt_ps")
        vt_done = sem("vt_done")
        silu_done = sem("silu_done")
        dve_ch, act_ch = sem("dve_ch"), sem("act_ch")
        in_cst, in_lam, in_bc, in_x, in_d = sem("in_cst"), sem("in_lam"), sem("in_bc"), sem("in_x"), sem("in_d")
        in_h, in_y, in_p, in_pos = sem("in_h"), sem("in_y"), sem("in_p"), sem("in_pos")
        in_a1, in_rt, in_cm = sem("in_a1"), sem("in_rt"), sem("in_cm")
        fin, out_sem = sem("fin"), sem("out_sem")
        tabs, ang, sq_x, ss_x, ss_ps, std_x, u_ready = (sem(n) for n in ("tabs", "ang", "sq_x", "ss_x", "ss_ps", "std_x", "u_ready"))
        e_ready, e_used, et_ps, et_sb, v_ps, v_sb, vp, z_ready, zp, s_ready = (
            sem(n) for n in ("e_ready", "e_used", "et_ps", "et_sb", "v_ps", "v_sb", "vp", "z_ready", "zp", "s_ready"))
        kst_ready, t_zero, toep, g_ready, y_ps, yg_ready = (sem(n) for n in ("kst_ready", "t_zero", "toep", "g_ready", "y_ps", "yg_ready"))
        y_out = [sem("y_out0"), sem("y_out1")]
        sc_ps, sc_out, p_ready, pt_ps, pt_ready, o_ps, o_out = (sem(n) for n in ("sc_ps", "sc_out", "p_ready", "pt_ps", "pt_ready", "o_ps", "o_out"))
        rk_ps, rs_ps, rk_sb, rs_sb, rkv_ps, rpv, r_ps, r_out = (
            sem(n) for n in ("rk_ps", "rs_ps", "rk_sb", "rs_sb", "rkv_ps", "rpv", "r_ps", "r_out"))

        def C(name):
            return cst[:, CC[name]]

        def gain(name, m):
            return gp[:, GC[name].start + m:GC[name].start + m + 1]

        eps = C("eps")
        U1 = 8 * 2 * 2
        U3 = MH * NB
        MSCALE = float(MN + MR) ** -0.5
        LAT_K = {"qb": 3, "kvb": 2}

        block = top.enter_context(nc.Block())

        @block.sync
        def _(sp):
            sp.dma_start(lam[:, :, :], a["lam"]).then_inc(in_lam, 16)
            sp.dma_start(cst[:, :], a["cst"]).then_inc(in_cst, 16)
            sp.dma_start(u[:, :, :], a["xch"]).then_inc(in_x, 16)
            sp.dma_start(bc[:, :, :], a["bc"]).then_inc(in_bc, 16)
            sp.dma_start(blk[:, :], a["blk"]).then_inc(in_d, 16)
            sp.dma_start(gch[:, :], a["gch"]).then_inc(in_d, 16)
            sp.dma_start(d16[:, :, :], a["d16"]).then_inc(in_d, 16)
            sp.dma_start(gp[:, :], a["gp"]).then_inc(in_cst, 16)
            for r in range(RING):
                sp.dma_start(raw[:, r, :], a["w"][r, :, :]).then_inc(raw_in[r], 16)
            sp.wait_ge(kst_ready, 1)
            sp.wait_ge(t_zero, 1)
            for t in range(ST):
                sp.dma_start(T[GH * (ST - 1 - t):P, GH * t:GH * (t + 1), :], kst[0:GH * (t + 1), :, :]).then_inc(toep, 16)
            for sl in range(NSL):
                sp.wait_ge(yg_ready, sl + 1)
                sp.dma_start(ysc[sl, :, :], yg[:, sl % 2, :]).then_inc(y_out[sl % 2], 16)
            for r in range(2):
                sp.wait_ge(y_out[r], 16 * NSL // 2)
            sp.dma_start(ev[:, :, :], a["p"][0, :, :, :]).then_inc(in_p, 16)
            for sl in range(NSL):
                for g in range(SG):
                    sp.dma_start(yfm[GH * g:GH * (g + 1), sl, :, :],
                                 ysc[sl, :, g * NC:(g + 1) * NC].rearrange("(t h) c -> h t c", h=GH)).then_inc(in_y, 16)
            sp.dma_start(h[:, :, :], a["xfm"]).then_inc(in_h, 16)
            sp.dma_start(acc[:, :].bitcast(I32), a["pos"].partition_broadcast(P)).then_inc(in_pos, 16)
            sp.dma_start(rmask[:, :, :], a["rmask"]).then_inc(in_rt, 16)
            sp.dma_start(xi[:, :, :], a["xi"]).then_inc(in_rt, 16)
            with sp.Fori(1, NS // RING) as i:
                for r in range(RING):
                    sp.wait_ge(lo_ready, RING * i + (r - RING + 1))
                    sp.dma_start(raw[:, r, :], a["w"][RING * i + r, :, :]).then_inc(raw_in[r], 16)
            for m in range(KT):
                sp.wait_ge(fin, m + 1)
                sp.dma_start(a["out"][m, :, :], h[:, m, :]).then_inc(out_sem, 16)
            sp.wait_ge(out_sem, 16 * KT)

        @block.gpsimd
        def _(pool):
            nc.gpsimd.memset(T[:, :, :], 0.0).then_inc(t_zero, 1)
            with pool.Fori(0, NS // RING) as i:
                for r in range(RING):
                    pool.wait_ge(hi_ready, RING * i + r + 1)
                    nc.gpsimd.tensor_tensor(wlo[:, r, :], raw[:, r, :], whi[:, r, :].bitcast(F32), ALU.subtract).then_inc(lo_ready, 1)

        @block.scalar
        def _(act):
            ch = Chain(act, act_ch)
            got = [0]
            nrm = [0]
            xs = [0]

            act.wait_ge(in_lam, 16)
            nc.scalar.activation(tab[:, 0, :], lam[:, 2, :], ACT.Exp).then_inc(tabs, 1)
            act.wait_ge(in_x, 16)
            nc.scalar.activation(S[:, :, :], u[:, :, :], ACT.Square).then_inc(sq_x, 1)
            act.wait_ge(ang, 1)
            act.wait_ge(in_cst, 32)
            nc.scalar.activation(tab[:, 5, :], tab[:, 1, :], ACT.Exp)
            nc.scalar.activation(tab[:, 6, :], tab[:, 4, :], ACT.Sin)
            ch.link(nc.scalar.activation(tab[:, 7, :], tab[:, 4, :], ACT.Abs))
            nc.scalar.activation(tab[:, 8, :], tab[:, 7, :], ACT.Sin, bias=C("halfpi"), scale=-1.0).then_inc(tabs, 1)
            act.wait_ge(ss_ps, 1)
            nc.scalar.activation(ssum[:, 1, :], ps[:, NRM, 0:NC], ACT.Sqrt, bias=eps, scale=1.0 / D).then_inc(std_x, 1)
            for sl in range(NSL):
                if sl:
                    act.wait_ge(v_ps, sl)
                for half in range(2):
                    act.wait_ge(et_ps, 2 * sl + half + 1)
                    nc.scalar.copy(ET[:, 4 * half:4 * half + 4, :], ps[:, 2 + half, :].rearrange("p (g n) -> p g n", g=4)).then_inc(et_sb, 1)
                act.wait_ge(v_ps, sl + 1)
                if sl:
                    act.wait_ge(z_ready, sl)
                nc.scalar.copy(vsb[:, :], ps[:, SX, :]).then_inc(v_sb, 1)
            for sl in range(NSL):
                act.wait_ge(y_ps, sl + 1)
                if sl >= 2:
                    act.wait_ge(y_out[sl % 2], 16 * (sl // 2))
                nc.scalar.activation(yg[:, sl % 2, :], ps[:, 2 + sl % 2, :], ACT.Gelu_apprx_tanh).then_inc(yg_ready, 1)
            for r in range(2):
                act.wait_ge(y_out[r], 16 * NSL // 2)

            def split_strip(t, seg, slot=None, turn=None):
                if slot is None:
                    slot, turn = t % RING, t // RING + 1
                act.wait_ge(raw_in[slot], 16 * turn)
                if not isinstance(seg, int) or seg > 0:
                    act.wait_ge(seg_done, seg)
                nc.scalar.activation(whi[:, slot, :], raw[:, slot, :], ACT.Copy).then_inc(hi_ready, 1)

            def ahead(name, l):
                t = S0[name] + l + LEAD
                if t < NS:
                    split_strip(t, SEG0[name] + SEGS[name] * l)

            def ahead_loop(name, i, j):
                t = S0[name] + j + LEAD
                split_strip(None, SEG0[name] + SEGS[name] * j + SEGS[name] * RING * i, t % RING, t // RING + 1 + i)

            def answer(ins):
                ins.then_inc(to_dve, 1)

            def asked():
                got[0] += 1
                act.wait_ge(to_act, got[0])

            def high(dst, m, src, scale=None):
                if scale is None:
                    nc.scalar.activation(X[dst][0][:, m, :], src, ACT.Copy).then_inc(x_hi, 1)
                else:
                    nc.scalar.activation(X[dst][0][:, m, :], src, ACT.Copy, scale=scale).then_inc(x_hi, 1)
                xs[0] += 1

            def root(n):
                nrm[0] += 1
                act.wait_ge(nrm_ps, nrm[0])
                nc.scalar.activation(std[:, :], ps[:, NRM, :], ACT.Sqrt, bias=eps, scale=1.0 / n).then_inc(nrm_std, 1)

            for t in range(LEAD):
                split_strip(t, 0)
            act.wait_ge(in_p, 16)
            for k in range(2):
                high("C", k, ev[:, k, :])
            act.wait_ge(in_y, 16 * NSL * SG)
            for m in range(KT):
                nc.scalar.activation(X["A"][0][:, m, :].rearrange("p (c t) -> p c t", t=ST),
                                     yfm[:, m, :, :].rearrange("p t c -> p c t"), ACT.Copy).then_inc(x_hi, 1)
                xs[0] += 1
            asked()
            nc.scalar.activation(rsin[:, :], std[:, :], ACT.Sin)
            ch.link(nc.scalar.activation(sg[:, :], std[:, :], ACT.Abs))
            answer(nc.scalar.activation(rcos[:, :], sg[:, :], ACT.Sin, bias=C("halfpi"), scale=-1.0))
            for l in range(2):
                ahead("proj0", l)
            for m in range(KT):
                ahead("glu", 2 * m)
                ahead("glu", 2 * m + 1)
                o = OUT0["glu"] + 2 * m
                act.wait_ge(seg_done, SEG0["glu"] + 2 * m + 1)
                answer(nc.scalar.activation(sg[:, :], ps[:, o % RING, :], ACT.Sigmoid))
                asked()
                nc.scalar.activation(sq[:, :], h[:, m, :], ACT.Square)
                high("B", m, h[:, m, :], gain("mlp0", m))

            def mlp(layer):
                root(D)
                for kind, c in (("up", 0), ("up", 1), ("down", 0), ("up", 2), ("down", 1), ("up", 3), ("down", 2), ("down", 3)):
                    name = f"{kind}{layer}_{c}"
                    if kind == "up":
                        dst = X["AC"[c % 2]][0]
                        with act.Fori(0, 8 // RING) as i:
                            for j in range(RING):
                                ahead_loop(name, i, j)
                                act.wait_ge(evac, OUT0[name] + RING * i + j + 1)
                                nc.scalar.activation(sg[:, :], ev[:, 0, :], ACT.Square)
                                nc.scalar.activation(dst[:, RING * i + j, :], ev[:, 0, :], ACT.Square).then_inc(x_hi, 1)
                        xs[0] += 8
                    elif c < CHUNKS - 1:
                        with act.Fori(0, 8 // RING) as i:
                            for j in range(RING):
                                ahead_loop(name, i, j)
                    else:
                        for m in range(KT):
                            ahead(name, m)
                            act.wait_ge(evac, OUT0[name] + m + 1)
                            nc.scalar.activation(sq[:, :], h[:, m, :], ACT.Square)
                            high("B", m, h[:, m, :], gain(f"ple{layer}", m))

            def gate(layer):
                root(D)
                for m in range(KT):
                    ahead(f"gate{layer}", m)
                    act.wait_ge(evac, OUT0[f"gate{layer}"] + m + 1)
                    answer(nc.scalar.activation(sg[:, :], ev[:, 0, :], ACT.Sigmoid))
                    asked()
                    if layer == 0:
                        nc.scalar.activation(sq[:, :], h[:, m, :], ACT.Square)
                        high("A", m, h[:, m, :], gain("kvn", m))
                        high("C", m, h[:, m, :], gain("mix1", m))
                    else:
                        answer(nc.scalar.activation(sq[:, :], h[:, m, :], ACT.Square))

            mlp(0)
            gate(0)
            act.wait_ge(seg_done, SEG0["kv"])
            act.wait_ge(x_lo, XT["kvq"] + 16)
            act.dma_start(rope1[:, :, :], a["rope1"]).then_inc(in_a1, 16)
            act.dma_start(msk1[:, :, :], a["msk1"]).then_inc(in_a1, 16)
            root(D)
            for l in range(NSTR["kv"]):
                ahead("kv", l)
            with act.Fori(0, 8 // RING) as i:
                for j in range(RING):
                    ahead_loop("q", i, j)
            for j in range(2):
                act.wait_ge(vt_ps, j + 1)
                nc.scalar.copy(v1[:, :, j * P:(j + 1) * P], ps[:, NRM, :].rearrange("p (n d) -> p n d", n=NB)).then_inc(vt_done, 1)

            def exp1(un):
                b, q0 = un // 2 % 2, 16 * (un % 2)
                sink = gain("sink", un // 4 * 2 + b)
                asked()
                for n in range(2):
                    nc.scalar.activation(sm1[:, un % 2, n, :], sm1[:, un % 2, n, :], ACT.Exp, bias=cols[:, q0 + 4 + n:q0 + 5 + n],
                                         scale=float(HD) ** -0.5, accum_out=cols[:, q0 + 6 + n:q0 + 7 + n])
                answer(nc.scalar.activation(cols[:, q0 + 8:q0 + 10], cols[:, q0 + 4:q0 + 6], ACT.Exp, bias=sink))

            exp1(0)
            for un in range(U1):
                if un + 1 < U1:
                    exp1(un + 1)
                act.wait_ge(pt_ps, un + 1)
                nc.scalar.copy(pt1[:, un % 2, :], ps[:, 2 + un % 2, :]).then_inc(pt_ready, 1)
                if un % 4 == 1 and un > 4:
                    m = un // 4 - 1
                    act.wait_ge(o_ps, m + 1)
                    high("A", m, ps[:, SX + m % 2, :])
            act.wait_ge(o_ps, KT)
            high("A", KT - 1, ps[:, SX + (KT - 1) % 2, :])
            for m in range(KT):
                ahead("wo", m)
                act.wait_ge(evac, OUT0["wo"] + m + 1)
                nc.scalar.activation(sq[:, :], h[:, m, :], ACT.Square)
                high("B", m, h[:, m, :], gain("mlp1", m))
            act.wait_ge(x_lo, XT["mlp1"] + 8)
            act.dma_start(ev[:, :, :], a["p"][1, :, :, :]).then_inc(in_p, 16)
            act.wait_ge(in_p, 32)
            for k in range(2):
                high("C", k, ev[:, k, :])
            for l in range(2):
                ahead("proj1", l)
            mlp(1)
            gate(1)
            root(D)
            for m in range(KT):
                asked()
                nc.scalar.activation(sq[:, :], h[:, m, :], ACT.Square)
                high("C", m, h[:, m, :], gain("pre0", m))
            root(D)
            E0 = OUT0["even"]
            for l in range(8):
                ahead("even", l)

            def value(n, dst, m):
                act.wait_ge(vt_ps, n + 1)
                nc.scalar.copy(dst[:, :, m * P:(m + 1) * P], ps[:, SZ, :].rearrange("p (n d) -> p n d", n=NB)).then_inc(vt_done, 1)

            for m in range(8):
                ahead("even", 8 + m)
                if m:
                    value(2 + m - 1, v2, m - 1)
            value(2 + 7, v2, 7)
            for m in range(8):
                ahead("even", 16 + m)
                act.wait_ge(evac, E0 + 16 + m + 1)
                nc.scalar.activation(sgr[:, m, :], ev[:, m % 2, :], ACT.Silu).then_inc(silu_done, 1)
            for t in range(8):
                for j in range(4):
                    ahead("even", 24 + 4 * t + j)
                asked()
                answer(nc.scalar.activation(cy[:, :], cu[:, 0:TOK], ACT.Identity, bias=gain("cb", t), scale=gain("cw", t)))
                act.wait_ge(evac, E0 + 24 + 4 * t + 4)
                answer(nc.scalar.activation(sg[:, :], ev[:, 1, :], ACT.Silu))
                asked()
                high("A", t, cy[:, :])
            for hh in range(RH):
                act.wait_ge(r_ps, hh + 1)
                nc.scalar.activation(sq[:, :], ps[:, 2 + hh % 2, :], ACT.Square).then_inc(ssq_ready, 1)
                root(P)
                asked()
                high("C", hh, ev[:, hh % 2, :])

            def post(name):
                for m in range(KT):
                    for l in ((2 * m, 2 * m + 1) if name == "eout" else (m,)):
                        ahead(name, l)
                    act.wait_ge(evac, OUT0[name] + m + 1)
                    answer(nc.scalar.activation(sq[:, :], (ybuf if name == "eout" else ybuf3)[:, m, :], ACT.Square))
                root(D)

            post("eout")
            act.dma_start(cm[:, :], a["cm"]).then_inc(in_cm, 16)
            for m in range(KT):
                asked()
                nc.scalar.activation(sq[:, :], h[:, m, :], ACT.Square)
                high("A", m, h[:, m, :], gain("pre1", m))
            root(D)
            O0 = OUT0["odd"]
            for m in range(8):
                ahead("odd", m)
                act.wait_ge(evac, O0 + m + 1)
                nc.scalar.activation(sg3[:, m, :], ev[:, m % 2, :], ACT.Silu).then_inc(silu_done, 1)
            ahead("odd", 8)
            for m in range(5):
                ahead("odd", 9 + m)
                act.wait_ge(evac, O0 + 9 + m + 1)
                answer(nc.scalar.activation(sq[:, :], kn[:, m, :], ACT.Square))
                if m == 2:
                    root(QL)
            act.wait_ge(seg_done, SEG0["qb"])
            for m in range(5):
                high("A", m, kn[:, m, :], gain("qa", m) if m < 3 else gain("kva", m - 3))
            for l in range(NSTR["qb"]):
                ahead("qb", l)
            root(KL)
            for l in range(NSTR["kvb"]):
                ahead("kvb", l)
                if l >= 2:
                    for m in range(4 * (l - 2), 4 * (l - 1)):
                        value(10 + m, v3, m)

            def exp3(un):
                n, q0 = (un % NB + 1) * P, 8 * (un % 2)
                asked()
                answer(nc.scalar.activation(sm3[:, un % 2, 0:n], sm3[:, un % 2, 0:n], ACT.Exp, bias=cols[:, q0 + 1:q0 + 2],
                                            scale=MSCALE, accum_out=cols[:, q0 + 2:q0 + 3]))

            exp3(0)
            for un in range(U3):
                n = (un % NB + 1) * P
                if un + 1 < U3:
                    exp3(un + 1)
                act.wait_ge(pt_ps, U1 + un + 1)
                nc.scalar.copy(ev[:, un % 2, 0:n], ps[:, 2 + un % 2, 0:n]).then_inc(pt_ready, 1)
                if un % NB == 1 and un > NB:
                    act.wait_ge(o_out, un // NB)
                    high("A", un // NB - 1, sg[:, :])
            act.wait_ge(o_out, MH)
            high("A", MH - 1, sg[:, :])
            post("oout")
            assert xs[0] == XT["oo"] + 8

        @block.tensor
        def _(pe):
            nrm = [0]
            pe.wait_ge(in_d, 48)
            pe.wait_ge(in_cst, 32)
            pe.wait_ge(ss_x, 1)
            nc.tensor.matmul(ps[:, NRM, 0:NC], blk[:, :], ssum[:, 0, :], start=True, stop=True).then_inc(ss_ps, 1)

            def second_turn(sl):
                pe.wait_ge(z_ready, sl + 1)
                if sl:
                    pe.wait_ge(s_ready, sl)
                nc.tensor.matmul(ps[:, SZ, :], C("permz"), z2[:, :], start=True, stop=True).then_inc(zp, 1)

            for sl in range(NSL):
                pe.wait_ge(e_ready, sl + 1)
                for g in range(SG):
                    gg = sl * SG + g
                    nc.tensor.matmul(ps[:, gg // 32, gg % 32 * GH:(gg % 32 + 1) * GH], E[:, g, :], bc[:, 2, gg * GH:(gg + 1) * GH],
                                     start=True, stop=True)
                for half in range(2):
                    if sl:
                        pe.wait_ge(et_sb, 2 * sl - 1 + half)
                    for g in range(4):
                        last = nc.tensor.transpose(ps[:, 2 + half, g * P:(g + 1) * P], E[:, 4 * half + g, :], C("ident"))
                    last.then_inc(et_ps, 1)
                pe.wait_ge(et_sb, 2 * sl + 2)
                pe.wait_ge(u_ready, 1)
                if sl:
                    pe.wait_ge(v_sb, sl)
                for g in range(SG):
                    last = nc.tensor.matmul(ps[:, SX, g * NC:(g + 1) * NC], ET[:, g, :], u[:, sl * SG + g, :], start=True, stop=True)
                last.then_inc(v_ps, 1)
                if sl:
                    second_turn(sl - 1)
                pe.wait_ge(v_sb, sl + 1)
                nc.tensor.matmul(ps[:, SY, :], C("permz"), vsb[:, :], start=True, stop=True).then_inc(vp, 1)
            second_turn(NSL - 1)
            pe.wait_ge(toep, 16 * ST)
            pe.wait_ge(s_ready, NSL)
            for sl in range(NSL):
                pe.wait_ge(g_ready, sl + 1)
                if sl >= 2:
                    pe.wait_ge(yg_ready, sl - 1)
                for g in range(SG):
                    gg = sl * SG + g
                    nc.tensor.matmul(ps[:, 2 + sl % 2, g * NC:(g + 1) * NC], T[:, :, gg], u[:, gg, :],
                                     start=True, stop=False)
                    last = nc.tensor.matmul(ps[:, 2 + sl % 2, g * NC:(g + 1) * NC], G[:, sl % 2, g * P:(g + 1) * P], S[:, gg, :],
                                            start=False, stop=True)
                last.then_inc(y_ps, 1)

            def product(slot, k, bank, xh, xl, first, last):
                w = slice(k * P, (k + 1) * P)
                out = ps[:, bank, :]
                nc.tensor.matmul(out, whi[:, slot, w], xh, start=first, stop=False)
                nc.tensor.matmul(out, whi[:, slot, w], xl, start=False, stop=False)
                return nc.tensor.matmul(out, wlo[:, slot, w], xh, start=False, stop=last)

            def strip(name, l, j, x, xt, step=1):
                slot, bank = (S0[name] + j) % RING, (OUT0[name] + j) % RING
                pe.wait_ge(lo_ready, S0[name] + l + 1)
                pe.wait_ge(evac, OUT0[name] + l - RING + 1)
                for k in range(KT):
                    if j == 0:
                        pe.wait_ge(x_lo, xt + step * k + 1)
                    last = product(slot, k, bank, X[x][0][:, k, :], X[x][1][:, k, :], k == 0, k == KT - 1)
                last.then_inc(seg_done, 1)

            def strips(name, x, xt, step=1, n=8):
                with pe.Fori(0, n // RING) as i:
                    for j in range(RING):
                        strip(name, RING * i + j, j, x, xt, step)

            def short_strip(name, l, per, k_tiles, x, xt, x0=0):
                slot = (S0[name] + l) % RING
                pe.wait_ge(lo_ready, S0[name] + l + 1)
                for q in range(per):
                    o = OUT0[name] + per * l + q
                    if o >= RING:
                        pe.wait_ge(evac, o - RING + 1)
                    for k in range(k_tiles):
                        pe.wait_ge(x_lo, xt + x0 + k + 1)
                        last = product(slot, q * k_tiles + k, o % RING, X[x][0][:, x0 + k, :], X[x][1][:, x0 + k, :], k == 0, k == k_tiles - 1)
                    last.then_inc(seg_done, 1)

            def norm(src=None):
                nrm[0] += 1
                pe.wait_ge(ssq_ready, nrm[0])
                nc.tensor.matmul(ps[:, NRM, :], C("ones"), acc[:, :] if src is None else src, start=True, stop=True).then_inc(nrm_ps, 1)

            def mlp(layer):
                norm()
                for kind, c in (("up", 0), ("up", 1), ("down", 0), ("up", 2), ("down", 1), ("up", 3), ("down", 2), ("down", 3)):
                    if kind == "up":
                        strips(f"up{layer}_{c}", "B", XT[f"mlp{layer}"])
                    else:
                        strips(f"down{layer}_{c}", "AC"[c % 2], XT[f"hid{layer}_{c}"])
                norm()
                strips(f"gate{layer}", "B", XT[f"gate{layer}"])

            def partners(n, perm, src, bank):
                nc.tensor.matmul(ps[:, bank, :], C(perm), src, start=True, stop=True).then_inc(rope_ps, 1)

            def transposes(src, bank, n=NB):
                for k in range(n):
                    last = nc.tensor.transpose(ps[:, bank, k * P:(k + 1) * P], src[:, k * P:(k + 1) * P], C("ident"))
                return last

            for l in range(2):
                short_strip("proj0", l, 4, 2, "C", XT["p0"])
            strips("glu", "A", XT["y"], n=16)
            mlp(0)
            norm()
            for l in range(NSTR["kv"]):
                strip("kv", l, l, "A", XT["kvq"], 2)
            strips("q", "C", XT["kvq"] + 1, 2)
            pe.wait_ge(evac, OUT0["wo"])
            partners(0, "perm1", kv1[:, 0, :], SX)
            partners(1, "perm1", kv1[:, 1, :], SY)
            for j in range(2):
                if j:
                    pe.wait_ge(vt_done, j)
                transposes(kv1[:, 2 + j, :], NRM).then_inc(vt_ps, 1)
            partners(2, "perm1", q1[:, 0, :], SZ)

            def scores1(un):
                m, b, r = un // 4, un // 2 % 2, slice(64 * (un // 2 % 2), 64 * (un // 2 % 2) + 64)
                pe.wait_ge(rope_done, 3 + m)
                if un >= 2:
                    pe.wait_ge(sc_out, un - 1)
                for k in range(2):
                    n = un % 2 * 2 + k
                    last = nc.tensor.matmul(ps[:, un % 2, k * 256:(k + 1) * 256], q1[r, m, n * P:(n + 1) * P],
                                            k1[r, m // 4, n * P:(n + 2) * P], start=True, stop=True)
                last.then_inc(sc_ps, 1)

            scores1(0)
            scores1(1)
            for un in range(U1):
                m, b = un // 4, un // 2 % 2
                r = slice(64 * b, 64 * b + 64)
                if un % 4 == 0 and m + 1 < KT:
                    pe.wait_ge(rope_done, 3 + m)
                    partners(3 + m, "perm1", q1[:, m + 1, :], SZ)
                pe.wait_ge(p_ready, un + 1)
                if un >= 2:
                    pe.wait_ge(pt_ready, un - 1)
                for k in range(4):
                    last = nc.tensor.transpose(ps[:, 2 + un % 2, k * P:(k + 1) * P], sm1[:, un % 2, k // 2, k % 2 * P:(k % 2 + 1) * P], C("ident"))
                last.then_inc(pt_ps, 1)
                if un + 2 < U1:
                    scores1(un + 2)
                pe.wait_ge(pt_ready, un + 1)
                if un == 0:
                    pe.wait_ge(vt_done, 2)
                if un % 4 == 0 and m >= 2:
                    pe.wait_ge(x_lo, XT["o"] + m - 1)
                for k in range(2):
                    n = un % 2 * 2 + k
                    for kb in range(2):
                        if n + kb == 0:
                            continue
                        v = v1[:, n + kb - 1, m // 4 * P + 64 * b:m // 4 * P + 64 * b + 64]
                        last = nc.tensor.matmul(ps[r, SX + m % 2, n * P:(n + 1) * P], v, pt1[:, un % 2, (2 * k + kb) * P:(2 * k + kb + 1) * P],
                                                start=(kb == 0 or n == 0), stop=(kb == 1))
                if un % 4 == 3:
                    last.then_inc(o_ps, 1)
            strips("wo", "A", XT["o"])
            for l in range(2):
                short_strip("proj1", l, 4, 2, "C", XT["p1"])
            mlp(1)
            norm()
            norm()
            strips("even", "C", XT["even"])

            def even(l):
                strip("even", l, l, "C", XT["even"])

            for m in range(8):
                even(8 + m)
                if m >= 2:
                    pe.wait_ge(rope_done, 10 + m - 1)
                partners(10 + m, "perm2", (q2 if m < 4 else k2)[:, m % 4, :], SX + m % 2)
                if m:
                    pe.wait_ge(evac, OUT0["even"] + 8 + m)
                    if m > 1:
                        pe.wait_ge(vt_done, 2 + m - 1)
                    transposes(ev[:, (m - 1) % 2, :], SZ).then_inc(vt_ps, 1)
            pe.wait_ge(evac, OUT0["even"] + 16)
            pe.wait_ge(vt_done, 2 + 7)
            transposes(ev[:, 1, :], SZ).then_inc(vt_ps, 1)
            with pe.Fori(0, 40 // RING) as i:
                for j in range(RING):
                    strip("even", 16 + RING * i + j, 16 + j, "C", XT["even"])
            pe.wait_ge(evac, OUT0["eout"])
            pe.wait_ge(rope_done, 18)
            pe.wait_ge(vt_done, 10)
            for jp in range(RH // 2):
                if jp:
                    pe.wait_ge(rk_sb, jp)
                transposes(k2[:, jp, :], SX).then_inc(rk_ps, 1)
                for b in range(2):
                    r = slice(64 * b, 64 * b + 64)
                    if jp:
                        pe.wait_ge(rs_sb, 2 * (jp - 1) + b + 1)
                    for n in range(NB):
                        cc = slice(n * P, (n + 1) * P)
                        last = nc.tensor.matmul(ps[:, b, cc], k2[r, jp, cc], q2[r, jp, cc], start=True, stop=True)
                    last.then_inc(rs_ps, 1)
                pe.wait_ge(rk_sb, jp + 1)
                if jp:
                    pe.wait_ge(rpv, jp)
                for n in range(NB - 1):
                    for b in range(2):
                        hh = 2 * jp + b
                        last = nc.tensor.matmul(ps[64 * b:64 * b + 64, SY, n * P:(n + 1) * P], cy[:, n * P + 64 * b:n * P + 64 * b + 64],
                                                v2[:, n, hh * P:(hh + 1) * P], start=True, stop=True)
                last.then_inc(rkv_ps, 1)
                pe.wait_ge(rs_sb, 2 * jp + 2)
                pe.wait_ge(rpv, jp + 1)
                for b in range(2):
                    hh, r = 2 * jp + b, slice(64 * b, 64 * b + 64)
                    if jp:
                        pe.wait_ge(r_out, hh - 1)
                    for n in range(NB):
                        cc = slice(n * P, (n + 1) * P)
                        last = nc.tensor.matmul(ps[:, 2 + b, cc], v2[:, n, hh * P:(hh + 1) * P], ev[:, b, cc], start=True, stop=(n == 0))
                        if n:
                            last = nc.tensor.matmul(ps[:, 2 + b, cc], acc[r, cc], sg[r, cc], start=False, stop=True)
                    last.then_inc(r_ps, 1)
                for b in range(2):
                    norm(sq[:, :])
            with pe.Fori(0, 2) as i:
                for j in range(8):
                    slot, bank = (S0["eout"] + j) % RING, (OUT0["eout"] + j // 2) % RING
                    pe.wait_ge(lo_ready, S0["eout"] + j + 1 + 8 * i)
                    if j % 2 == 0:
                        pe.wait_ge(evac, OUT0["eout"] + j // 2 - RING + 1 + 4 * i)
                    x, xt = ("C", XT["ret"]) if j % 2 == 0 else ("A", XT["conv"])
                    for k in range(KT):
                        if j < 2:
                            pe.wait_ge(x_lo, xt + k + 1)
                        last = product(slot, k, bank, X[x][0][:, k, :], X[x][1][:, k, :], j % 2 == 0 and k == 0, j % 2 == 1 and k == KT - 1)
                    last.then_inc(seg_done, 1)
            norm()
            norm()
            strips("odd", "A", XT["odd"])
            for l in range(8, 14):
                strip("odd", l, l, "A", XT["odd"])
                if l == 9:
                    pe.wait_ge(evac, OUT0["odd"] + 9)
                    partners(18, "perm2", kr[:, :], SX)
            norm()
            for l in range(NSTR["qb"]):
                short_strip("qb", l, 2, 3, "A", XT["lat"])
            norm()
            for l in range(NSTR["kvb"]):
                short_strip("kvb", l, 4, 2, "A", XT["lat"], 3)
                if l >= 2:
                    for m in range(4 * (l - 2), 4 * (l - 1)):
                        pe.wait_ge(evac, OUT0["kvb"] + 8 + m + 1)
                        pe.wait_ge(vt_done, 10 + m)
                        transposes(ev[:, m % 2, :], SZ).then_inc(vt_ps, 1)
            for m in range(4):
                if m >= 1:
                    pe.wait_ge(rope_done, 18 + m)
                partners(19 + m, "perm2", qr[:, m, :], SX + m % 2)
            pe.wait_ge(evac, OUT0["oout"])

            def scores3(un):
                hh, n = un // NB, un % NB
                r = slice(64 * (hh % 2), 64 * (hh % 2) + 64)
                pe.wait_ge(rope_done, 19 + hh // 2 + 1)
                if un >= 2:
                    pe.wait_ge(sc_out, U1 + un - 1)
                keys, qs = (n + 1) * P, slice(n * P, (n + 1) * P)
                nc.tensor.matmul(ps[:, un % 2, 0:keys], qn[:, hh, qs], kn[:, hh, 0:keys], start=True, stop=False)
                nc.tensor.matmul(ps[:, un % 2, 0:keys], qr[r, hh // 2, qs], kr[r, 0:keys], start=False, stop=True).then_inc(sc_ps, 1)

            scores3(0)
            scores3(1)
            for un in range(U3):
                hh, n = un // NB, un % NB
                pe.wait_ge(p_ready, U1 + un + 1)
                if un >= 2:
                    pe.wait_ge(pt_ready, U1 + un - 1)
                transposes(sm3[:, un % 2, :], 2 + un % 2, n + 1).then_inc(pt_ps, 1)
                if un + 2 < U3:
                    scores3(un + 2)
                pe.wait_ge(pt_ready, U1 + un + 1)
                if un == 0:
                    pe.wait_ge(vt_done, 18)
                if n == 0 and hh >= 2:
                    pe.wait_ge(o_out, hh - 1)
                for kb in range(n + 1):
                    last = nc.tensor.matmul(ps[:, SX + hh % 2, n * P:(n + 1) * P], v3[:, kb, hh * P:(hh + 1) * P], ev[:, un % 2, kb * P:(kb + 1) * P],
                                            start=(kb == 0), stop=(kb == n))
                if n == NB - 1:
                    last.then_inc(o_ps, 1)
            strips("oout", "A", XT["oo"])
            norm()

        @block.vector
        def _(dve):
            ch = Chain(dve, dve_ch)
            V = nc.vector
            asks, given, nrm, xs = [0], [0], [0], [0]

            def t(k):
                return tab[:, k, :]

            def over(x, axis, n):
                x = x.unsqueeze(axis)
                shape = list(x.shape)
                shape[axis] = n
                return x.to_broadcast(shape)

            dt, lr, th, y, r, mag, sn, cs, ar, ai, den, inv, nr, cr, ci, sci, nsci, t1, t2, m8, w_r, w_i = (
                t(k) for k in (0, 1, 2, 3, 4, 5, 6, 8, 9, 10, 11, 12, 13, 14, 15, 16, 17, 18, 19, 20, 21, 22))
            lre, lim = lam[:, 0, :], lam[:, 1, :]
            dve.wait_ge(in_lam, 16)
            dve.wait_ge(tabs, 1)
            V.tensor_tensor(lr, lre, dt, ALU.mult)
            ch.link(V.tensor_tensor(th, lim, dt, ALU.mult))

            def reduce_angle(x, k):
                ch.link(V.tensor_scalar(k, x, 1.0 / TWO_PI, ROUND, ALU.mult, ALU.add))
                ch.link(V.tensor_scalar(k, k, ROUND, None, ALU.subtract))
                for part in (PI_A, PI_B, PI_C):
                    ch.link(V.scalar_tensor_tensor(x, k, -part, x, ALU.mult, ALU.add))

            reduce_angle(th, y)
            V.tensor_scalar(r, th, -PI_IN, PI_IN, ALU.max, ALU.min).then_inc(ang, 1)
            dve.wait_ge(sq_x, 1)
            V.tensor_reduce(ssum[:, 0, :], S[:, :, :].rearrange("p g c -> p c g"), AX_X, ALU.add).then_inc(ss_x, 1)
            dve.wait_ge(tabs, 2)
            dve.wait_ge(in_cst, 32)
            V.tensor_tensor(ar, mag, cs, ALU.mult)
            V.tensor_tensor(ai, mag, sn, ALU.mult)
            V.tensor_tensor(t1, lre, lre, ALU.mult)
            ch.link(V.tensor_tensor(t2, lim, lim, ALU.mult))
            V.tensor_tensor(den, t1, t2, ALU.add)
            ch.link(V.tensor_scalar(nr, ar, 1.0, None, ALU.subtract))
            V.reciprocal(inv, den)
            V.tensor_tensor(t1, nr, lre, ALU.mult)
            ch.link(V.tensor_tensor(t2, ai, lim, ALU.mult))
            ch.link(V.tensor_tensor(cr, t1, t2, ALU.add))
            V.tensor_tensor(cr, cr, inv, ALU.mult)
            V.tensor_tensor(t1, ai, lre, ALU.mult)
            ch.link(V.tensor_tensor(t2, nr, lim, ALU.mult))
            ch.link(V.tensor_tensor(ci, t1, t2, ALU.subtract))
            ch.link(V.tensor_tensor(ci, ci, inv, ALU.mult))
            V.tensor_scalar(sci, ci, C("nsgn"), None, ALU.mult)
            V.tensor_scalar(nsci, ci, C("sgn"), None, ALU.mult)

            def cmul(o_r, o_i, a_r, a_i, b_r, b_i, s1, s2):
                V.tensor_tensor(s1, a_r, b_r, ALU.mult)
                ch.link(V.tensor_tensor(s2, a_i, b_i, ALU.mult))
                ch.link(V.tensor_tensor(o_r, s1, s2, ALU.subtract))
                V.tensor_tensor(s1, a_r, b_i, ALU.mult)
                ch.link(V.tensor_tensor(s2, a_i, b_r, ALU.mult))
                ch.link(V.tensor_tensor(o_i, s1, s2, ALU.add))

            V.memset(pwr[:, 0, :], 1.0)
            V.memset(pwi[:, 0, :], 0.0)
            V.tensor_copy(pwr[:, 1, :], ar)
            ch.link(V.tensor_copy(pwi[:, 1, :], ai))
            m = 1
            while m < ST:
                ab_r, ab_i = (over(pw[:, m, :], 1, m) for pw in (pwr, pwi))
                s1, s2 = (bt[:, k * 256:k * 256 + GR * m].rearrange("p (r g) -> p r g", r=m) for k in range(2))
                cmul(pwr[:, m + 1:2 * m + 1, :], pwi[:, m + 1:2 * m + 1, :], pwr[:, 1:m + 1, :], pwi[:, 1:m + 1, :], ab_r, ab_i, s1, s2)
                m *= 2
            ch.link(V.tensor_scalar(spi[:, :, :], pwi[:, :, :], C("nsgn"), None, ALU.mult))
            ch.link(V.tensor_tensor(m8, mag, mag, ALU.mult))
            ch.link(V.tensor_tensor(m8, m8, m8, ALU.mult))
            ch.link(V.tensor_tensor(m8, m8, m8, ALU.mult))
            V.tensor_copy(w_r, cs)
            ch.link(V.tensor_copy(w_i, sn))

            def square_turn():
                ch.link(V.tensor_tensor(dt, w_r, w_i, ALU.mult))
                V.tensor_tensor(t1, w_r, w_r, ALU.mult)
                ch.link(V.tensor_tensor(t2, w_i, w_i, ALU.mult))
                V.tensor_tensor(w_r, t1, t2, ALU.subtract)
                ch.link(V.tensor_scalar(w_i, dt, 2.0, None, ALU.mult))

            for _ in range(3):
                square_turn()
            dve.wait_ge(std_x, 1)
            ch.link(V.reciprocal(ssum[:, 2, :], ssum[:, 1, :]))
            ch.link(V.tensor_tensor(u[:, :, :], u[:, :, :], over(ssum[:, 2, :], 1, GR), ALU.mult))
            dve.wait_ge(in_d, 48)
            V.tensor_tensor(u[:, :, :], u[:, :, :], over(gch[:, :], 2, NC), ALU.mult).then_inc(u_ready, 1)
            V.memset(Wc[:, :, 0:1], 1.0)
            ch.link(V.memset(Wsn[:, :, 0:1], 0.0))
            Sf = S[:, :, :].rearrange("p g c -> p (g c)")
            m = 1
            while m < NC:
                s1, s2 = (Sf[:, k * 2048:k * 2048 + GR * m].rearrange("p (g c) -> p g c", g=GR) for k in range(2))
                cmul(Wc[:, :, m:2 * m], Wsn[:, :, m:2 * m], Wc[:, :, 0:m], Wsn[:, :, 0:m], over(w_r, 2, m), over(w_i, 2, m), s1, s2)
                m *= 2
                if m < NC:
                    square_turn()
            dve.wait_ge(in_bc, 16)

            def per_group(x):
                return over(x, 2, GH)

            def by_group(x):
                return x.rearrange("p (g h) -> p g h", h=GH)

            b1, b2 = by_group(bc[:, 0, :]), by_group(bc[:, 1, :])
            bb1, bb2, btg = by_group(bb[:, 0, :]), by_group(bb[:, 1, :]), by_group(bt[:, :])
            for o, x, z, s in ((bb1, b1, b2, sci), (bb2, b2, b1, nsci)):
                V.tensor_tensor(o, x, per_group(cr), ALU.mult)
                ch.link(V.tensor_tensor(btg, z, per_group(s), ALU.mult))
                ch.link(V.tensor_tensor(o, o, btg, ALU.add))
            V.tensor_scalar(bc[:, 2, :], bc[:, 2, :], C("sgn"), None, ALU.mult)
            V.memset(S[:, :, 0:1], 0.0)
            V.memset(dec[:, :, 0:1], 0.0)

            def matrices(out, tr, pw, pi, first, x, z, gs, op):
                def pws(p):
                    return over(p[:, first:first + ST, gs].rearrange("p r g -> p g r"), 3, GH)

                def mat(x):
                    return over(x[:, gs, :], 2, ST)

                def cols4(x):
                    return x.rearrange("p (g r h) -> p g r h", r=ST, h=GH)

                V.tensor_tensor(cols4(out), pws(pw), mat(x), ALU.mult)
                ch.link(V.tensor_tensor(cols4(tr), pws(pi), mat(z), ALU.mult))
                return V.tensor_tensor(out, out, tr, op)

            def turn(sl):
                gs = slice(sl * SG, (sl + 1) * SG)
                cw, sw = Wc[:, gs, :], Wsn[:, gs, :]

                def gc(x):
                    return x.rearrange("p (g c) -> p g c", g=SG)

                dve.wait_ge(v_sb, sl + 1)
                V.tensor_tensor(gc(z1[:, :]), cw, gc(vsb[:, :]), ALU.mult)
                V.tensor_copy(dec[:, :, 1:NC], over(m8[:, gs], 2, NC - 1))
                dve.wait_ge(vp, sl + 1)
                ch.link(V.tensor_tensor(gc(z2[:, :]), sw, gc(ps[:, SY, :]), ALU.mult))
                ch.link(V.tensor_tensor(z1[:, :], z1[:, :], z2[:, :], ALU.add))
                V.tensor_tensor_scan(z2[:, :], dec[:, :, :].rearrange("p g c -> p (g c)"), z1[:, :], 0.0, ALU.mult, ALU.add).then_inc(z_ready, 1)
                dve.wait_ge(z_ready, sl + 1)
                V.tensor_tensor(gc(z1[:, :]), cw, gc(z2[:, :]), ALU.mult)
                dve.wait_ge(zp, sl + 1)
                ch.link(V.tensor_tensor(gc(bt[:, 0:512]), sw, gc(ps[:, SZ, :]), ALU.mult))
                V.tensor_tensor(S[:, gs, 1:NC], gc(z1[:, :])[:, :, 0:NC - 1], gc(bt[:, 0:512])[:, :, 0:NC - 1], ALU.subtract).then_inc(s_ready, 1)
                dve.wait_ge(s_ready, sl + 1)

            for sl in range(NSL):
                gs = slice(sl * SG, (sl + 1) * SG)
                if sl:
                    dve.wait_ge(et_ps, 2 * sl)
                matrices(E[:, :, :].rearrange("p g n -> p (g n)"), bt[:, :], pwr, spi, 0, bb1, bb2, gs, ALU.add).then_inc(e_ready, 1)
                if sl:
                    turn(sl - 1)
            dve.wait_ge(et_ps, 2 * NSL)
            V.tensor_tensor(bt[0:GH, :], d16[:, 0, :], d16[:, 1, :], ALU.mult)
            for b in range(2):
                copied = V.tensor_copy(kst[:, :, 32 * b:32 * b + 32].rearrange("p h g -> p g h"), by_group(ps[:, b, :]))
            ch.link(copied)
            V.tensor_tensor(kst[0:GH, :, :], kst[0:GH, :, :], bt[0:GH, :].rearrange("p (h g) -> p h g", g=GR), ALU.add).then_inc(kst_ready, 1)
            turn(NSL - 1)
            for sl in range(NSL):
                gs = slice(sl * SG, (sl + 1) * SG)
                if sl >= 2:
                    dve.wait_ge(y_ps, sl - 1)
                if sl == 0:
                    dve.wait_ge(s_ready, NSL)
                    dve.wait_ge(kst_ready, 1)
                matrices(G[:, sl % 2, :], bt[:, :], pwr, pwi, 1, by_group(bc[:, 2, :]), by_group(bc[:, 3, :]), gs, ALU.subtract).then_inc(g_ready, 1)
                dve.wait_ge(g_ready, sl + 1)
            for k in range(2):
                dve.wait_ge(y_out[k], 16 * NSL // 2)

            def ask(ins):
                ins.then_inc(to_act, 1)
                asks[0] += 1

            def answered():
                given[0] += 1
                dve.wait_ge(to_dve, given[0])

            def out_ready(name, o, ends=1):
                dve.wait_ge(seg_done, SEG0[name] + ends * (o + 1))

            def bank(name, o):
                return ps[:, (OUT0[name] + o) % RING, :]

            def low(dst, m, src, g=None):
                xs[0] += 1
                dve.wait_ge(x_hi, xs[0])
                hi, lo = X[dst][0][:, m, :].bitcast(F32), X[dst][1][:, m, :]
                if g is None:
                    V.tensor_tensor(lo, src, hi, ALU.subtract).then_inc(x_lo, 1)
                else:
                    V.scalar_tensor_tensor(lo, src, g, hi, ALU.mult, ALU.subtract).then_inc(x_lo, 1)

            adds = [0]

            def start_sum():
                V.memset(acc[:, :], 0.0).then_inc(acc_add, 1)
                adds[0] += 1

            def add_square(last):
                dve.wait_ge(acc_add, adds[0])
                V.tensor_tensor(acc[:, :], acc[:, :], sq[:, :], ALU.add).then_inc(ssq_ready if last else acc_add, 1)
                adds[0] += not last

            def root():
                nrm[0] += 1
                dve.wait_ge(nrm_std, nrm[0])
                ch.link(V.reciprocal(rstd[:, :], std[:, :]))

            def scaled(name, o, dst, ends=1):
                out_ready(name, o, ends)
                V.tensor_tensor(dst, bank(name, o), rstd[:, :], ALU.mult).then_inc(evac, 1)

            def rotate(n, src, dst, part_bank, cos, sin, s1, s2):
                V.tensor_tensor(s1, src, cos, ALU.mult)
                dve.wait_ge(rope_ps, n + 1)
                ch.link(V.tensor_tensor(s2, part_bank, sin, ALU.mult))
                V.tensor_tensor(dst, s1, s2, ALU.add).then_inc(rope_done, 1)

            dve.wait_ge(in_p, 16)
            for k in range(2):
                low("C", k, ev[:, k, :])
            dve.wait_ge(in_y, 16 * NSL * SG)
            for m in range(KT):
                xs[0] += 1
                dve.wait_ge(x_hi, xs[0])
                V.tensor_tensor(X["A"][1][:, m, :].rearrange("p (c t) -> p c t", t=ST), yfm[:, m, :, :].rearrange("p t c -> p c t"),
                                X["A"][0][:, m, :].bitcast(F32).rearrange("p (c t) -> p c t", t=ST), ALU.subtract).then_inc(x_lo, 1)
            dve.wait_ge(in_pos, 16)
            ch.link(V.tensor_copy(std[:, :], acc[:, :].bitcast(I32)))
            ch.link(V.tensor_scalar(std[:, :], std[:, :], C("inv"), None, ALU.mult))
            reduce_angle(std[:, :], sq[:, :])
            ask(V.tensor_scalar(std[:, :], std[:, :], -PI_IN, PI_IN, ALU.max, ALU.min))
            answered()
            for o in range(8):
                out_ready("proj0", o)
                V.tensor_copy(ple[:, o, :], bank("proj0", o)).then_inc(evac, 1)
            start_sum()
            dve.wait_ge(in_h, 16)
            for m in range(KT):
                answered()
                out_ready("glu", 2 * m + 1)
                V.tensor_tensor(ev[:, 0, :], bank("glu", 2 * m + 1), sg[:, :], ALU.mult).then_inc(evac, 2)
                dve.wait_ge(evac, OUT0["glu"] + 2 * m + 2)
                ask(V.tensor_tensor(h[:, m, :], h[:, m, :], ev[:, 0, :], ALU.add))
                low("B", m, h[:, m, :], gain("mlp0", m))
                add_square(m == KT - 1)

            def mlp(layer):
                root()
                for kind, c in (("up", 0), ("up", 1), ("down", 0), ("up", 2), ("down", 1), ("up", 3), ("down", 2), ("down", 3)):
                    name = f"{kind}{layer}_{c}"
                    if kind == "up":
                        x = X["AC"[c % 2]]
                        with dve.Fori(0, 8 // RING) as i:
                            for j in range(RING):
                                o = RING * i + j
                                dve.wait_ge(seg_done, SEG0[name] + o + 1)
                                V.scalar_tensor_tensor(ev[:, 0, :], bank(name, j), 0.0, rstd[:, :], ALU.max, ALU.mult).then_inc(evac, 1)
                                dve.wait_ge(x_hi, xs[0] + o + 1)
                                V.tensor_tensor(x[1][:, o, :], sg[:, :], x[0][:, o, :].bitcast(F32), ALU.subtract).then_inc(x_lo, 1)
                        xs[0] += 8
                    elif c < CHUNKS - 1:
                        with dve.Fori(0, 8 // RING) as i:
                            for j in range(RING):
                                o = RING * i + j
                                dve.wait_ge(seg_done, SEG0[name] + o + 1)
                                V.tensor_tensor(h[:, o, :], bank(name, j), h[:, o, :], ALU.add).then_inc(evac, 1)
                    else:
                        dve.wait_ge(evac, OUT0[name])
                        start_sum()
                        for m in range(KT):
                            out_ready(name, m)
                            V.tensor_tensor(h[:, m, :], bank(name, m), h[:, m, :], ALU.add).then_inc(evac, 1)
                            dve.wait_ge(evac, OUT0[name] + m + 1)
                            low("B", m, h[:, m, :], gain(f"ple{layer}", m))
                            add_square(m == KT - 1)

            def gate(layer):
                name = f"gate{layer}"
                root()
                start_sum()
                for m in range(KT):
                    scaled(name, m, ev[:, 0, :])
                    answered()
                    ch.link(V.tensor_tensor(ev[:, 1, :], sg[:, :], ple[:, m, :], ALU.mult))
                    ask(V.tensor_tensor(h[:, m, :], h[:, m, :], ev[:, 1, :], ALU.add))
                    dve.wait_ge(to_act, asks[0])
                    if layer == 0:
                        low("A", m, h[:, m, :], gain("kvn", m))
                        low("C", m, h[:, m, :], gain("mix1", m))
                    else:
                        answered()
                    add_square(m == KT - 1)

            mlp(0)
            gate(0)
            root()
            dve.wait_ge(seg_done, SEG0["kv"])
            V.memset(k1[:, :, 0:P], 0.0)
            for o in range(4):
                scaled("kv", o, kv1[:, o, :])
            for o in range(8):
                scaled("q", o, q1[:, o, :])
            dve.wait_ge(evac, OUT0["wo"])
            dve.wait_ge(in_a1, 32)
            rc, rs = rope1[:, 0, :], rope1[:, 1, :]
            for j in range(2):
                rotate(j, kv1[:, j, :], k1[:, j, P:], ps[:, SX + j, :], rc, rs, ev[:, 0, :], ev[:, 1, :])
                dve.wait_ge(rope_done, j + 1)

            def rotate_q(m):
                rotate(2 + m, q1[:, m, :], q1[:, m, :], ps[:, SZ, :], rc, rs, ev[:, 0, :], ev[:, 1, :])

            def masked_max(un):
                q0 = 16 * (un % 2)
                mx, mm, ng = cols[:, q0:q0 + 2], cols[:, q0 + 2:q0 + 4], cols[:, q0 + 4:q0 + 6]
                msk = msk1[:, 0:2, :] if un % 2 == 0 else msk1[:, 1:3, :]
                dve.wait_ge(sc_ps, un + 1)
                V.tensor_tensor(sm1[:, un % 2, :, :], ps[:, un % 2, :].rearrange("p (n k) -> p n k", n=2), msk, ALU.add).then_inc(sc_out, 1)
                dve.wait_ge(sc_out, un + 1)
                ch.link(V.tensor_reduce(mx, sm1[:, un % 2, :, :], AX_X, ALU.max))
                ch.link(V.tensor_scalar(mm, mx, float(HD) ** -0.5, gain("sink", un // 4 * 2 + un // 2 % 2), ALU.mult, ALU.max))
                ask(V.tensor_scalar(ng, mm, -1.0, None, ALU.mult))

            def normed(un):
                q0 = 16 * (un % 2)
                rsum, es, dn, rc_ = (cols[:, q0 + k:q0 + k + 2] for k in (6, 8, 10, 12))
                answered()
                ch.link(V.tensor_tensor(dn, rsum, es, ALU.add))
                ch.link(V.reciprocal(rc_, dn))
                V.tensor_scalar(sm1[:, un % 2, 0, :], sm1[:, un % 2, 0, :], rc_[:, 0:1], None, ALU.mult)
                V.tensor_scalar(sm1[:, un % 2, 1, :], sm1[:, un % 2, 1, :], rc_[:, 1:2], None, ALU.mult).then_inc(p_ready, 1)

            rotate_q(0)
            masked_max(0)
            for un in range(U1):
                if un % 4 == 1 and un // 4 + 1 < KT:
                    dve.wait_ge(rope_done, 3 + un // 4)
                    rotate_q(un // 4 + 1)
                if un + 1 < U1:
                    if un >= 1:
                        dve.wait_ge(pt_ps, un)
                    masked_max(un + 1)
                normed(un)
                if un % 4 == 1 and un > 4:
                    low("A", un // 4 - 1, ps[:, SX + (un // 4 - 1) % 2, :])
            low("A", KT - 1, ps[:, SX + (KT - 1) % 2, :])
            start_sum()
            for m in range(KT):
                out_ready("wo", m)
                V.tensor_tensor(h[:, m, :], bank("wo", m), h[:, m, :], ALU.add).then_inc(evac, 1)
                dve.wait_ge(evac, OUT0["wo"] + m + 1)
                low("B", m, h[:, m, :], gain("mlp1", m))
                add_square(m == KT - 1)
            dve.wait_ge(in_p, 32)
            for k in range(2):
                low("C", k, ev[:, k, :])
            for o in range(8):
                out_ready("proj1", o)
                V.tensor_copy(ple[:, o, :], bank("proj1", o)).then_inc(evac, 1)
            mlp(1)
            gate(1)
            root()
            start_sum()
            for m in range(KT):
                ask(V.scalar_tensor_tensor(h[:, m, :], h[:, m, :], gain("fin", m), rstd[:, :], ALU.mult, ALU.mult))
                dve.wait_ge(to_act, asks[0])
                low("C", m, h[:, m, :], gain("pre0", m))
                add_square(m == KT - 1)
            root()
            V.memset(cu[:, 0:2], 0.0)
            for o in range(8):
                scaled("even", o, (q2 if o < 4 else k2)[:, o % 4, :])
            for m in range(8):
                if m >= 2:
                    dve.wait_ge(vt_ps, 2 + m - 1)
                scaled("even", 8 + m, ev[:, m % 2, :])
                qk = (q2 if m < 4 else k2)[:, m % 4, :]
                if m == 0:
                    dve.wait_ge(evac, OUT0["even"] + 8)
                rotate(10 + m, qk, qk, ps[:, SX + m % 2, :], rcos[:, :], rsin[:, :], acc[:, :], cy[:, :])
                dve.wait_ge(rope_done, 10 + m + 1)
            for m in range(8):
                if m < 2:
                    dve.wait_ge(vt_ps, 2 + 7 + m)
                else:
                    dve.wait_ge(silu_done, m - 1)
                scaled("even", 16 + m, ev[:, m % 2, :])
            dve.wait_ge(silu_done, 8)
            E0 = OUT0["even"]
            for k in range(8):
                o = 24 + 4 * k
                scaled("even", o, ev[:, 0, :])
                scaled("even", o + 1, ev[:, 1, :])
                dve.wait_ge(evac, E0 + o + 2)
                ask(V.tensor_tensor(cu[:, 2:], ev[:, 0, :], ev[:, 1, :], ALU.mult))
                dve.wait_ge(to_act, asks[0])
                scaled("even", o + 2, ev[:, 0, :])
                answered()
                ch.link(V.scalar_tensor_tensor(cy[:, :], cu[:, 1:TOK + 1], gain("cw", 8 + k), cy[:, :], ALU.mult, ALU.add))
                ch.link(V.scalar_tensor_tensor(cy[:, :], cu[:, 2:TOK + 2], gain("cw", 16 + k), cy[:, :], ALU.mult, ALU.add))
                ch.link(V.tensor_tensor(cy[:, :], cy[:, :], ev[:, 0, :], ALU.mult))
                scaled("even", o + 3, ev[:, 1, :])
                answered()
                ask(V.tensor_tensor(cy[:, :], cy[:, :], sg[:, :], ALU.mult))
                dve.wait_ge(to_act, asks[0])
                low("A", k, cy[:, :])

            def by_chunk(x):
                return x.rearrange("p (n k) -> p n k", n=NB)

            dve.wait_ge(in_rt, 32)
            dve.wait_ge(x_lo, xs[0])
            for jp in range(RH // 2):
                dve.wait_ge(rk_ps, jp + 1)
                for b in range(2):
                    cc = slice(64 * b, 64 * b + 64)
                    last = V.tensor_scalar(by_chunk(cy[:, :])[:, :, cc], by_chunk(ps[:, SX, :])[:, :, cc],
                                           cst[:, CC["zeta"].start + 2 * jp + b:CC["zeta"].start + 2 * jp + b + 1], None, ALU.mult)
                last.then_inc(rk_sb, 1)
                V.tensor_tensor(by_chunk(sg[:, :]), by_chunk(q2[:, jp, :]), over(xi[:, jp, :], 1, NB), ALU.mult)
                dve.wait_ge(x_lo, xs[0])
                for b in range(2):
                    dve.wait_ge(rs_ps, 2 * jp + b + 1)
                    V.tensor_tensor(by_chunk(ev[:, b, :]), by_chunk(ps[:, b, :]), over(rmask[:, 2 * jp + b, :], 1, NB), ALU.mult).then_inc(rs_sb, 1)
                dve.wait_ge(rkv_ps, jp + 1)
                ch.link(V.tensor_copy(acc[:, P:2 * P], ps[:, SY, 0:P]))
                gam = cst[:, CC["gam"].start + jp:CC["gam"].start + jp + 1]
                for n in range(2, NB):
                    last = V.scalar_tensor_tensor(acc[:, n * P:(n + 1) * P], acc[:, (n - 1) * P:n * P], gam,
                                                  ps[:, SY, (n - 1) * P:n * P], ALU.mult, ALU.add)
                    if n < NB - 1:
                        ch.link(last)
                last.then_inc(rpv, 1)
                for b in range(2):
                    hh = 2 * jp + b
                    root()
                    dve.wait_ge(r_ps, 2 * jp + 2)
                    V.tensor_tensor(ev[:, b, :], ps[:, 2 + b, :], rstd[:, :], ALU.mult).then_inc(r_out, 1)
                    dve.wait_ge(r_out, hh + 1)
                    ask(V.scalar_tensor_tensor(ev[:, b, :], ev[:, b, :], gain("gn", hh), sgr[:, hh, :], ALU.mult, ALU.mult))
                    dve.wait_ge(to_act, asks[0])
                    low("C", hh, ev[:, b, :])

            def post(name, buf, g, ends):
                start_sum()
                for m in range(KT):
                    out_ready(name, m, ends)
                    V.tensor_copy(buf[:, m, :], bank(name, m)).then_inc(evac, 1)
                    answered()
                    add_square(m == KT - 1)
                root()
                if name == "eout":
                    start_sum()
                for m in range(KT):
                    if name == "oout" and m >= 2:
                        dve.wait_ge(fin, m - 1)
                    ch.link(V.scalar_tensor_tensor(ev[:, m % 2, :], buf[:, m, :], gain(g, m), rstd[:, :], ALU.mult, ALU.mult))
                    last = V.tensor_tensor(h[:, m, :], h[:, m, :], ev[:, m % 2, :], ALU.add)
                    if name == "eout":
                        ask(last)
                        dve.wait_ge(to_act, asks[0])
                        low("A", m, h[:, m, :], gain("pre1", m))
                        add_square(m == KT - 1)
                    else:
                        last.then_inc(fin, 1)

            post("eout", ybuf, "post0", 2)
            root()
            for m in range(8):
                if m >= 2:
                    dve.wait_ge(silu_done, 8 + m - 1)
                scaled("odd", m, ev[:, m % 2, :])
            scaled("odd", 8, kr[:, :])
            start_sum()
            for m in range(5):
                scaled("odd", 9 + m, kn[:, m, :])
                answered()
                add_square(m in (2, 4))
                if m == 2:
                    dve.wait_ge(nrm_ps, nrm[0] + 1)
                    start_sum()
            root()
            for m in range(5):
                low("A", m, kn[:, m, :], gain("qa", m) if m < 3 else gain("kva", m - 3))
            dve.wait_ge(silu_done, 16)
            rotate(18, kr[:, :], kr[:, :], ps[:, SX, :], rcos[:, :], rsin[:, :], ev[:, 0, :], ev[:, 1, :])
            dve.wait_ge(rope_done, 19)
            for o in range(12):
                scaled("qb", o, qn[:, o, :] if o < 8 else qr[:, o - 8, :])
            dve.wait_ge(evac, OUT0["kvb"])
            root()
            dve.wait_ge(x_lo, xs[0])
            for o in range(8):
                scaled("kvb", o, kn[:, o, :])
            for m in range(8):
                if m >= 2:
                    dve.wait_ge(vt_ps, 10 + m - 1)
                scaled("kvb", 8 + m, ev[:, m % 2, :])
            dve.wait_ge(evac, OUT0["oout"])
            for m in range(4):
                rotate(19 + m, qr[:, m, :], qr[:, m, :], ps[:, SX + m % 2, :], rcos[:, :], rsin[:, :], sq[:, :], sg[:, :])
                dve.wait_ge(rope_done, 20 + m)
            dve.wait_ge(in_cm, 16)

            def masked_max3(un):
                n, q0 = (un % NB + 1) * P, 8 * (un % 2)
                dve.wait_ge(sc_ps, U1 + un + 1)
                V.tensor_tensor(sm3[:, un % 2, 0:n], ps[:, un % 2, 0:n], cm[:, TOK - n:TOK], ALU.add).then_inc(sc_out, 1)
                dve.wait_ge(sc_out, U1 + un + 1)
                ch.link(V.tensor_reduce(cols[:, q0:q0 + 1], sm3[:, un % 2, 0:n], AX_X, ALU.max))
                ask(V.tensor_scalar(cols[:, q0 + 1:q0 + 2], cols[:, q0:q0 + 1], -MSCALE, None, ALU.mult))

            def normed3(un):
                n, q0 = (un % NB + 1) * P, 8 * (un % 2)
                answered()
                ch.link(V.reciprocal(cols[:, q0 + 3:q0 + 4], cols[:, q0 + 2:q0 + 3]))
                V.tensor_scalar(sm3[:, un % 2, 0:n], sm3[:, un % 2, 0:n], cols[:, q0 + 3:q0 + 4], None, ALU.mult).then_inc(p_ready, 1)

            def gated(hh):
                dve.wait_ge(o_ps, KT + hh + 1)
                V.tensor_tensor(sg[:, :], ps[:, SX + hh % 2, :], sg3[:, hh, :], ALU.mult).then_inc(o_out, 1)
                dve.wait_ge(o_out, hh + 1)
                low("A", hh, sg[:, :])

            masked_max3(0)
            for un in range(U3):
                if un + 1 < U3:
                    if un >= 1:
                        dve.wait_ge(pt_ps, U1 + un)
                    masked_max3(un + 1)
                normed3(un)
                if un % NB == 1 and un > NB:
                    gated(un // NB - 1)
            gated(MH - 1)
            post("oout", ybuf3, "post1", 1)
            assert xs[0] == XT["oo"] + 8
        return nc


def constants():
    f = np.float32
    cst = np.zeros((P, NCC), f)
    cst[:, CC["ident"]] = np.eye(P)
    cst[:, CC["ones"]] = 1.0
    m1, m2, mz = (np.zeros((P, P), f) for _ in range(3))
    for b in (0, 64):
        for d in range(8):
            m1[b + d + 8, b + d], m1[b + d, b + d + 8] = -1.0, 1.0
        for d in range(32):
            m2[b + d + 32, b + d], m2[b + d, b + d + 32] = -1.0, 1.0
    for d in range(64):
        mz[d + 64, d], mz[d, d + 64] = 1.0, -1.0
    cst[:, CC["perm1"]], cst[:, CC["perm2"]], cst[:, CC["permz"]] = m1, m2, mz
    cst[:, CC["eps"]] = EPS
    cst[:, CC["halfpi"]] = np.pi / 2
    cst[:, CC["sgn"]] = np.where(np.arange(P) < 64, 1.0, -1.0)[:, None]
    cst[:, CC["nsgn"]] = -cst[:, CC["sgn"]]
    inv = (f(10000.0) ** (-np.arange(0, MR, 2, dtype=f) / f(MR))).astype(f)
    cst[:, CC["inv"]] = inv[np.arange(P) % 32][:, None]
    lg = np.log1p(-np.exp2(-5.0 - np.arange(RH)))
    k = np.arange(P)
    cst[:, CC["zeta"]] = np.exp(lg[None, :] * (P - 1.0 - k[:, None])) * RDK ** -0.5
    for j in range(4):
        cst[:, CC["gam"].start + j] = np.exp(lg[2 * j + (k >= 64)] * P)
    rel = k[None, :] - k[:, None]
    rmask = np.where(rel[:, None, :] >= 0, np.exp(lg[None, :, None] * np.maximum(rel, 0)[:, None, :]), 0.0) * RDK ** -0.5
    xi = np.stack([np.exp(lg[2 * j + (k >= 64)][:, None] * (k[None, :] + 1.0)) for j in range(4)], 1)
    inv1 = (f(500000.0) ** (-np.arange(0, 16, 2, dtype=f) / f(16))).astype(f)
    ang = (np.arange(TOK, dtype=f)[None, :] * inv1[:, None]).astype(f)
    rope1 = np.zeros((P, 2, TOK), f)
    rope1[:, 0] = 1.0
    for b in (0, 64):
        for q in (0, 8):
            rope1[b + q:b + q + 8, 0], rope1[b + q:b + q + 8, 1] = np.cos(ang), np.sin(ang)
    kj, qi = np.arange(256)[None, :], k[:, None] + P
    band = (kj <= qi) & (qi - kj < WIN)
    gen, first = np.where(band, 0.0, NEG), np.where(band & (kj >= P), 0.0, NEG)
    cm = np.zeros((P, TOK), f)
    cm[:, TOK - P:] = np.where(k[None, :] <= k[:, None], 0.0, NEG)
    blk = (k[:, None] // GH == k[None, :] // GH).astype(f)
    diag = np.repeat(np.eye(GH, dtype=f), GR, 1)
    return {"cst": cst, "rmask": rmask.astype(f), "xi": xi.astype(f), "rope1": rope1, "msk1": np.stack([first, gen, gen], 1).astype(f),
            "cm": cm, "blk": blk}, diag


def strips_of(w, k_tiles=KT):
    K, M = w.shape
    per = KT // k_tiles
    b = w.reshape(k_tiles, P, M // P // per, per, P).transpose(2, 1, 3, 0, 4).reshape(M // P // per, P, per * k_tiles * P)
    return b if b.shape[2] == D else np.concatenate([b, np.zeros(b.shape[:2] + (D - b.shape[2],), w.dtype)], 2)


def layouts(v):
    consts, diag = constants()
    heads = [(2 * j + b) * GQA + g for j in range(2) for g in range(GQA) for b in range(2)]
    hc = (np.array(heads)[:, None] * HD + np.arange(HD)[None, :]).ravel()
    w = {"proj0": strips_of(v["w_ple_proj"][0], 2), "proj1": strips_of(v["w_ple_proj"][1], 2)}
    glu = strips_of(v["ssm_w_glu"][0])
    w["glu"] = np.stack([glu[8:], glu[:8]], 1).reshape(16, P, D)
    for i in range(2):
        for c in range(CHUNKS):
            w[f"up{i}_{c}"] = strips_of(v["w_up"][i][:, c * D:(c + 1) * D])
            w[f"down{i}_{c}"] = strips_of(v["w_down"][i][c * D:(c + 1) * D])
        w[f"gate{i}"] = strips_of(v["w_ple_gate"][i])
    w["kv"] = np.concatenate([strips_of(v["w_k"]), strips_of(v["w_v"])])
    w["q"] = strips_of(v["w_q"][0][:, hc])
    w["wo"] = strips_of(v["w_o"][0][hc])
    ein = strips_of(v["even_w_in_2"][0])
    w["even"] = np.concatenate([ein[:24], np.stack([ein[32:40], ein[40:48], ein[24:32], ein[48:56]], 1).reshape(32, P, D)])
    eo = v["even_w_out_2"][0]
    w["eout"] = np.stack([strips_of(eo[:D]), strips_of(eo[D:])], 1).reshape(16, P, D)
    oi = v["odd_w_in_2"][0]
    kr = oi[:, QL + KL:QL + KL + MR]
    w["odd"] = np.concatenate([strips_of(oi[:, QL + KL + MR:]), strips_of(np.concatenate([kr, kr], 1)), strips_of(oi[:, :QL + KL])])
    qb = v["w_qb_2"][0].reshape(QL, MH, MN + MR)
    qb = np.concatenate([qb[:, :, :MN].reshape(QL, -1), qb[:, :, MN:].reshape(QL, -1)], 1)
    w["qb"] = strips_of(qb, 3)
    kvb = v["w_kvb_2"][0].reshape(KL, MH, 2 * P)
    w["kvb"] = strips_of(np.concatenate([kvb[:, :, :P].reshape(KL, -1), kvb[:, :, P:].reshape(KL, -1)], 1), 2)
    w["oout"] = strips_of(v["odd_w_out_2"][0])

    def cols(x):
        return x.reshape(-1, P).T

    g = {"mix1": v["norm_mix"][1], "kvn": v["kv_norm"], "mlp0": v["norm_mlp"][0], "mlp1": v["norm_mlp"][1], "ple0": v["norm_ple"][0],
         "ple1": v["norm_ple"][1], "fin": v["norm_final"], "pre0": v["pre_norm_2"][0], "pre1": v["pre_norm_2"][1],
         "post0": v["post_norm_2"][0], "post1": v["post_norm_2"][1], "gn": v["ret_gn_2"][0], "qa": v["q_a_norm_2"][0],
         "kva": v["kv_a_norm_2"][0], "cw": v["even_conv_w_2"][0].reshape(-1), "cb": v["even_conv_b_2"][0]}
    gpack = np.concatenate([cols(g[n]) if n != "sink" else np.broadcast_to(v["attn_sinks"][0][heads][None, :], (P, 16)) for n in GC], 1)
    x = v["x"][0]
    xt = x.reshape(NC, ST, GR, GH)[:, ::-1]
    dup = lambda z: np.concatenate([z, z], 0)
    lam = np.stack([dup(v["ssm_lambda_re"][0].T), dup(v["ssm_lambda_im"][0].T),
                    np.broadcast_to(v["ssm_log_dt"][0][None, :], (P, GR))], 1)
    br, bi = (v[n][0].transpose(1, 0, 2).reshape(NST, -1) for n in ("ssm_b_re", "ssm_b_im"))
    cr, ci = (v[n][0].transpose(2, 0, 1).reshape(NST, -1) for n in ("ssm_c_re", "ssm_c_im"))
    bcp = np.stack([np.concatenate(z, 0) for z in ((br, bi), (bi, br), (cr, ci), (ci, cr))], 1)
    d16 = np.stack([np.broadcast_to(v["ssm_d"][0].reshape(GR, GH).T.reshape(1, D), (GH, D)), diag], 1)
    return consts | {
        "w": np.concatenate([w[n] for n, _, _ in PHASES]), "gp": gpack, "lam": lam, "bc": bcp, "d16": d16,
        "gch": np.tile(v["norm_mix"][0].reshape(GR, GH).T, (ST, 1)),
        "xch": xt.transpose(1, 3, 2, 0).reshape(P, GR, NC),
        "xfm": x.T.reshape(KT, P, TOK).transpose(1, 0, 2),
        "p": v["p"][:, 0].transpose(0, 2, 1).reshape(2, 2, P, TOK).transpose(0, 2, 1, 3),
        "pos": v["positions_2"][0],
    }


def kernel(**inputs):
    import concourse.bacc as bacc
    from concourse.bass_utils import run_bass_kernel_spmd as run

    arrays = {k: np.ascontiguousarray(x) for k, x in layouts({k: np.asarray(x) for k, x in inputs.items()}).items()}
    nc = bacc.Bacc("TRN2", target_bir_lowering=False, num_devices=1)
    a = {k: nc.dram_tensor("in_" + k, x.shape, mybir.dt.from_np(x.dtype), kind="ExternalInput").ap() for k, x in arrays.items()}
    a["out"] = nc.dram_tensor("out", (KT, P, TOK), F32, kind="ExternalOutput").ap()
    program(nc, a)
    arrays = {"in_" + k: x for k, x in arrays.items()}
    got = run(nc, [arrays], core_ids=[0]).results[0]["out"]
    return np.ascontiguousarray(got.reshape(D, TOK).T)[None]
```

```python
from contextlib import ExitStack

import numpy as np

import concourse.bass as bass
from concourse import mybir

F32 = mybir.dt.float32
FR = mybir.dt.float32r
I32 = mybir.dt.int32
ALU = mybir.AluOpType
ACT = mybir.ActivationFunctionType
AX_X = mybir.AxisListType.X

P = 128
TOK = 512
D = 1024
KT = D // P
FF = 4 * D
CHUNKS = FF // D
PLE = 256
EPS = 1e-6
NEG = -1e30

GR, GH, NST = 64, 16, 64
ST = P // GH
NC = TOK // ST
LEVELS = 6
assert 2 ** LEVELS == NC
SG = 8
NSL = GR // SG
W8 = SG * P

HD, NKV, GQA, WIN = 64, 4, 4, 128
NB = TOK // P
RH, RDK = 8, 64
MH, MN, MR = 8, 128, 64
QL, KL = 384, 256

RING = 4
SLOTS = 4
LEAD = RING - 1

PHASES = [
    ("proj0", 2, 4), ("glu", 16, 1),
    *[(f"{k}0_{c}", 8, 1) for k, c in (("up", 0), ("up", 1), ("down", 0), ("up", 2), ("down", 1), ("up", 3), ("down", 2), ("down", 3))],
    ("gate0", 8, 1), ("kv", 4, 1), ("q", 8, 1), ("wo", 8, 1), ("proj1", 2, 4),
    *[(f"{k}1_{c}", 8, 1) for k, c in (("up", 0), ("up", 1), ("down", 0), ("up", 2), ("down", 1), ("up", 3), ("down", 2), ("down", 3))],
    ("gate1", 8, 1), ("even", 56, 1), ("eout", 16, 1), ("odd", 6, 1), ("qb", 6, 2), ("kvb", 4, 4), ("mgate", 8, 1), ("oout", 8, 1),
]
N_OUT = {"eout": 8}
S0, SEG0, OUT0, NSTR, SEGS = {}, {}, {}, {}, {}
_s = _g = _o = 0
for _name, _n, _k in PHASES:
    S0[_name], SEG0[_name], OUT0[_name], NSTR[_name], SEGS[_name] = _s, _g, _o, _n, _k
    _s, _g, _o = _s + _n, _g + _n * _k, _o + N_OUT.get(_name, _n * _k)
NS = _s
assert NS % RING == 0

XT = {}
_x = 0
for _name, _n in [("p0", 2), ("y", 8), ("mlp0", 8), ("hid0_0", 8), ("hid0_1", 8), ("hid0_2", 8), ("hid0_3", 8), ("gate0", 8),
                  ("kvq", 16), ("o", 8), ("p1", 2), ("mlp1", 8), ("hid1_0", 8), ("hid1_1", 8), ("hid1_2", 8), ("hid1_3", 8),
                  ("gate1", 8), ("even", 8), ("conv", 8), ("ret", 8), ("odd", 8), ("lat", 5), ("oo", 8)]:
    XT[_name] = _x
    _x += _n

CC = {}
_c = 0
for _name, _n in [("ident", P), ("perm1", P), ("perm2", P), ("permz", P), ("ones", P),
                  ("eps", 1), ("halfpi", 1), ("sgn", 1), ("nsgn", 1), ("inv", 1), ("gam", 4), ("zeta", RH)]:
    CC[_name] = slice(_c, _c + _n)
    _c += _n
NCC = _c
GC = {}
_c = 0
for _name, _n in [("mix1", 8), ("kvn", 8), ("mlp0", 8), ("mlp1", 8), ("ple0", 8), ("ple1", 8), ("fin", 8), ("pre0", 8), ("pre1", 8),
                  ("post0", 8), ("post1", 8), ("gn", 8), ("qa", 3), ("kva", 2), ("cw", 24), ("cb", 8), ("sink", 16)]:
    GC[_name] = slice(_c, _c + _n)
    _c += _n
NGC = _c

TWO_PI = 2 * np.pi
ROUND = 12582912.0
PI_A = 6.28125
PI_B = float(np.float32(np.round((TWO_PI - PI_A) * 2**20) / 2**20))
PI_C = float(TWO_PI - PI_A - PI_B)
PI_IN = 3.1415925


class Chain:

    def __init__(self, eng, sem):
        self.eng, self.sem, self.n, self.at = eng, sem, 0, None

    def now(self):
        return self.n if self.at is None else self.n + self.at[0] * self.at[1]

    def link(self, ins):
        ins.then_inc(self.sem, 1)
        self.n += 1
        self.eng.wait_ge(self.sem, self.now())

    def each(self, i, per):
        self.at, self.first = (i, per), self.n

    def done(self, count):
        assert self.n - self.first == self.at[1], (self.n - self.first, self.at[1])
        self.n, self.at = self.first + self.at[1] * count, None


def program(nc, a):
    with ExitStack() as top:
        def sem(name):
            return top.enter_context(nc.semaphore(name))

        def area(stack, name, shape, dt=F32):
            return stack.enter_context(nc.sbuf_tensor(name, shape, dt))

        ps = top.enter_context(nc.psum_tensor("ps", [P, 8, 512], F32))
        NRM, SX, SY, SZ = 4, 5, 6, 7
        raw = area(top, "raw", [P, RING, D])
        cst = area(top, "cst", [P, NCC])
        gp = area(top, "gp", [P, NGC])
        with ExitStack() as s5:
            Wc = area(s5, "Wc", [P, GR, NC])
            Wsn = area(s5, "Wsn", [P, GR, NC])
            bb = area(s5, "bb", [P, 2, GR * GH])
            E = area(s5, "E", [P, 2, SG, P])
            ET = area(s5, "ET", [P, SG, P])
            vsb = area(s5, "vsb", [P, 512])
            z1 = area(s5, "z1", [P, 512])
            z2 = area(s5, "z2", [P, 512])
            z3 = area(s5, "z3", [P, 512])
            dec = area(s5, "dec", [P, SG, NC])
            lam = area(s5, "lam", [P, 3, GR])
            wt = area(s5, "wt", [P, LEVELS, 2, GR])
            T = area(s5, "T", [P, ST * GH, GR])
            S = area(s5, "S", [P, GR, NC])
            u = area(s5, "u", [P, GR, NC])
            bB = area(s5, "bB", [P, 2, GR * GH])
            d16 = area(s5, "d16", [GH, 2, D])
            tab = area(s5, "tab", [P, 24, GR])
            bC = area(s5, "bC", [P, 2, GR * GH])
            pwr = area(s5, "pwr", [P, ST + 1, GR])
            pwi = area(s5, "pwi", [P, ST + 1, GR])
            spi = area(s5, "spi", [P, ST + 1, GR])
            bt = area(s5, "bt", [P, W8])
            kst = area(s5, "kst", [P, GH, GR])
            blk = area(s5, "blk", [P, P])
            gch = area(s5, "gch", [P, GR])
            ssum = area(s5, "ssum", [P, 3, NC])
            G = area(s5, "G", [P, 2, SG * P])
            yg = area(s5, "yg", [P, 2, 512])
        main = top.enter_context(ExitStack())
        whi = area(main, "whi", [P, RING, D], FR)
        wlo = area(main, "wlo", [P, RING, D], FR)
        h = area(main, "h", [P, KT, TOK])
        rcos = area(main, "rcos", [P, TOK])
        rsin = area(main, "rsin", [P, TOK])
        ev = area(main, "ev", [P, 2, TOK])
        sg = area(main, "sg", [P, TOK])
        sq = area(main, "sq", [P, TOK])
        acc = area(main, "acc", [P, TOK])
        std = area(main, "std", [P, TOK])
        rstd = area(main, "rstd", [P, TOK])
        cols = area(main, "cols", [P, 64])
        X = {}

        def pair(stack, name, tiles=KT):
            X[name] = (area(stack, name + "h", [P, tiles, TOK], FR), area(stack, name + "l", [P, tiles, TOK], FR))

        pair(main, "A")
        with ExitStack() as st:
            pair(st, "C")
            with ExitStack() as st2:
                pair(st2, "B")
                ple = area(st2, "ple", [P, KT, TOK])
            with ExitStack() as st2:
                yfm = area(st2, "yfm", [P, KT, ST, NC])
            with ExitStack() as st2:
                q1 = area(st2, "q1", [P, 8, TOK])
                k1 = area(st2, "k1", [P, 2, TOK + P])
                kv1 = area(st2, "kv1", [P, 4, TOK])
                v1 = area(st2, "v1", [P, NB, 256])
                rope1 = area(st2, "rope1", [P, 2, TOK])
                msk1 = area(st2, "msk1", [P, 3, 256])
                sm1 = area(st2, "sm1", [P, SLOTS, 2, 256])
                pt1 = area(st2, "pt1", [P, 2, 512])
            with ExitStack() as st2:
                q2 = area(st2, "q2", [P, 4, TOK])
                k2 = area(st2, "k2", [P, 4, TOK])
                v2 = area(st2, "v2", [P, NB, D])
                sgr = area(st2, "sgr", [P, KT, TOK])
                cu = area(st2, "cu", [P, TOK + 2])
                cy = area(st2, "cy", [P, TOK])
            with ExitStack() as st2:
                ybuf = area(st2, "ybuf", [P, KT, TOK])
        with ExitStack() as st2:
            for k in ("C",):
                area(st2, "pad_c", [P, 2 * KT * TOK])
            area(st2, "pad_b", [P, 3 * KT * TOK + SLOTS * TOK // 2 + 8])
            rmask = area(st2, "rmask", [P, RH, P])
            xi = area(st2, "xi", [P, 4, P])
        with ExitStack() as st:
            qn = area(st, "qn", [P, MH, TOK])
            kn = area(st, "kn", [P, MH, TOK])
            qr = area(st, "qr", [P, 4, TOK])
            kr = area(st, "kr", [P, TOK])
            v3 = area(st, "v3", [P, NB, D])
            cm = area(st, "cm", [P, TOK])
            sm3 = area(st, "sm3", [P, SLOTS, TOK])
            with ExitStack() as st2:
                pair(st2, "L", 5)
            with ExitStack() as st2:
                sg3 = area(st2, "sg3", [P, KT, TOK])
        ybuf3 = sg3
        ysc = nc.dram_tensor("ysc", [NSL, P, 512], F32, kind="Internal").ap()

        raw_in = [sem(f"raw_in{r}") for r in range(RING)]
        hi_ready = sem("hi_ready")
        lo_ready = sem("lo_ready")
        seg_done = sem("seg_done")
        evac = sem("evac")
        x_hi = sem("x_hi")
        x_lo = sem("x_lo")
        to_act = sem("to_act")
        to_dve = sem("to_dve")
        ssq_ready = sem("ssq_ready")
        sq_used = sem("sq_used")
        nrm_ps = sem("nrm_ps")
        nrm_std = sem("nrm_std")
        acc_add = sem("acc_add")
        rope_ps = sem("rope_ps")
        rope_done = sem("rope_done")
        vt_ps = sem("vt_ps")
        vt_done = sem("vt_done")
        silu_done = sem("silu_done")
        dve_ch, act_ch, pool_ch = sem("dve_ch"), sem("act_ch"), sem("pool_ch")
        in_cst, in_lam, in_bc, in_x, in_d = sem("in_cst"), sem("in_lam"), sem("in_bc"), sem("in_x"), sem("in_d")
        in_h, in_p, in_pos = sem("in_h"), sem("in_p"), sem("in_pos")
        in_y = [sem(f"in_y{sl}") for sl in range(NSL)]
        in_a1, in_rt, in_cm = sem("in_a1"), sem("in_rt"), sem("in_cm")
        fin, out_sem = sem("fin"), sem("out_sem")
        tabs, ang, sq_x, ss_x, ss_ps, std_x, u_ready = (sem(n) for n in ("tabs", "ang", "sq_x", "ss_x", "ss_ps", "std_x", "u_ready"))
        c_ready = sem("c_ready")
        u_gain, turns, w_ready = sem("u_gain"), sem("turns"), sem("w_ready")
        e_ready, e_used, et_ps, et_sb, v_ps, v_sb, vp, z_ready, zp, s_ready = (
            sem(n) for n in ("e_ready", "e_used", "et_ps", "et_sb", "v_ps", "v_sb", "vp", "z_ready", "zp", "s_ready"))
        kst_ready, t_zero, toep, g_ready, y_ps, yg_ready = (sem(n) for n in ("kst_ready", "t_zero", "toep", "g_ready", "y_ps", "yg_ready"))
        y_out = [sem("y_out0"), sem("y_out1")]
        sc_ps, sc_out, p_ready, pt_ps, pt_ready, o_ps, o_out = (sem(n) for n in ("sc_ps", "sc_out", "p_ready", "pt_ps", "pt_ready", "o_ps", "o_out"))
        rk_ps, rs_ps, rk_sb, rs_sb, rkv_ps, rpv, r_ps, r_out = (
            sem(n) for n in ("rk_ps", "rs_ps", "rk_sb", "rs_sb", "rkv_ps", "rpv", "r_ps", "r_out"))

        def C(name):
            return cst[:, CC[name]]

        def gain(name, m):
            return gp[:, GC[name].start + m:GC[name].start + m + 1]

        eps = C("eps")
        U1 = 8 * 2 * 2
        U3 = MH * NB
        MSCALE = float(MN + MR) ** -0.5
        LAT_K = {"qb": 3, "kvb": 2}

        squares = (sq, cy)
        finpre = cols[:, 0:KT]
        acc2 = cu[:, 2:]

        block = top.enter_context(nc.Block())

        @block.sync
        def _(sp):
            sp.dma_start(lam[:, :, :], a["lam"]).then_inc(in_lam, 16)
            sp.dma_start(cst[:, :], a["cst"]).then_inc(in_cst, 16)
            sp.dma_start(gp[:, :], a["gp"]).then_inc(in_cst, 16)
            sp.dma_start(bB[:, :, :], a["bc"][:, 0:2, :]).then_inc(in_bc, 16)
            sp.dma_start(u[:, :, :], a["xch"]).then_inc(in_x, 16)
            sp.dma_start(gch[:, :], a["gch"]).then_inc(in_d, 16)
            sp.dma_start(blk[:, :], a["blk"]).then_inc(in_d, 16)
            sp.dma_start(bC[:, :, :], a["bc"][:, 2:4, :]).then_inc(in_bc, 16)
            sp.dma_start(d16[:, :, :], a["d16"]).then_inc(in_d, 16)
            for r in range(RING):
                sp.dma_start(raw[:, r, :], a["w"][r, :, :]).then_inc(raw_in[r], 16)
            sp.wait_ge(kst_ready, 1)
            sp.wait_ge(t_zero, 1)
            for t in range(ST):
                sp.dma_start(T[GH * (ST - 1 - t):P, GH * t:GH * (t + 1), :], kst[0:GH * (t + 1), :, :]).then_inc(toep, 16)
            sp.wait_ge(s_ready, NSL)
            sp.dma_start(ev[:, :, :], a["p"][0, :, :, :]).then_inc(in_p, 16)
            sp.dma_start(h[:, :, :], a["xfm"]).then_inc(in_h, 16)
            sp.dma_start(rcos[:, :].bitcast(I32), a["pos"].partition_broadcast(P)).then_inc(in_pos, 16)

            def back(sl):
                sp.wait_ge(y_out[sl % 2], 16 * (sl // 2 + 1))
                for g in range(SG):
                    sp.dma_start(yfm[GH * g:GH * (g + 1), sl, :, :],
                                 ysc[sl, :, g * NC:(g + 1) * NC].rearrange("(t h) c -> h t c", h=GH)).then_inc(in_y[sl], 16)

            for sl in range(NSL):
                sp.wait_ge(yg_ready, sl + 1)
                sp.dma_start(ysc[sl, :, :], yg[:, sl % 2, :]).then_inc(y_out[sl % 2], 16)
                if sl:
                    back(sl - 1)
            back(NSL - 1)
            sp.dma_start(rmask[:, :, :], a["rmask"]).then_inc(in_rt, 16)
            sp.dma_start(xi[:, :, :], a["xi"]).then_inc(in_rt, 16)
            with sp.Fori(1, NS // RING) as i:
                for r in range(RING):
                    sp.wait_ge(lo_ready, RING * i + (r - RING + 1))
                    sp.dma_start(raw[:, r, :], a["w"][RING * i + r, :, :]).then_inc(raw_in[r], 16)
            for m in range(KT):
                sp.wait_ge(fin, m + 1)
                sp.dma_start(a["out"][m, :, :], h[:, m, :]).then_inc(out_sem, 16)
            sp.wait_ge(out_sem, 16 * KT)

        @block.gpsimd
        def _(pool):
            ch = Chain(pool, pool_ch)
            pool.wait_ge(sq_x, 1)
            pool.wait_ge(in_d, 48)
            nc.gpsimd.tensor_tensor(u[:, :, :], u[:, :, :], gch[:, :].unsqueeze(2).to_broadcast([P, GR, NC]), ALU.mult).then_inc(u_gain, 1)
            pool.wait_ge(turns, 1)
            Tf = T[:, :, :].rearrange("p m g -> p (m g)")
            for half in range(2):
                gs = slice(half * GR // 2, (half + 1) * GR // 2)
                nc.gpsimd.memset(Wc[:, gs, 0:1], 1.0)
                ch.link(nc.gpsimd.memset(Wsn[:, gs, 0:1], 0.0))
                for k in range(LEVELS):
                    m = 2 ** k
                    w_r, w_i = (wt[:, k, q, gs].unsqueeze(2).to_broadcast([P, GR // 2, m]) for q in range(2))
                    s1, s2, s3, s4 = (Tf[:, q * 1024:q * 1024 + GR // 2 * m].rearrange("p (g c) -> p g c", c=m) for q in range(4))
                    nc.gpsimd.tensor_tensor(s1, Wc[:, gs, 0:m], w_r, ALU.mult)
                    nc.gpsimd.tensor_tensor(s2, Wsn[:, gs, 0:m], w_i, ALU.mult)
                    nc.gpsimd.tensor_tensor(s3, Wc[:, gs, 0:m], w_i, ALU.mult)
                    ch.link(nc.gpsimd.tensor_tensor(s4, Wsn[:, gs, 0:m], w_r, ALU.mult))
                    nc.gpsimd.tensor_tensor(Wc[:, gs, m:2 * m], s1, s2, ALU.subtract)
                    last = nc.gpsimd.tensor_tensor(Wsn[:, gs, m:2 * m], s3, s4, ALU.add)
                    if k < LEVELS - 1:
                        ch.link(last)
                last.then_inc(w_ready, 1)
                pool.wait_ge(w_ready, half + 1)
            nc.gpsimd.memset(T[:, :, :], 0.0).then_inc(t_zero, 1)
            with pool.Fori(0, NS // RING) as i:
                for r in range(RING):
                    pool.wait_ge(hi_ready, RING * i + r + 1)
                    nc.gpsimd.tensor_tensor(wlo[:, r, :], raw[:, r, :], whi[:, r, :].bitcast(F32), ALU.subtract).then_inc(lo_ready, 1)

        @block.scalar
        def _(act):
            ch = Chain(act, act_ch)
            got = [0]
            nrm = [0]
            xs = [0]

            act.wait_ge(in_lam, 16)
            nc.scalar.activation(tab[:, 0, :], lam[:, 2, :], ACT.Exp).then_inc(tabs, 1)
            act.wait_ge(ang, 1)
            act.wait_ge(in_cst, 32)
            nc.scalar.activation(tab[:, 5, :], tab[:, 1, :], ACT.Exp)
            nc.scalar.activation(tab[:, 6, :], tab[:, 4, :], ACT.Sin)
            ch.link(nc.scalar.activation(tab[:, 7, :], tab[:, 4, :], ACT.Abs))
            nc.scalar.activation(tab[:, 8, :], tab[:, 7, :], ACT.Sin, bias=C("halfpi"), scale=-1.0).then_inc(tabs, 1)
            act.wait_ge(in_x, 16)
            nc.scalar.activation(S[:, :, :], u[:, :, :], ACT.Square).then_inc(sq_x, 1)
            act.wait_ge(ss_ps, 1)
            nc.scalar.activation(ssum[:, 1, :], ps[:, NRM, 0:NC], ACT.Sqrt, bias=eps, scale=1.0 / D).then_inc(std_x, 1)
            for sl in range(NSL):
                if sl:
                    act.wait_ge(v_ps, sl)
                for half in range(2):
                    act.wait_ge(et_ps, 2 * sl + half + 1)
                    nc.scalar.copy(ET[:, 4 * half:4 * half + 4, :], ps[:, 2 + half, :].rearrange("p (g n) -> p g n", g=4)).then_inc(et_sb, 1)
                act.wait_ge(v_ps, sl + 1)
                if sl:
                    act.wait_ge(z_ready, sl)
                nc.scalar.copy(vsb[:, :], ps[:, SX, :]).then_inc(v_sb, 1)
            def split_strip(t, seg, slot=None, turn=None):
                if slot is None:
                    slot, turn = t % RING, t // RING + 1
                act.wait_ge(raw_in[slot], 16 * turn)
                if not isinstance(seg, int) or seg > 0:
                    act.wait_ge(seg_done, seg)
                nc.scalar.activation(whi[:, slot, :], raw[:, slot, :], ACT.Copy).then_inc(hi_ready, 1)

            def ahead(name, l):
                t = S0[name] + l + LEAD
                if t < NS:
                    split_strip(t, SEG0[name] + SEGS[name] * l)

            def ahead_loop(name, i, j):
                t = S0[name] + j + LEAD
                split_strip(None, SEG0[name] + SEGS[name] * j + SEGS[name] * RING * i, t % RING, t // RING + 1 + i)

            def answer(ins):
                ins.then_inc(to_dve, 1)

            def asked():
                got[0] += 1
                act.wait_ge(to_act, got[0])

            def high(dst, m, src, scale=None):
                if scale is None:
                    nc.scalar.activation(X[dst][0][:, m, :], src, ACT.Copy).then_inc(x_hi, 1)
                else:
                    nc.scalar.activation(X[dst][0][:, m, :], src, ACT.Copy, scale=scale).then_inc(x_hi, 1)
                xs[0] += 1

            def root(n):
                nrm[0] += 1
                act.wait_ge(nrm_ps, nrm[0])
                nc.scalar.activation(std[:, :], ps[:, NRM, :], ACT.Sqrt, bias=eps, scale=1.0 / n).then_inc(nrm_std, 1)

            act.wait_ge(s_ready, NSL)
            for t in range(LEAD):
                split_strip(t, 0)
            for sl in range(NSL):
                act.wait_ge(y_ps, sl + 1)
                if sl >= 2:
                    act.wait_ge(y_out[sl % 2], 16 * (sl // 2))
                nc.scalar.activation(yg[:, sl % 2, :], ps[:, 2 + sl % 2, :], ACT.Gelu_apprx_tanh).then_inc(yg_ready, 1)
            act.wait_ge(in_p, 16)
            for k in range(2):
                high("C", k, ev[:, k, :])
            for m in range(KT):
                act.wait_ge(in_y[m], 16 * SG)
                nc.scalar.activation(X["A"][0][:, m, :].rearrange("p (c t) -> p c t", t=ST),
                                     yfm[:, m, :, :].rearrange("p t c -> p c t"), ACT.Copy).then_inc(x_hi, 1)
                xs[0] += 1
            for l in range(2):
                ahead("proj0", l)
            asked()
            ch.link(nc.scalar.activation(rcos[:, :], rsin[:, :], ACT.Abs))
            nc.scalar.activation(rsin[:, :], rsin[:, :], ACT.Sin)
            answer(nc.scalar.activation(rcos[:, :], rcos[:, :], ACT.Sin, bias=C("halfpi"), scale=-1.0))
            for m in range(KT):
                ahead("glu", 2 * m)
                ahead("glu", 2 * m + 1)
                o = OUT0["glu"] + 2 * m
                act.wait_ge(seg_done, SEG0["glu"] + 2 * m + 1)
                answer(nc.scalar.activation(sg[:, :], ps[:, o % RING, :], ACT.Sigmoid))
                asked()
                nc.scalar.activation(sq[:, :], h[:, m, :], ACT.Square)
                high("B", m, h[:, m, :], gain("mlp0", m))

            def mlp(layer):
                root(D)
                for kind, c in (("up", 0), ("up", 1), ("down", 0), ("up", 2), ("down", 1), ("up", 3), ("down", 2), ("down", 3)):
                    name = f"{kind}{layer}_{c}"
                    if kind == "up":
                        dst = X["AC"[c % 2]][0]
                        with act.Fori(0, 8 // RING) as i:
                            for j in range(RING):
                                ahead_loop(name, i, j)
                                act.wait_ge(evac, OUT0[name] + RING * i + j + 1)
                                nc.scalar.activation(sg[:, :], ev[:, 0, :], ACT.Square)
                                nc.scalar.activation(dst[:, RING * i + j, :], ev[:, 0, :], ACT.Square).then_inc(x_hi, 1)
                        xs[0] += 8
                    elif c < CHUNKS - 1:
                        with act.Fori(0, 8 // RING) as i:
                            for j in range(RING):
                                ahead_loop(name, i, j)
                    else:
                        for m in range(KT):
                            ahead(name, m)
                            act.wait_ge(evac, OUT0[name] + m + 1)
                            nc.scalar.activation(sq[:, :], h[:, m, :], ACT.Square)
                            high("B", m, h[:, m, :], gain(f"ple{layer}", m))

            def gate(layer):
                root(D)
                for m in range(KT):
                    ahead(f"gate{layer}", m)
                    act.wait_ge(evac, OUT0[f"gate{layer}"] + m + 1)
                    answer(nc.scalar.activation(sg[:, :], ev[:, 0, :], ACT.Sigmoid))
                    asked()
                    nc.scalar.activation(sq[:, :], h[:, m, :], ACT.Square)
                    if layer == 0:
                        high("A", m, h[:, m, :], gain("kvn", m))
                        high("C", m, h[:, m, :], gain("mix1", m))
                    else:
                        nc.scalar.activation(cy[:, :], h[:, m, :], ACT.Square, scale=gain("fin", m))
                        high("C", m, h[:, m, :], finpre[:, m:m + 1])

            mlp(0)
            gate(0)
            act.wait_ge(seg_done, SEG0["kv"])
            act.wait_ge(x_lo, XT["kvq"] + 16)
            act.dma_start(rope1[:, :, :], a["rope1"]).then_inc(in_a1, 16)
            act.dma_start(msk1[:, :, :], a["msk1"]).then_inc(in_a1, 16)
            root(D)
            for l in range(NSTR["kv"]):
                ahead("kv", l)
            for l in range(2):
                ahead("q", l)
            for j in range(2):
                act.wait_ge(vt_ps, j + 1)
                nc.scalar.copy(v1[:, :, j * P:(j + 1) * P], ps[:, NRM, :].rearrange("p (n d) -> p n d", n=NB)).then_inc(vt_done, 1)

            act.dma_start(sq[:, :], a["p"][1, :, 0, :]).then_inc(in_p, 16)
            act.dma_start(acc[:, :], a["p"][1, :, 1, :]).then_inc(in_p, 16)

            def exp1(un):
                b, q0 = un // 2 % 2, 16 * (un % SLOTS)
                sink = gain("sink", un // 4 * 2 + b)
                asked()
                for n in range(2):
                    nc.scalar.activation(sm1[:, un % SLOTS, n, :], sm1[:, un % SLOTS, n, :], ACT.Exp, bias=cols[:, q0 + 4 + n:q0 + 5 + n],
                                         scale=float(HD) ** -0.5, accum_out=cols[:, q0 + 6 + n:q0 + 7 + n])
                answer(nc.scalar.activation(cols[:, q0 + 8:q0 + 10], cols[:, q0 + 4:q0 + 6], ACT.Exp, bias=sink))

            exp1(0)
            exp1(1)
            for un in range(U1):
                if un + 2 < U1:
                    exp1(un + 2)
                if un % 4 == 1 and un // 4 + 2 < NSTR["q"]:
                    ahead("q", un // 4 + 2)
                act.wait_ge(pt_ps, un + 1)
                nc.scalar.copy(pt1[:, un % 2, :], ps[:, 2 + un % 2, :]).then_inc(pt_ready, 1)
                if un % 4 == 1 and un > 4:
                    m = un // 4 - 1
                    act.wait_ge(o_ps, m + 1)
                    high("A", m, ps[:, SX + m % 2, :])
            act.wait_ge(o_ps, KT)
            high("A", KT - 1, ps[:, SX + (KT - 1) % 2, :])
            act.wait_ge(in_p, 48)
            for k in range(2):
                high("C", k, (sq, acc)[k][:, :])
            for m in range(KT):
                ahead("wo", m)
                act.wait_ge(evac, OUT0["wo"] + m + 1)
                nc.scalar.activation(sq[:, :], h[:, m, :], ACT.Square)
                high("B", m, h[:, m, :], gain("mlp1", m))
            for l in range(2):
                ahead("proj1", l)
            mlp(1)
            gate(1)
            E0 = OUT0["even"]
            for l in range(2):
                ahead("even", l)
            root(D)
            nrm[0] += 1
            asked()
            nc.scalar.activation(std[:, :], sq[:, :], ACT.Sqrt, bias=eps, scale=1.0 / D).then_inc(nrm_std, 1)
            for l in range(2, 8):
                ahead("even", l)

            def value(n, dst, m):
                act.wait_ge(vt_ps, n + 1)
                nc.scalar.copy(dst[:, :, m * P:(m + 1) * P], ps[:, SZ, :].rearrange("p (n d) -> p n d", n=NB)).then_inc(vt_done, 1)

            for m in range(8):
                ahead("even", 8 + m)
                if m:
                    value(2 + m - 1, v2, m - 1)
            value(2 + 7, v2, 7)
            for m in range(8):
                ahead("even", 16 + m)
                act.wait_ge(evac, E0 + 16 + m + 1)
                nc.scalar.activation(sgr[:, m, :], ev[:, m % 2, :], ACT.Silu).then_inc(silu_done, 1)
            def head_squares(hh):
                act.wait_ge(r_ps, hh + 1)
                nc.scalar.activation(sq[:, :], ps[:, (SZ, SY)[hh % 2], :], ACT.Square).then_inc(ssq_ready, 1)

            for t in range(8):
                jp = t // 2
                ahead("even", 24 + 4 * t)
                if t % 2:
                    head_squares(2 * jp)
                ahead("even", 24 + 4 * t + 1)
                if t % 2:
                    root(P)
                    head_squares(2 * jp + 1)
                ahead("even", 24 + 4 * t + 2)
                asked()
                answer(nc.scalar.activation(cy[:, :], cu[:, 0:TOK], ACT.Identity, bias=gain("cb", t), scale=gain("cw", t)))
                if t % 2:
                    act.wait_ge(r_out, 2 * jp + 1)
                    root(P)
                ahead("even", 24 + 4 * t + 3)
                act.wait_ge(evac, E0 + 24 + 4 * t + 4)
                answer(nc.scalar.activation(sg[:, :], ev[:, 0, :], ACT.Silu))
                asked()
                high("A", t, cy[:, :])
            act.wait_ge(seg_done, SEG0["eout"])
            for hh in range(RH):
                act.wait_ge(r_out, hh + 1)
                high("C", hh, sgr[:, hh, :])

            def post(name):
                for m in range(KT):
                    for l in ((2 * m, 2 * m + 1) if name == "eout" else (m,)):
                        ahead(name, l)
                    act.wait_ge(evac, OUT0[name] + m + 1)
                    answer(nc.scalar.activation(sq[:, :], (ybuf if name == "eout" else ybuf3)[:, m, :], ACT.Square))
                root(D)

            post("eout")
            act.dma_start(cm[:, :], a["cm"]).then_inc(in_cm, 16)
            for m in range(KT):
                asked()
                if m >= 2:
                    act.wait_ge(sq_used, m - 1)
                nc.scalar.activation(squares[m % 2][:, :], h[:, m, :], ACT.Square)
                high("A", m, h[:, m, :], gain("pre1", m))
            root(D)
            O0 = OUT0["odd"]
            ahead("odd", 0)
            for m in range(5):
                ahead("odd", 1 + m)
                act.wait_ge(evac, O0 + 1 + m + 1)
                high("L", m, kn[:, m, :], gain("qa", m) if m < 3 else gain("kva", m - 3))
                answer(nc.scalar.activation(sq[:, :], kn[:, m, :], ACT.Square))
                if m == 2:
                    root(QL)
            for l in range(NSTR["qb"]):
                ahead("qb", l)
            root(KL)
            for l in range(NSTR["kvb"]):
                ahead("kvb", l)
                if l >= 2:
                    for m in range(4 * (l - 2), 4 * (l - 1)):
                        value(10 + m, v3, m)

            def exp3(un):
                n, q0 = (un % NB + 1) * P, 8 * (un % SLOTS)
                asked()
                answer(nc.scalar.activation(sm3[:, un % SLOTS, 0:n], sm3[:, un % SLOTS, 0:n], ACT.Exp, bias=cols[:, q0 + 1:q0 + 2],
                                            scale=MSCALE, accum_out=cols[:, q0 + 2:q0 + 3]))

            def gates(m):
                act.wait_ge(evac, OUT0["mgate"] + m + 1)
                nc.scalar.activation(sg3[:, m, :], sg3[:, m, :], ACT.Silu).then_inc(silu_done, 1)

            exp3(0)
            exp3(1)
            for un in range(U3):
                n = (un % NB + 1) * P
                if un + 2 < U3:
                    exp3(un + 2)
                if un % NB == 1:
                    ahead("mgate", un // NB)
                act.wait_ge(pt_ps, U1 + un + 1)
                nc.scalar.copy(ev[:, un % 2, 0:n], ps[:, 2 + un % 2, 0:n]).then_inc(pt_ready, 1)
                if un % NB == 0 and un:
                    gates(un // NB - 1)
                if un % NB == 1 and un > NB:
                    act.wait_ge(o_out, un // NB)
                    high("C", un // NB - 1, sg[:, :])
            gates(MH - 1)
            act.wait_ge(o_out, MH)
            high("C", MH - 1, sg[:, :])
            post("oout")
            assert xs[0] == XT["oo"] + 8

        @block.tensor
        def _(pe):
            nrm = [0]
            pe.wait_ge(in_d, 48)
            pe.wait_ge(in_cst, 32)
            pe.wait_ge(ss_x, 1)
            nc.tensor.matmul(ps[:, NRM, 0:NC], blk[:, :], ssum[:, 0, :], start=True, stop=True).then_inc(ss_ps, 1)

            def second_turn(sl):
                pe.wait_ge(z_ready, sl + 1)
                if sl:
                    pe.wait_ge(s_ready, sl)
                nc.tensor.matmul(ps[:, SZ, :], C("permz"), z2[:, :], start=True, stop=True).then_inc(zp, 1)

            for sl in range(NSL):
                pe.wait_ge(e_ready, sl + 1)
                pe.wait_ge(c_ready, 1)
                for g in range(SG):
                    gg = sl * SG + g
                    nc.tensor.matmul(ps[:, gg // 32, gg % 32 * GH:(gg % 32 + 1) * GH], E[:, sl % 2, g, :], bC[:, 0, gg * GH:(gg + 1) * GH],
                                     start=True, stop=True)
                for half in range(2):
                    if sl:
                        pe.wait_ge(et_sb, 2 * sl - 1 + half)
                    for g in range(4):
                        last = nc.tensor.transpose(ps[:, 2 + half, g * P:(g + 1) * P], E[:, sl % 2, 4 * half + g, :], C("ident"))
                    last.then_inc(et_ps, 1)
                if sl:
                    second_turn(sl - 1)
                pe.wait_ge(et_sb, 2 * sl + 2)
                pe.wait_ge(u_ready, 1)
                if sl:
                    pe.wait_ge(v_sb, sl)
                for g in range(SG):
                    last = nc.tensor.matmul(ps[:, SX, g * NC:(g + 1) * NC], ET[:, g, :], u[:, sl * SG + g, :], start=True, stop=True)
                last.then_inc(v_ps, 1)
                pe.wait_ge(v_sb, sl + 1)
                nc.tensor.matmul(ps[:, SY, :], C("permz"), vsb[:, :], start=True, stop=True).then_inc(vp, 1)
            second_turn(NSL - 1)
            pe.wait_ge(toep, 16 * ST)
            for sl in range(NSL):
                pe.wait_ge(g_ready, sl + 1)
                pe.wait_ge(s_ready, sl + 1)
                if sl >= 2:
                    pe.wait_ge(yg_ready, sl - 1)
                for g in range(SG):
                    gg = sl * SG + g
                    nc.tensor.matmul(ps[:, 2 + sl % 2, g * NC:(g + 1) * NC], T[:, :, gg], u[:, gg, :],
                                     start=True, stop=False)
                    last = nc.tensor.matmul(ps[:, 2 + sl % 2, g * NC:(g + 1) * NC], G[:, sl % 2, g * P:(g + 1) * P], S[:, gg, :],
                                            start=False, stop=True)
                last.then_inc(y_ps, 1)

            def product(slot, k, bank, xh, xl, first, last):
                w = slice(k * P, (k + 1) * P)
                out = ps[:, bank, :]
                nc.tensor.matmul(out, whi[:, slot, w], xh, start=first, stop=False)
                nc.tensor.matmul(out, whi[:, slot, w], xl, start=False, stop=False)
                return nc.tensor.matmul(out, wlo[:, slot, w], xh, start=False, stop=last)

            def strip(name, l, j, x, xt, step=1, each=None):
                slot, bank = (S0[name] + j) % RING, (OUT0[name] + j) % RING
                pe.wait_ge(lo_ready, S0[name] + l + 1)
                pe.wait_ge(evac, OUT0[name] + l - RING + 1)
                for k in range(KT):
                    if j == 0:
                        pe.wait_ge(x_lo, xt + step * k + 1)
                    last = product(slot, k, bank, X[x][0][:, k, :], X[x][1][:, k, :], k == 0, k == KT - 1)
                    if each is not None:
                        each(k)
                last.then_inc(seg_done, 1)

            def strip_part(name, l, part, x):
                slot = (S0[name] + l) % RING
                if part == 0:
                    pe.wait_ge(lo_ready, S0[name] + l + 1)
                    pe.wait_ge(evac, OUT0[name] + l)
                for k in (2 * part, 2 * part + 1):
                    last = product(slot, k, NRM, X[x][0][:, k, :], X[x][1][:, k, :], k == 0, k == KT - 1)
                if part == 3:
                    last.then_inc(seg_done, 1)

            def add_squares(k):
                last = nc.tensor.matmul(ps[:, NRM, :], C("ones"), squares[k % 2][:, :], start=(k == 0), stop=(k == KT - 1))
                last.then_inc(sq_used if k < KT - 1 else nrm_ps, 1)

            def strips(name, x, xt, step=1, n=8, between=None):
                if between is None:
                    with pe.Fori(0, n // RING) as i:
                        for j in range(RING):
                            strip(name, RING * i + j, j, x, xt, step)
                else:
                    for l in range(n):
                        strip(name, l, l, x, xt, step)
                        if l == 1:
                            between()

            def short_strip(name, l, per, k_tiles, x, xt, x0=0):
                slot = (S0[name] + l) % RING
                pe.wait_ge(lo_ready, S0[name] + l + 1)
                for q in range(per):
                    o = OUT0[name] + per * l + q
                    if o >= RING:
                        pe.wait_ge(evac, o - RING + 1)
                    for k in range(k_tiles):
                        pe.wait_ge(x_lo, xt + x0 + k + 1)
                        last = product(slot, q * k_tiles + k, o % RING, X[x][0][:, x0 + k, :], X[x][1][:, x0 + k, :], k == 0, k == k_tiles - 1)
                    last.then_inc(seg_done, 1)

            def norm(src=None, bank=NRM):
                nrm[0] += 1
                pe.wait_ge(ssq_ready, nrm[0])
                nc.tensor.matmul(ps[:, bank, :], C("ones"), acc[:, :] if src is None else src, start=True, stop=True).then_inc(nrm_ps, 1)

            def mlp(layer):
                for kind, c in (("up", 0), ("up", 1), ("down", 0), ("up", 2), ("down", 1), ("up", 3), ("down", 2), ("down", 3)):
                    if kind == "up":
                        strips(f"up{layer}_{c}", "B", XT[f"mlp{layer}"], between=None if c else norm)
                    else:
                        strips(f"down{layer}_{c}", "AC"[c % 2], XT[f"hid{layer}_{c}"])
                strips(f"gate{layer}", "B", XT[f"gate{layer}"], between=norm)

            def partners(n, perm, src, bank):
                nc.tensor.matmul(ps[:, bank, :], C(perm), src, start=True, stop=True).then_inc(rope_ps, 1)

            def transposes(src, bank, n=NB):
                for k in range(n):
                    last = nc.tensor.transpose(ps[:, bank, k * P:(k + 1) * P], src[:, k * P:(k + 1) * P], C("ident"))
                return last

            for l in range(2):
                short_strip("proj0", l, 4, 2, "C", XT["p0"])
            strips("glu", "A", XT["y"], n=16)
            mlp(0)
            strips("kv", "A", XT["kvq"], 2, n=NSTR["kv"], between=norm)
            strip("q", 0, 0, "C", XT["kvq"] + 1, 2)
            pe.wait_ge(evac, OUT0["q"] + 1)
            partners(0, "perm1", kv1[:, 0, :], SX)
            partners(1, "perm1", kv1[:, 1, :], SY)
            for j in range(2):
                if j:
                    pe.wait_ge(vt_done, j)
                transposes(kv1[:, 2 + j, :], NRM).then_inc(vt_ps, 1)
            partners(2, "perm1", q1[:, 0, :], SZ)
            pe.wait_ge(vt_done, 2)
            for part in range(4):
                strip_part("q", 1, part, "C")

            def scores1(un):
                m, b, r = un // 4, un // 2 % 2, slice(64 * (un // 2 % 2), 64 * (un // 2 % 2) + 64)
                pe.wait_ge(rope_done, 3 + m)
                if un >= 2:
                    pe.wait_ge(sc_out, un - 1)
                for k in range(2):
                    n = un % 2 * 2 + k
                    last = nc.tensor.matmul(ps[:, un % 2, k * 256:(k + 1) * 256], q1[r, m, n * P:(n + 1) * P],
                                            k1[r, m // 4, n * P:(n + 2) * P], start=True, stop=True)
                last.then_inc(sc_ps, 1)

            def values1(un):
                m, b = un // 4, un // 2 % 2
                r = slice(64 * b, 64 * b + 64)
                pe.wait_ge(pt_ready, un + 1)
                if un == 0:
                    pe.wait_ge(vt_done, 2)
                if un % 4 == 0 and m >= 2:
                    pe.wait_ge(x_lo, XT["o"] + m - 1)
                for k in range(2):
                    n = un % 2 * 2 + k
                    for kb in range(2):
                        if n + kb == 0:
                            continue
                        v = v1[:, n + kb - 1, m // 4 * P + 64 * b:m // 4 * P + 64 * b + 64]
                        last = nc.tensor.matmul(ps[r, SX + m % 2, n * P:(n + 1) * P], v, pt1[:, un % 2, (2 * k + kb) * P:(2 * k + kb + 1) * P],
                                                start=(kb == 0 or n == 0), stop=(kb == 1))
                if un % 4 == 3:
                    last.then_inc(o_ps, 1)

            for un in range(3):
                scores1(un)
            for un in range(U1):
                m = un // 4
                if m + 2 < KT:
                    strip_part("q", m + 2, un % 4, "C")
                if un % 4 == 0 and m + 1 < KT:
                    pe.wait_ge(rope_done, 3 + m)
                    pe.wait_ge(evac, OUT0["q"] + m + 2)
                    partners(3 + m, "perm1", q1[:, m + 1, :], SZ)
                if un + 3 < U1:
                    scores1(un + 3)
                pe.wait_ge(p_ready, un + 1)
                if un >= 2:
                    pe.wait_ge(pt_ready, un - 1)
                for k in range(4):
                    last = nc.tensor.transpose(ps[:, 2 + un % 2, k * P:(k + 1) * P], sm1[:, un % SLOTS, k // 2, k % 2 * P:(k % 2 + 1) * P], C("ident"))
                last.then_inc(pt_ps, 1)
                if un:
                    values1(un - 1)
            values1(U1 - 1)
            strips("wo", "A", XT["o"])
            for l in range(2):
                short_strip("proj1", l, 4, 2, "C", XT["p1"])
            mlp(1)
            def even(l):
                strip("even", l, l, "C", XT["even"])

            for l in range(8):
                even(l)
                if l == 1:
                    norm()
                    norm(acc2, SX)
            for m in range(8):
                even(8 + m)
                if m >= 2:
                    pe.wait_ge(rope_done, 10 + m - 1)
                partners(10 + m, "perm2", (q2 if m < 4 else k2)[:, m % 4, :], SX + m % 2)
                if m:
                    pe.wait_ge(evac, OUT0["even"] + 8 + m)
                    if m > 1:
                        pe.wait_ge(vt_done, 2 + m - 1)
                    transposes(ev[:, (m - 1) % 2, :], SZ).then_inc(vt_ps, 1)
            pe.wait_ge(evac, OUT0["even"] + 16)
            pe.wait_ge(vt_done, 2 + 7)
            transposes(ev[:, 1, :], SZ).then_inc(vt_ps, 1)
            with pe.Fori(0, 8 // RING) as i:
                for j in range(RING):
                    strip("even", 16 + RING * i + j, 16 + j, "C", XT["even"])
            pe.wait_ge(rope_done, 18)
            pe.wait_ge(vt_done, 10)

            def ret_scores(jp):
                if jp:
                    pe.wait_ge(rpv, jp)
                    pe.wait_ge(r_out, 2 * jp)
                transposes(k2[:, jp, :], SX).then_inc(rk_ps, 1)
                for b in range(2):
                    r = slice(64 * b, 64 * b + 64)
                    for n in range(NB):
                        cc = slice(n * P, (n + 1) * P)
                        last = nc.tensor.matmul(ps[:, (SZ, SY)[b], cc], k2[r, jp, cc], q2[r, jp, cc], start=True, stop=True)
                    last.then_inc(rs_ps, 1)

            def ret_keys_values(jp):
                pe.wait_ge(rk_sb, jp + 1)
                for n in range(NB - 1):
                    for b in range(2):
                        hh = 2 * jp + b
                        last = nc.tensor.matmul(ps[64 * b:64 * b + 64, SX, n * P:(n + 1) * P], k2[:, jp, n * P + 64 * b:n * P + 64 * b + 64],
                                                v2[:, n, hh * P:(hh + 1) * P], start=True, stop=True)
                last.then_inc(rkv_ps, 1)

            def ret_out(jp, b):
                hh, r = 2 * jp + b, slice(64 * b, 64 * b + 64)
                pe.wait_ge(rs_sb, hh + 1)
                pe.wait_ge(rpv, jp + 1)
                for n in range(NB):
                    cc = slice(n * P, (n + 1) * P)
                    last = nc.tensor.matmul(ps[:, (SZ, SY)[b], cc], v2[:, n, hh * P:(hh + 1) * P], ev[:, 1, cc], start=True, stop=(n == 0))
                    if n:
                        last = nc.tensor.matmul(ps[:, (SZ, SY)[b], cc], acc[r, cc], q2[r, jp, cc], start=False, stop=True)
                last.then_inc(r_ps, 1)

            for l in range(32):
                even(24 + l)
                jp = l // 8
                if l % 8 == 0:
                    ret_scores(jp)
                elif l % 8 == 2:
                    ret_keys_values(jp)
                elif l % 8 == 3:
                    ret_out(jp, 0)
                elif l % 8 == 4:
                    norm(sq[:, :])
                    ret_out(jp, 1)
                elif l % 8 == 5:
                    norm(sq[:, :])
            with pe.Fori(0, 2) as i:
                for j in range(8):
                    slot, bank = (S0["eout"] + j) % RING, (OUT0["eout"] + j // 2) % RING
                    pe.wait_ge(lo_ready, S0["eout"] + j + 1 + 8 * i)
                    if j % 2 == 0:
                        pe.wait_ge(evac, OUT0["eout"] + j // 2 - RING + 1 + 4 * i)
                    x, xt = ("A", XT["conv"]) if j % 2 == 0 else ("C", XT["ret"])
                    for k in range(KT):
                        if j < 2:
                            pe.wait_ge(x_lo, xt + k + 1)
                        last = product(slot, k, bank, X[x][0][:, k, :], X[x][1][:, k, :], j % 2 == 0 and k == 0, j % 2 == 1 and k == KT - 1)
                    last.then_inc(seg_done, 1)
            norm()
            for l in range(NSTR["odd"]):
                strip("odd", l, l, "A", XT["odd"], each=None if l else add_squares)
                if l == 1:
                    pe.wait_ge(evac, OUT0["odd"] + 1)
                    partners(18, "perm2", kr[:, :], SX)
                if l == 4:
                    norm()
            for l in range(NSTR["qb"]):
                short_strip("qb", l, 2, 3, "L", XT["lat"])
            norm()
            for l in range(NSTR["kvb"]):
                short_strip("kvb", l, 4, 2, "L", XT["lat"], 3)
                if l >= 2:
                    for m in range(4 * (l - 2), 4 * (l - 1)):
                        pe.wait_ge(evac, OUT0["kvb"] + 8 + m + 1)
                        pe.wait_ge(vt_done, 10 + m)
                        transposes(ev[:, m % 2, :], SZ).then_inc(vt_ps, 1)
            for m in range(4):
                if m >= 1:
                    pe.wait_ge(rope_done, 18 + m)
                partners(19 + m, "perm2", qr[:, m, :], SX + m % 2)
            pe.wait_ge(evac, OUT0["mgate"])

            def scores3(un):
                hh, n = un // NB, un % NB
                r = slice(64 * (hh % 2), 64 * (hh % 2) + 64)
                pe.wait_ge(rope_done, 19 + hh // 2 + 1)
                if un >= 2:
                    pe.wait_ge(sc_out, U1 + un - 1)
                keys, qs = (n + 1) * P, slice(n * P, (n + 1) * P)
                nc.tensor.matmul(ps[:, un % 2, 0:keys], qn[:, hh, qs], kn[:, hh, 0:keys], start=True, stop=False)
                nc.tensor.matmul(ps[:, un % 2, 0:keys], qr[r, hh // 2, qs], kr[r, 0:keys], start=False, stop=True).then_inc(sc_ps, 1)

            def values3(un):
                hh, n = un // NB, un % NB
                pe.wait_ge(pt_ready, U1 + un + 1)
                if un == 0:
                    pe.wait_ge(vt_done, 18)
                if n == 0 and hh >= 2:
                    pe.wait_ge(o_out, hh - 1)
                for kb in range(n + 1):
                    last = nc.tensor.matmul(ps[:, SX + hh % 2, n * P:(n + 1) * P], v3[:, kb, hh * P:(hh + 1) * P], ev[:, un % 2, kb * P:(kb + 1) * P],
                                            start=(kb == 0), stop=(kb == n))
                if n == NB - 1:
                    last.then_inc(o_ps, 1)

            for un in range(3):
                scores3(un)
            for un in range(U3):
                strip_part("mgate", un // 4, un % 4, "A")
                if un + 3 < U3:
                    scores3(un + 3)
                pe.wait_ge(p_ready, U1 + un + 1)
                if un >= 2:
                    pe.wait_ge(pt_ready, U1 + un - 1)
                transposes(sm3[:, un % SLOTS, :], 2 + un % 2, un % NB + 1).then_inc(pt_ps, 1)
                if un:
                    values3(un - 1)
            values3(U3 - 1)
            strips("oout", "C", XT["oo"])
            norm()

        @block.vector
        def _(dve):
            ch = Chain(dve, dve_ch)
            V = nc.vector
            asks, given, nrm, xs = [0], [0], [0], [0]

            def t(k):
                return tab[:, k, :]

            def over(x, axis, n):
                x = x.unsqueeze(axis)
                shape = list(x.shape)
                shape[axis] = n
                return x.to_broadcast(shape)

            dt, lr, th, y, r, mag, sn, cs, ar, ai, den, inv, nr, cr, ci, sci, nsci, t1, t2, m8, w_r, w_i = (
                t(k) for k in (0, 1, 2, 3, 4, 5, 6, 8, 9, 10, 11, 12, 13, 14, 15, 16, 17, 18, 19, 20, 21, 22))
            lre, lim = lam[:, 0, :], lam[:, 1, :]
            dve.wait_ge(in_lam, 16)
            dve.wait_ge(tabs, 1)
            V.tensor_tensor(lr, lre, dt, ALU.mult)
            ch.link(V.tensor_tensor(th, lim, dt, ALU.mult))

            def reduce_angle(x, k):
                ch.link(V.tensor_scalar(k, x, 1.0 / TWO_PI, ROUND, ALU.mult, ALU.add))
                ch.link(V.tensor_scalar(k, k, ROUND, None, ALU.subtract))
                for part in (PI_A, PI_B, PI_C):
                    ch.link(V.scalar_tensor_tensor(x, k, -part, x, ALU.mult, ALU.add))

            reduce_angle(th, y)
            V.tensor_scalar(r, th, -PI_IN, PI_IN, ALU.max, ALU.min).then_inc(ang, 1)
            dve.wait_ge(tabs, 2)
            dve.wait_ge(in_cst, 32)
            V.tensor_tensor(ar, mag, cs, ALU.mult)
            V.tensor_tensor(ai, mag, sn, ALU.mult)
            V.tensor_tensor(t1, lre, lre, ALU.mult)
            ch.link(V.tensor_tensor(t2, lim, lim, ALU.mult))
            V.tensor_tensor(den, t1, t2, ALU.add)
            ch.link(V.tensor_scalar(nr, ar, 1.0, None, ALU.subtract))
            V.reciprocal(inv, den)
            V.tensor_tensor(t1, nr, lre, ALU.mult)
            ch.link(V.tensor_tensor(t2, ai, lim, ALU.mult))
            ch.link(V.tensor_tensor(cr, t1, t2, ALU.add))
            V.tensor_tensor(cr, cr, inv, ALU.mult)
            V.tensor_tensor(t1, ai, lre, ALU.mult)
            ch.link(V.tensor_tensor(t2, nr, lim, ALU.mult))
            ch.link(V.tensor_tensor(ci, t1, t2, ALU.subtract))
            ch.link(V.tensor_tensor(ci, ci, inv, ALU.mult))
            V.tensor_scalar(sci, ci, C("nsgn"), None, ALU.mult)
            V.tensor_scalar(nsci, ci, C("sgn"), None, ALU.mult)

            def cmul(o_r, o_i, a_r, a_i, b_r, b_i, s1, s2):
                V.tensor_tensor(s1, a_r, b_r, ALU.mult)
                ch.link(V.tensor_tensor(s2, a_i, b_i, ALU.mult))
                ch.link(V.tensor_tensor(o_r, s1, s2, ALU.subtract))
                V.tensor_tensor(s1, a_r, b_i, ALU.mult)
                ch.link(V.tensor_tensor(s2, a_i, b_r, ALU.mult))
                ch.link(V.tensor_tensor(o_i, s1, s2, ALU.add))

            V.memset(pwr[:, 0, :], 1.0)
            V.memset(pwi[:, 0, :], 0.0)
            V.tensor_copy(pwr[:, 1, :], ar)
            ch.link(V.tensor_copy(pwi[:, 1, :], ai))
            m = 1
            while m < ST:
                ab_r, ab_i = (over(pw[:, m, :], 1, m) for pw in (pwr, pwi))
                s1, s2 = (bt[:, k * 256:k * 256 + GR * m].rearrange("p (r g) -> p r g", r=m) for k in range(2))
                cmul(pwr[:, m + 1:2 * m + 1, :], pwi[:, m + 1:2 * m + 1, :], pwr[:, 1:m + 1, :], pwi[:, 1:m + 1, :], ab_r, ab_i, s1, s2)
                m *= 2
            ch.link(V.tensor_scalar(spi[:, :, :], pwi[:, :, :], C("nsgn"), None, ALU.mult))
            ch.link(V.tensor_tensor(m8, mag, mag, ALU.mult))
            ch.link(V.tensor_tensor(m8, m8, m8, ALU.mult))
            ch.link(V.tensor_tensor(m8, m8, m8, ALU.mult))
            V.tensor_copy(w_r, cs)
            ch.link(V.tensor_copy(w_i, sn))

            def square_turn(o_r, o_i, w_r, w_i):
                ch.link(V.tensor_tensor(dt, w_r, w_i, ALU.mult))
                V.tensor_tensor(t1, w_r, w_r, ALU.mult)
                ch.link(V.tensor_tensor(t2, w_i, w_i, ALU.mult))
                V.tensor_tensor(o_r, t1, t2, ALU.subtract)
                return V.tensor_scalar(o_i, dt, 2.0, None, ALU.mult)

            def turn_by(k):
                return wt[:, k, 0, :], wt[:, k, 1, :]

            ch.link(square_turn(w_r, w_i, w_r, w_i))
            ch.link(square_turn(w_r, w_i, w_r, w_i))
            ch.link(square_turn(*turn_by(0), w_r, w_i))
            for k in range(1, LEVELS):
                last = square_turn(*turn_by(k), *turn_by(k - 1))
                if k < LEVELS - 1:
                    ch.link(last)
            last.then_inc(turns, 1)
            dve.wait_ge(in_bc, 32)

            def per_group(x):
                return over(x, 2, GH)

            def by_group(x):
                return x.rearrange("p (g h) -> p g h", h=GH)

            b1, b2 = by_group(bB[:, 0, :]), by_group(bB[:, 1, :])
            bb1, bb2, btg = by_group(bb[:, 0, :]), by_group(bb[:, 1, :]), by_group(bt[:, :])
            for o, x, z, s in ((bb1, b1, b2, sci), (bb2, b2, b1, nsci)):
                V.tensor_tensor(o, x, per_group(cr), ALU.mult)
                ch.link(V.tensor_tensor(btg, z, per_group(s), ALU.mult))
                ch.link(V.tensor_tensor(o, o, btg, ALU.add))
            V.tensor_scalar(bC[:, 0, :], bC[:, 0, :], C("sgn"), None, ALU.mult).then_inc(c_ready, 1)
            V.memset(dec[:, :, 0:1], 0.0)

            def matrices(out, tr, pw, pi, first, x, z, gs, op):
                def pws(p):
                    return over(p[:, first:first + ST, gs].rearrange("p r g -> p g r"), 3, GH)

                def mat(x):
                    return over(x[:, gs, :], 2, ST)

                def cols4(x):
                    return x.rearrange("p (g r h) -> p g r h", r=ST, h=GH)

                V.tensor_tensor(cols4(out), pws(pw), mat(x), ALU.mult)
                ch.link(V.tensor_tensor(cols4(tr), pws(pi), mat(z), ALU.mult))
                return V.tensor_tensor(out, out, tr, op)

            def gc(x):
                return x.rearrange("p (g c) -> p g c", g=SG)

            def scan(sl):
                gs = slice(sl * SG, (sl + 1) * SG)
                dve.wait_ge(v_sb, sl + 1)
                dve.wait_ge(w_ready, 2 * sl // NSL + 1)
                V.tensor_tensor(gc(z1[:, :]), Wc[:, gs, :], gc(vsb[:, :]), ALU.mult)
                V.tensor_copy(dec[:, :, 1:NC], over(m8[:, gs], 2, NC - 1))
                dve.wait_ge(vp, sl + 1)
                ch.link(V.tensor_tensor(gc(z2[:, :]), Wsn[:, gs, :], gc(ps[:, SY, :]), ALU.mult))
                ch.link(V.tensor_tensor(z1[:, :], z1[:, :], z2[:, :], ALU.add))
                V.tensor_tensor_scan(z2[:, :], dec[:, :, :].rearrange("p g c -> p (g c)"), z1[:, :], 0.0, ALU.mult, ALU.add).then_inc(z_ready, 1)

            def turn_back(sl):
                gs = slice(sl * SG, (sl + 1) * SG)
                dve.wait_ge(z_ready, sl + 1)
                V.tensor_tensor(gc(z1[:, :]), Wc[:, gs, :], gc(z2[:, :]), ALU.mult)
                dve.wait_ge(zp, sl + 1)
                ch.link(V.tensor_tensor(gc(z3[:, :]), Wsn[:, gs, :], gc(ps[:, SZ, :]), ALU.mult))
                V.tensor_tensor(S[:, gs, 1:NC], gc(z1[:, :])[:, :, 0:NC - 1], gc(z3[:, :])[:, :, 0:NC - 1], ALU.subtract).then_inc(s_ready, 1)
                dve.wait_ge(s_ready, sl + 1)

            def inputs(sl):
                gs = slice(sl * SG, (sl + 1) * SG)
                if sl:
                    dve.wait_ge(e_ready, sl)
                if sl >= 2:
                    dve.wait_ge(et_ps, 2 * sl - 2)
                matrices(E[:, sl % 2, :, :].rearrange("p g n -> p (g n)"), bt[:, :], pwr, spi, 0, bb1, bb2, gs, ALU.add).then_inc(e_ready, 1)

            def outputs(sl):
                gs = slice(sl * SG, (sl + 1) * SG)
                if sl:
                    dve.wait_ge(g_ready, sl)
                if sl >= 2:
                    dve.wait_ge(y_ps, sl - 1)
                matrices(G[:, sl % 2, :], bt[:, :], pwr, pwi, 1, by_group(bC[:, 0, :]), by_group(bC[:, 1, :]), gs, ALU.subtract).then_inc(g_ready, 1)

            inputs(0)
            dve.wait_ge(sq_x, 1)
            V.tensor_reduce(ssum[:, 0, :], S[:, :, :].rearrange("p g c -> p c g"), AX_X, ALU.add).then_inc(ss_x, 1)
            inputs(1)
            dve.wait_ge(ss_x, 1)
            V.memset(S[:, :, 0:1], 0.0)
            dve.wait_ge(std_x, 1)
            ch.link(V.reciprocal(ssum[:, 2, :], ssum[:, 1, :]))
            dve.wait_ge(u_gain, 1)
            V.tensor_tensor(u[:, :, :], u[:, :, :], over(ssum[:, 2, :], 1, GR), ALU.mult).then_inc(u_ready, 1)
            for sl in range(NSL):
                if sl == NSL - 1:
                    dve.wait_ge(et_ps, 2 * NSL)
                    dve.wait_ge(g_ready, 1)
                    ch.link(V.tensor_tensor(bt[0:GH, :], d16[:, 0, :], d16[:, 1, :], ALU.mult))
                    for b in range(2):
                        copied = V.tensor_copy(kst[:, :, 32 * b:32 * b + 32].rearrange("p h g -> p g h"), by_group(ps[:, b, :]))
                    ch.link(copied)
                    V.tensor_tensor(kst[0:GH, :, :], kst[0:GH, :, :], bt[0:GH, :].rearrange("p (h g) -> p h g", g=GR), ALU.add).then_inc(kst_ready, 1)
                    dve.wait_ge(kst_ready, 1)
                scan(sl)
                if sl + 2 < NSL:
                    inputs(sl + 2)
                else:
                    if sl + 2 == NSL:
                        dve.wait_ge(e_ready, NSL)
                    outputs(sl + 2 - NSL)
                turn_back(sl)
            for sl in range(2, NSL):
                outputs(sl)
            dve.wait_ge(g_ready, NSL)

            def ask(ins):
                ins.then_inc(to_act, 1)
                asks[0] += 1

            def answered():
                given[0] += 1
                dve.wait_ge(to_dve, given[0])

            def out_ready(name, o, ends=1):
                dve.wait_ge(seg_done, SEG0[name] + ends * (o + 1))

            def bank(name, o):
                return ps[:, (OUT0[name] + o) % RING, :]

            def low(dst, m, src, g=None):
                xs[0] += 1
                dve.wait_ge(x_hi, xs[0])
                hi, lo = X[dst][0][:, m, :].bitcast(F32), X[dst][1][:, m, :]
                if g is None:
                    V.tensor_tensor(lo, src, hi, ALU.subtract).then_inc(x_lo, 1)
                else:
                    V.scalar_tensor_tensor(lo, src, g, hi, ALU.mult, ALU.subtract).then_inc(x_lo, 1)

            adds = [0]

            def start_sum():
                V.memset(acc[:, :], 0.0).then_inc(acc_add, 1)
                adds[0] += 1

            def add_square(last):
                dve.wait_ge(acc_add, adds[0])
                V.tensor_tensor(acc[:, :], acc[:, :], sq[:, :], ALU.add).then_inc(ssq_ready if last else acc_add, 1)
                adds[0] += not last

            def root(dst=rstd):
                nrm[0] += 1
                dve.wait_ge(nrm_std, nrm[0])
                ch.link(V.reciprocal(dst[:, :], std[:, :]))

            def scaled(name, o, dst, ends=1, at=None, by=None):
                out_ready(name, o, ends)
                V.tensor_tensor(dst, bank(name, o) if at is None else ps[:, at, :], (rstd if by is None else by)[:, :], ALU.mult).then_inc(evac, 1)

            def rotate(n, src, dst, part_bank, cos, sin, s1, s2):
                V.tensor_tensor(s1, src, cos, ALU.mult)
                dve.wait_ge(rope_ps, n + 1)
                ch.link(V.tensor_tensor(s2, part_bank, sin, ALU.mult))
                V.tensor_tensor(dst, s1, s2, ALU.add).then_inc(rope_done, 1)

            dve.wait_ge(in_p, 16)
            for k in range(2):
                low("C", k, ev[:, k, :])
            for m in range(KT):
                out_ready("proj0", m)
                V.tensor_copy(ple[:, m, :], bank("proj0", m)).then_inc(evac, 1)
                xs[0] += 1
                dve.wait_ge(x_hi, xs[0])
                V.tensor_tensor(X["A"][1][:, m, :].rearrange("p (c t) -> p c t", t=ST), yfm[:, m, :, :].rearrange("p t c -> p c t"),
                                X["A"][0][:, m, :].bitcast(F32).rearrange("p (c t) -> p c t", t=ST), ALU.subtract).then_inc(x_lo, 1)
            dve.wait_ge(in_pos, 16)
            ch.link(V.tensor_copy(rsin[:, :], rcos[:, :].bitcast(I32)))
            ch.link(V.tensor_scalar(rsin[:, :], rsin[:, :], C("inv"), None, ALU.mult))
            reduce_angle(rsin[:, :], rcos[:, :])
            ask(V.tensor_scalar(rsin[:, :], rsin[:, :], -PI_IN, PI_IN, ALU.max, ALU.min))
            answered()
            start_sum()
            dve.wait_ge(in_h, 16)
            for m in range(KT + 1):
                if m < KT:
                    answered()
                    out_ready("glu", 2 * m + 1)
                    V.tensor_tensor(ev[:, 0, :], bank("glu", 2 * m + 1), sg[:, :], ALU.mult).then_inc(evac, 2)
                if m:
                    low("B", m - 1, h[:, m - 1, :], gain("mlp0", m - 1))
                    add_square(m == KT)
                if m < KT:
                    dve.wait_ge(evac, OUT0["glu"] + 2 * m + 2)
                    ask(V.tensor_tensor(h[:, m, :], h[:, m, :], ev[:, 0, :], ALU.add))
                    dve.wait_ge(to_act, asks[0])

            def mlp(layer):
                root()
                for kind, c in (("up", 0), ("up", 1), ("down", 0), ("up", 2), ("down", 1), ("up", 3), ("down", 2), ("down", 3)):
                    name = f"{kind}{layer}_{c}"
                    if kind == "up":
                        x = X["AC"[c % 2]]
                        with dve.Fori(0, 8 // RING) as i:
                            for j in range(RING):
                                o = RING * i + j
                                dve.wait_ge(seg_done, SEG0[name] + o + 1)
                                V.scalar_tensor_tensor(ev[:, 0, :], bank(name, j), 0.0, rstd[:, :], ALU.max, ALU.mult).then_inc(evac, 1)
                                dve.wait_ge(x_hi, xs[0] + o + 1)
                                V.tensor_tensor(x[1][:, o, :], sg[:, :], x[0][:, o, :].bitcast(F32), ALU.subtract).then_inc(x_lo, 1)
                        xs[0] += 8
                    elif c < CHUNKS - 1:
                        with dve.Fori(0, 8 // RING) as i:
                            for j in range(RING):
                                o = RING * i + j
                                dve.wait_ge(seg_done, SEG0[name] + o + 1)
                                V.tensor_tensor(h[:, o, :], bank(name, j), h[:, o, :], ALU.add).then_inc(evac, 1)
                    else:
                        dve.wait_ge(evac, OUT0[name])
                        start_sum()
                        for m in range(KT):
                            out_ready(name, m)
                            V.tensor_tensor(h[:, m, :], bank(name, m), h[:, m, :], ALU.add).then_inc(evac, 1)
                            dve.wait_ge(evac, OUT0[name] + m + 1)
                            low("B", m, h[:, m, :], gain(f"ple{layer}", m))
                            add_square(m == KT - 1)

            def gate(layer):
                name = f"gate{layer}"
                if layer == 1:
                    ch.link(V.tensor_tensor(finpre, gp[:, GC["fin"]], gp[:, GC["pre0"]], ALU.mult))
                root()
                start_sum()
                if layer == 1:
                    ch.link(V.memset(acc2, 0.0))

                def finish(m):
                    if layer == 0:
                        low("A", m, h[:, m, :], gain("kvn", m))
                        low("C", m, h[:, m, :], gain("mix1", m))
                        add_square(m == KT - 1)
                    else:
                        low("C", m, h[:, m, :], finpre[:, m:m + 1])
                        add_square(m == KT - 1)
                        last = V.tensor_tensor(acc2, acc2, cy[:, :], ALU.add)
                        if m < KT - 1:
                            ch.link(last)
                        else:
                            last.then_inc(ssq_ready, 1)

                for m in range(KT + 1):
                    if m < KT:
                        scaled(name, m, ev[:, 0, :])
                    if m:
                        finish(m - 1)
                    if m < KT:
                        answered()
                        ch.link(V.tensor_tensor(ev[:, 1, :], sg[:, :], ple[:, m, :], ALU.mult))
                        ask(V.tensor_tensor(h[:, m, :], h[:, m, :], ev[:, 1, :], ALU.add))
                        dve.wait_ge(to_act, asks[0])

            mlp(0)
            gate(0)
            root()
            dve.wait_ge(seg_done, SEG0["kv"])
            V.memset(k1[:, :, 0:P], 0.0)
            for o in range(4):
                scaled("kv", o, kv1[:, o, :])
            scaled("q", 0, q1[:, 0, :])
            dve.wait_ge(evac, OUT0["q"] + 1)
            dve.wait_ge(in_a1, 32)
            rc, rs = rope1[:, 0, :], rope1[:, 1, :]
            for j in range(2):
                rotate(j, kv1[:, j, :], k1[:, j, P:], ps[:, SX + j, :], rc, rs, ev[:, 0, :], ev[:, 1, :])
                dve.wait_ge(rope_done, j + 1)

            def rotate_q(m):
                rotate(2 + m, q1[:, m, :], q1[:, m, :], ps[:, SZ, :], rc, rs, ev[:, 0, :], ev[:, 1, :])

            def masked_max(un):
                q0 = 16 * (un % SLOTS)
                mx, mm, ng = cols[:, q0:q0 + 2], cols[:, q0 + 2:q0 + 4], cols[:, q0 + 4:q0 + 6]
                msk = msk1[:, 0:2, :] if un % 2 == 0 else msk1[:, 1:3, :]
                dve.wait_ge(sc_ps, un + 1)
                V.tensor_tensor(sm1[:, un % SLOTS, :, :], ps[:, un % 2, :].rearrange("p (n k) -> p n k", n=2), msk, ALU.add).then_inc(sc_out, 1)
                dve.wait_ge(sc_out, un + 1)
                ch.link(V.tensor_reduce(mx, sm1[:, un % SLOTS, :, :], AX_X, ALU.max))
                ch.link(V.tensor_scalar(mm, mx, float(HD) ** -0.5, gain("sink", un // 4 * 2 + un // 2 % 2), ALU.mult, ALU.max))
                ask(V.tensor_scalar(ng, mm, -1.0, None, ALU.mult))

            def normed(un):
                q0 = 16 * (un % SLOTS)
                rsum, es, dn, rc_ = (cols[:, q0 + k:q0 + k + 2] for k in (6, 8, 10, 12))
                answered()
                ch.link(V.tensor_tensor(dn, rsum, es, ALU.add))
                ch.link(V.reciprocal(rc_, dn))
                V.tensor_scalar(sm1[:, un % SLOTS, 0, :], sm1[:, un % SLOTS, 0, :], rc_[:, 0:1], None, ALU.mult)
                V.tensor_scalar(sm1[:, un % SLOTS, 1, :], sm1[:, un % SLOTS, 1, :], rc_[:, 1:2], None, ALU.mult).then_inc(p_ready, 1)

            rotate_q(0)
            scaled("q", 1, q1[:, 1, :], at=NRM)
            masked_max(0)
            masked_max(1)
            for un in range(U1):
                if un % 4 == 1 and un // 4 + 1 < KT:
                    dve.wait_ge(rope_done, 3 + un // 4)
                    rotate_q(un // 4 + 1)
                if un + 2 < U1:
                    if un + 2 >= SLOTS:
                        dve.wait_ge(pt_ps, un + 3 - SLOTS)
                    masked_max(un + 2)
                normed(un)
                if un % 4 == 1 and un > 4:
                    low("A", un // 4 - 1, ps[:, SX + (un // 4 - 1) % 2, :])
                if un % 4 == 3 and un // 4 + 2 < KT:
                    scaled("q", un // 4 + 2, q1[:, un // 4 + 2, :], at=NRM)
            low("A", KT - 1, ps[:, SX + (KT - 1) % 2, :])
            dve.wait_ge(in_p, 48)
            for k in range(2):
                low("C", k, (sq, acc)[k][:, :])
            dve.wait_ge(x_lo, xs[0])
            start_sum()
            for m in range(KT):
                out_ready("wo", m)
                V.tensor_tensor(h[:, m, :], bank("wo", m), h[:, m, :], ALU.add).then_inc(evac, 1)
                dve.wait_ge(evac, OUT0["wo"] + m + 1)
                low("B", m, h[:, m, :], gain("mlp1", m))
                add_square(m == KT - 1)
            for o in range(8):
                out_ready("proj1", o)
                V.tensor_copy(ple[:, o, :], bank("proj1", o)).then_inc(evac, 1)
            mlp(1)
            gate(1)
            root()
            nrm[0] += 1
            dve.wait_ge(nrm_ps, nrm[0])
            ch.link(V.tensor_tensor(sq[:, :], ps[:, SX, :], rstd[:, :], ALU.mult))
            V.tensor_copy(sgr[:, KT - 1, :], rstd[:, :])
            ask(V.tensor_tensor(sq[:, :], sq[:, :], rstd[:, :], ALU.mult))
            dve.wait_ge(nrm_std, nrm[0])
            ch.link(V.reciprocal(sq[:, :], std[:, :]))
            ch.link(V.tensor_tensor(rstd[:, :], rstd[:, :], sq[:, :], ALU.mult))
            for o in range(8):
                scaled("even", o, (q2 if o < 4 else k2)[:, o % 4, :])
            for m in range(KT):
                last = V.scalar_tensor_tensor(h[:, m, :], h[:, m, :], gain("fin", m), sgr[:, KT - 1, :], ALU.mult, ALU.mult)
            ch.link(last)
            V.memset(cu[:, 0:2], 0.0)
            for m in range(8):
                if m >= 2:
                    dve.wait_ge(vt_ps, 2 + m - 1)
                scaled("even", 8 + m, ev[:, m % 2, :])
                qk = (q2 if m < 4 else k2)[:, m % 4, :]
                if m == 0:
                    dve.wait_ge(evac, OUT0["even"] + 8)
                rotate(10 + m, qk, qk, ps[:, SX + m % 2, :], rcos[:, :], rsin[:, :], acc[:, :], cy[:, :])
                dve.wait_ge(rope_done, 10 + m + 1)
            for m in range(8):
                if m < 2:
                    dve.wait_ge(vt_ps, 2 + 7 + m)
                else:
                    dve.wait_ge(silu_done, m - 1)
                scaled("even", 16 + m, ev[:, m % 2, :])
            dve.wait_ge(silu_done, 8)
            E0 = OUT0["even"]
            dve.wait_ge(in_rt, 32)

            def by_chunk(x):
                return x.rearrange("p (n k) -> p n k", n=NB)

            def masked_scores(jp, b):
                hh = 2 * jp + b
                if hh:
                    dve.wait_ge(r_ps, hh)
                V.tensor_tensor(by_chunk(ev[:, 1, :]), by_chunk(ps[:, (SZ, SY)[b], :]), over(rmask[:, hh, :], 1, NB), ALU.mult).then_inc(rs_sb, 1)

            def decayed(jp):
                dve.wait_ge(rk_ps, jp + 1)
                dve.wait_ge(rs_ps, 2 * jp + 2)
                for b in range(2):
                    cc = slice(64 * b, 64 * b + 64)
                    last = V.tensor_scalar(by_chunk(k2[:, jp, :])[:, :, cc], by_chunk(ps[:, SX, :])[:, :, cc],
                                           cst[:, CC["zeta"].start + 2 * jp + b:CC["zeta"].start + 2 * jp + b + 1], None, ALU.mult)
                last.then_inc(rk_sb, 1)
                V.tensor_tensor(by_chunk(q2[:, jp, :]), by_chunk(q2[:, jp, :]), over(xi[:, jp, :], 1, NB), ALU.mult)
                masked_scores(jp, 0)

            def states(jp):
                dve.wait_ge(rkv_ps, jp + 1)
                ch.link(V.tensor_copy(acc[:, P:2 * P], ps[:, SX, 0:P]))
                gam = cst[:, CC["gam"].start + jp:CC["gam"].start + jp + 1]
                for n in range(2, NB):
                    last = V.scalar_tensor_tensor(acc[:, n * P:(n + 1) * P], acc[:, (n - 1) * P:n * P], gam,
                                                  ps[:, SX, (n - 1) * P:n * P], ALU.mult, ALU.add)
                    if n < NB - 1:
                        ch.link(last)
                last.then_inc(rpv, 1)

            def head_out(jp, b):
                hh = 2 * jp + b
                nrm[0] += 1
                dve.wait_ge(nrm_std, nrm[0])
                ch.link(V.reciprocal(std[:, :], std[:, :]))
                ch.link(V.tensor_tensor(std[:, :], ps[:, (SZ, SY)[b], :], std[:, :], ALU.mult))
                V.scalar_tensor_tensor(sgr[:, hh, :], std[:, :], gain("gn", hh), sgr[:, hh, :], ALU.mult, ALU.mult).then_inc(r_out, 1)

            for k in range(8):
                o, jp = 24 + 4 * k, k // 2
                scaled("even", o, cu[:, 2:])
                scaled("even", o + 1, ev[:, 0, :])
                dve.wait_ge(evac, E0 + o + 2)
                ask(V.tensor_tensor(cu[:, 2:], cu[:, 2:], ev[:, 0, :], ALU.mult))
                if k % 2 == 0:
                    decayed(jp)
                else:
                    head_out(jp, 0)
                dve.wait_ge(to_act, asks[0])
                scaled("even", o + 2, ev[:, 0, :])
                answered()
                ch.link(V.scalar_tensor_tensor(cy[:, :], cu[:, 1:TOK + 1], gain("cw", 8 + k), cy[:, :], ALU.mult, ALU.add))
                ch.link(V.scalar_tensor_tensor(cy[:, :], cu[:, 2:TOK + 2], gain("cw", 16 + k), cy[:, :], ALU.mult, ALU.add))
                ch.link(V.tensor_tensor(cy[:, :], cy[:, :], ev[:, 0, :], ALU.mult))
                if k % 2 == 0:
                    states(jp)
                else:
                    head_out(jp, 1)
                scaled("even", o + 3, ev[:, 0, :])
                answered()
                ask(V.tensor_tensor(cy[:, :], cy[:, :], sg[:, :], ALU.mult))
                dve.wait_ge(to_act, asks[0])
                low("A", k, cy[:, :])
                if k % 2 == 0:
                    masked_scores(jp, 1)
            dve.wait_ge(r_out, RH)
            for hh in range(RH):
                low("C", hh, sgr[:, hh, :])

            def post(name, buf, g, ends):
                start_sum()
                for m in range(KT):
                    out_ready(name, m, ends)
                    V.tensor_copy(buf[:, m, :], bank(name, m)).then_inc(evac, 1)
                    answered()
                    add_square(m == KT - 1)
                root()
                for m in range(KT + 1):
                    if m < KT:
                        if m >= 2 and name == "eout":
                            dve.wait_ge(to_act, asks[0] - 1)
                        elif m >= 2:
                            dve.wait_ge(fin, m - 1)
                        ch.link(V.scalar_tensor_tensor(ev[:, m % 2, :], buf[:, m, :], gain(g, m), rstd[:, :], ALU.mult, ALU.mult))
                        last = V.tensor_tensor(h[:, m, :], h[:, m, :], ev[:, m % 2, :], ALU.add)
                        if name == "eout":
                            ask(last)
                        else:
                            last.then_inc(fin, 1)
                    if m and name == "eout":
                        dve.wait_ge(to_act, asks[0] - (m < KT))
                        low("A", m - 1, h[:, m - 1, :], gain("pre1", m - 1))

            post("eout", ybuf, "post0", 2)
            root()
            scaled("odd", 0, kr[:, :])
            start_sum()
            for m in range(5):
                scaled("odd", 1 + m, kn[:, m, :])
                answered()
                add_square(m in (2, 4))
                low("L", m, kn[:, m, :], gain("qa", m) if m < 3 else gain("kva", m - 3))
                if m == 1:
                    rotate(18, kr[:, :], kr[:, :], ps[:, SX, :], rcos[:, :], rsin[:, :], ev[:, 0, :], ev[:, 1, :])
                if m == 2:
                    dve.wait_ge(nrm_ps, nrm[0] + 1)
                    start_sum()
            dve.wait_ge(rope_done, 19)
            root(sg)
            for o in range(12):
                scaled("qb", o, qn[:, o, :] if o < 8 else qr[:, o - 8, :], by=sg)
            root(sq)
            dve.wait_ge(x_lo, xs[0])
            for o in range(8):
                scaled("kvb", o, kn[:, o, :], by=sq)
            for m in range(8):
                if m >= 2:
                    dve.wait_ge(vt_ps, 10 + m - 1)
                scaled("kvb", 8 + m, ev[:, m % 2, :], by=sq)
            dve.wait_ge(evac, OUT0["mgate"])
            for m in range(4):
                rotate(19 + m, qr[:, m, :], qr[:, m, :], ps[:, SX + m % 2, :], rcos[:, :], rsin[:, :], sq[:, :], sg[:, :])
                dve.wait_ge(rope_done, 20 + m)
            dve.wait_ge(in_cm, 16)

            def masked_max3(un):
                n, q0 = (un % NB + 1) * P, 8 * (un % SLOTS)
                dve.wait_ge(sc_ps, U1 + un + 1)
                V.tensor_tensor(sm3[:, un % SLOTS, 0:n], ps[:, un % 2, 0:n], cm[:, TOK - n:TOK], ALU.add).then_inc(sc_out, 1)
                dve.wait_ge(sc_out, U1 + un + 1)
                ch.link(V.tensor_reduce(cols[:, q0:q0 + 1], sm3[:, un % SLOTS, 0:n], AX_X, ALU.max))
                ask(V.tensor_scalar(cols[:, q0 + 1:q0 + 2], cols[:, q0:q0 + 1], -MSCALE, None, ALU.mult))

            def normed3(un):
                n, q0 = (un % NB + 1) * P, 8 * (un % SLOTS)
                answered()
                ch.link(V.reciprocal(cols[:, q0 + 3:q0 + 4], cols[:, q0 + 2:q0 + 3]))
                V.tensor_scalar(sm3[:, un % SLOTS, 0:n], sm3[:, un % SLOTS, 0:n], cols[:, q0 + 3:q0 + 4], None, ALU.mult).then_inc(p_ready, 1)

            def gated(hh):
                dve.wait_ge(o_ps, KT + hh + 1)
                dve.wait_ge(silu_done, 8 + hh + 1)
                V.tensor_tensor(sg[:, :], ps[:, SX + hh % 2, :], sg3[:, hh, :], ALU.mult).then_inc(o_out, 1)
                dve.wait_ge(o_out, hh + 1)
                low("C", hh, sg[:, :])

            masked_max3(0)
            masked_max3(1)
            for un in range(U3):
                if un + 2 < U3:
                    if un + 2 >= SLOTS:
                        dve.wait_ge(pt_ps, U1 + un + 3 - SLOTS)
                    masked_max3(un + 2)
                normed3(un)
                if un % NB == 1 and un > NB:
                    gated(un // NB - 1)
                if un % NB == NB - 1:
                    scaled("mgate", un // NB, sg3[:, un // NB, :], at=NRM)
            gated(MH - 1)
            post("oout", ybuf3, "post1", 1)
            assert xs[0] == XT["oo"] + 8
        return nc


def constants():
    f = np.float32
    cst = np.zeros((P, NCC), f)
    cst[:, CC["ident"]] = np.eye(P)
    cst[:, CC["ones"]] = 1.0
    m1, m2, mz = (np.zeros((P, P), f) for _ in range(3))
    for b in (0, 64):
        for d in range(8):
            m1[b + d + 8, b + d], m1[b + d, b + d + 8] = -1.0, 1.0
        for d in range(32):
            m2[b + d + 32, b + d], m2[b + d, b + d + 32] = -1.0, 1.0
    for d in range(64):
        mz[d + 64, d], mz[d, d + 64] = 1.0, -1.0
    cst[:, CC["perm1"]], cst[:, CC["perm2"]], cst[:, CC["permz"]] = m1, m2, mz
    cst[:, CC["eps"]] = EPS
    cst[:, CC["halfpi"]] = np.pi / 2
    cst[:, CC["sgn"]] = np.where(np.arange(P) < 64, 1.0, -1.0)[:, None]
    cst[:, CC["nsgn"]] = -cst[:, CC["sgn"]]
    inv = (f(10000.0) ** (-np.arange(0, MR, 2, dtype=f) / f(MR))).astype(f)
    cst[:, CC["inv"]] = inv[np.arange(P) % 32][:, None]
    lg = np.log1p(-np.exp2(-5.0 - np.arange(RH)))
    k = np.arange(P)
    cst[:, CC["zeta"]] = np.exp(lg[None, :] * (P - 1.0 - k[:, None])) * RDK ** -0.5
    for j in range(4):
        cst[:, CC["gam"].start + j] = np.exp(lg[2 * j + (k >= 64)] * P)
    rel = k[None, :] - k[:, None]
    rmask = np.where(rel[:, None, :] >= 0, np.exp(lg[None, :, None] * np.maximum(rel, 0)[:, None, :]), 0.0) * RDK ** -0.5
    xi = np.stack([np.exp(lg[2 * j + (k >= 64)][:, None] * (k[None, :] + 1.0)) for j in range(4)], 1)
    inv1 = (f(500000.0) ** (-np.arange(0, 16, 2, dtype=f) / f(16))).astype(f)
    ang = (np.arange(TOK, dtype=f)[None, :] * inv1[:, None]).astype(f)
    rope1 = np.zeros((P, 2, TOK), f)
    rope1[:, 0] = 1.0
    for b in (0, 64):
        for q in (0, 8):
            rope1[b + q:b + q + 8, 0], rope1[b + q:b + q + 8, 1] = np.cos(ang), np.sin(ang)
    kj, qi = np.arange(256)[None, :], k[:, None] + P
    band = (kj <= qi) & (qi - kj < WIN)
    gen, first = np.where(band, 0.0, NEG), np.where(band & (kj >= P), 0.0, NEG)
    cm = np.zeros((P, TOK), f)
    cm[:, TOK - P:] = np.where(k[None, :] <= k[:, None], 0.0, NEG)
    blk = (k[:, None] // GH == k[None, :] // GH).astype(f)
    diag = np.repeat(np.eye(GH, dtype=f), GR, 1)
    return {"cst": cst, "rmask": rmask.astype(f), "xi": xi.astype(f), "rope1": rope1, "msk1": np.stack([first, gen, gen], 1).astype(f),
            "cm": cm, "blk": blk}, diag


def strips_of(w, k_tiles=KT):
    K, M = w.shape
    per = KT // k_tiles
    b = w.reshape(k_tiles, P, M // P // per, per, P).transpose(2, 1, 3, 0, 4).reshape(M // P // per, P, per * k_tiles * P)
    return b if b.shape[2] == D else np.concatenate([b, np.zeros(b.shape[:2] + (D - b.shape[2],), w.dtype)], 2)


def layouts(v):
    consts, diag = constants()
    heads = [(2 * j + b) * GQA + g for j in range(2) for g in range(GQA) for b in range(2)]
    hc = (np.array(heads)[:, None] * HD + np.arange(HD)[None, :]).ravel()
    w = {"proj0": strips_of(v["w_ple_proj"][0], 2), "proj1": strips_of(v["w_ple_proj"][1], 2)}
    glu = strips_of(v["ssm_w_glu"][0])
    w["glu"] = np.stack([glu[8:], glu[:8]], 1).reshape(16, P, D)
    for i in range(2):
        for c in range(CHUNKS):
            w[f"up{i}_{c}"] = strips_of(v["w_up"][i][:, c * D:(c + 1) * D])
            w[f"down{i}_{c}"] = strips_of(v["w_down"][i][c * D:(c + 1) * D])
        w[f"gate{i}"] = strips_of(v["w_ple_gate"][i])
    w["kv"] = np.concatenate([strips_of(v["w_k"]), strips_of(v["w_v"])])
    w["q"] = strips_of(v["w_q"][0][:, hc])
    w["wo"] = strips_of(v["w_o"][0][hc])
    ein = strips_of(v["even_w_in_2"][0])
    w["even"] = np.concatenate([ein[:24], np.stack([ein[32:40], ein[40:48], ein[24:32], ein[48:56]], 1).reshape(32, P, D)])
    eo = v["even_w_out_2"][0]
    w["eout"] = np.stack([strips_of(eo[D:]), strips_of(eo[:D])], 1).reshape(16, P, D)
    oi = v["odd_w_in_2"][0]
    kr = oi[:, QL + KL:QL + KL + MR]
    w["odd"] = np.concatenate([strips_of(np.concatenate([kr, kr], 1)), strips_of(oi[:, :QL + KL])])
    w["mgate"] = strips_of(oi[:, QL + KL + MR:])
    qb = v["w_qb_2"][0].reshape(QL, MH, MN + MR)
    qb = np.concatenate([qb[:, :, :MN].reshape(QL, -1), qb[:, :, MN:].reshape(QL, -1)], 1)
    w["qb"] = strips_of(qb, 3)
    kvb = v["w_kvb_2"][0].reshape(KL, MH, 2 * P)
    w["kvb"] = strips_of(np.concatenate([kvb[:, :, :P].reshape(KL, -1), kvb[:, :, P:].reshape(KL, -1)], 1), 2)
    w["oout"] = strips_of(v["odd_w_out_2"][0])

    def cols(x):
        return x.reshape(-1, P).T

    g = {"mix1": v["norm_mix"][1], "kvn": v["kv_norm"], "mlp0": v["norm_mlp"][0], "mlp1": v["norm_mlp"][1], "ple0": v["norm_ple"][0],
         "ple1": v["norm_ple"][1], "fin": v["norm_final"], "pre0": v["pre_norm_2"][0], "pre1": v["pre_norm_2"][1],
         "post0": v["post_norm_2"][0], "post1": v["post_norm_2"][1], "gn": v["ret_gn_2"][0], "qa": v["q_a_norm_2"][0],
         "kva": v["kv_a_norm_2"][0], "cw": v["even_conv_w_2"][0].reshape(-1), "cb": v["even_conv_b_2"][0]}
    gpack = np.concatenate([cols(g[n]) if n != "sink" else np.broadcast_to(v["attn_sinks"][0][heads][None, :], (P, 16)) for n in GC], 1)
    x = v["x"][0]
    xt = x.reshape(NC, ST, GR, GH)[:, ::-1]
    dup = lambda z: np.concatenate([z, z], 0)
    lam = np.stack([dup(v["ssm_lambda_re"][0].T), dup(v["ssm_lambda_im"][0].T),
                    np.broadcast_to(v["ssm_log_dt"][0][None, :], (P, GR))], 1)
    br, bi = (v[n][0].transpose(1, 0, 2).reshape(NST, -1) for n in ("ssm_b_re", "ssm_b_im"))
    cr, ci = (v[n][0].transpose(2, 0, 1).reshape(NST, -1) for n in ("ssm_c_re", "ssm_c_im"))
    bcp = np.stack([np.concatenate(z, 0) for z in ((br, bi), (bi, br), (cr, ci), (ci, cr))], 1)
    d16 = np.stack([np.broadcast_to(v["ssm_d"][0].reshape(GR, GH).T.reshape(1, D), (GH, D)), diag], 1)
    return consts | {
        "w": np.concatenate([w[n] for n, _, _ in PHASES]), "gp": gpack, "lam": lam, "bc": bcp, "d16": d16,
        "gch": np.tile(v["norm_mix"][0].reshape(GR, GH).T, (ST, 1)),
        "xch": xt.transpose(1, 3, 2, 0).reshape(P, GR, NC),
        "xfm": x.T.reshape(KT, P, TOK).transpose(1, 0, 2),
        "p": v["p"][:, 0].transpose(0, 2, 1).reshape(2, 2, P, TOK).transpose(0, 2, 1, 3),
        "pos": v["positions_2"][0],
    }


def kernel(**inputs):
    import concourse.bacc as bacc
    from concourse.bass_utils import run_bass_kernel_spmd as run

    arrays = {k: np.ascontiguousarray(x) for k, x in layouts({k: np.asarray(x) for k, x in inputs.items()}).items()}
    nc = bacc.Bacc("TRN2", target_bir_lowering=False, num_devices=1)
    a = {k: nc.dram_tensor("in_" + k, x.shape, mybir.dt.from_np(x.dtype), kind="ExternalInput").ap() for k, x in arrays.items()}
    a["out"] = nc.dram_tensor("out", (KT, P, TOK), F32, kind="ExternalOutput").ap()
    program(nc, a)
    arrays = {"in_" + k: x for k, x in arrays.items()}
    got = run(nc, [arrays], core_ids=[0]).results[0]["out"]
    return np.ascontiguousarray(got.reshape(D, TOK).T)[None]
```

```python
from contextlib import ExitStack

import numpy as np

import concourse.bass as bass
from concourse import mybir

F32 = mybir.dt.float32
FR = mybir.dt.float32r
I32 = mybir.dt.int32
ALU = mybir.AluOpType
ACT = mybir.ActivationFunctionType
AX_X = mybir.AxisListType.X

P = 128
TOK = 512
D = 1024
KT = D // P
FF = 4 * D
CHUNKS = FF // D
PLE = 256
EPS = 1e-6
NEG = -1e30

GR, GH, NST = 64, 16, 64
ST = P // GH
NC = TOK // ST
LEVELS = 6
assert 2 ** LEVELS == NC
SG = 8
NSL = GR // SG
QUARTERS = 4
GQ = GR // QUARTERS
W8 = SG * P

HD, NKV, GQA, WIN = 64, 4, 4, 128
NB = TOK // P
RH, RDK = 8, 64
MH, MN, MR = 8, 128, 64
QL, KL = 384, 256

RING = 4
SLOTS = 4
BACKS = ((0, 3), (3, 2), (5, 2), (7, 1))
LAST_BACK = [first + many - 1 for first, many in BACKS]
LEAD = RING - 1

PHASES = [
    ("proj0", 2, 4), ("glu", 16, 1),
    *[(f"{k}0_{c}", 8, 1) for k, c in (("up", 0), ("up", 1), ("down", 0), ("up", 2), ("down", 1), ("up", 3), ("down", 2), ("down", 3))],
    ("gate0", 8, 1), ("kv", 4, 1), ("q", 8, 1), ("wo", 8, 1), ("proj1", 2, 4),
    *[(f"{k}1_{c}", 8, 1) for k, c in (("up", 0), ("up", 1), ("down", 0), ("up", 2), ("down", 1), ("up", 3), ("down", 2), ("down", 3))],
    ("gate1", 8, 1), ("even", 56, 1), ("eout", 16, 1), ("odd", 6, 1), ("qb", 6, 2), ("kvb", 4, 4), ("mgate", 8, 1), ("oout", 8, 1),
]
N_OUT = {"eout": 8}
S0, SEG0, OUT0, NSTR, SEGS = {}, {}, {}, {}, {}
_s = _g = _o = 0
for _name, _n, _k in PHASES:
    S0[_name], SEG0[_name], OUT0[_name], NSTR[_name], SEGS[_name] = _s, _g, _o, _n, _k
    _s, _g, _o = _s + _n, _g + _n * _k, _o + N_OUT.get(_name, _n * _k)
NS = _s
assert NS % RING == 0

XT = {}
_x = 0
for _name, _n in [("p0", 2), ("y", 8), ("mlp0", 8), ("hid0_0", 8), ("hid0_1", 8), ("hid0_2", 8), ("hid0_3", 8), ("gate0", 8),
                  ("kvq", 16), ("o", 8), ("p1", 2), ("mlp1", 8), ("hid1_0", 8), ("hid1_1", 8), ("hid1_2", 8), ("hid1_3", 8),
                  ("gate1", 8), ("even", 8), ("conv", 8), ("ret", 8), ("odd", 8), ("lat", 5), ("oo", 8)]:
    XT[_name] = _x
    _x += _n

CC = {}
_c = 0
for _name, _n in [("ident", P), ("perm1", P), ("perm2", P), ("ones", P),
                  ("eps", 1), ("halfpi", 1), ("sgn", 1), ("nsgn", 1), ("inv", 1), ("gam", 4), ("zeta", RH)]:
    CC[_name] = slice(_c, _c + _n)
    _c += _n
NCC = _c
GC = {}
_c = 0
for _name, _n in [("mix1", 8), ("kvn", 8), ("mlp0", 8), ("mlp1", 8), ("ple0", 8), ("ple1", 8), ("fin", 8), ("pre0", 8), ("pre1", 8),
                  ("post0", 8), ("post1", 8), ("gn", 8), ("qa", 3), ("kva", 2), ("cw", 24), ("cb", 8), ("sink", 16)]:
    GC[_name] = slice(_c, _c + _n)
    _c += _n
NGC = _c

TWO_PI = 2 * np.pi
ROUND = 12582912.0
PI_A = 6.28125
PI_B = float(np.float32(np.round((TWO_PI - PI_A) * 2**20) / 2**20))
PI_C = float(TWO_PI - PI_A - PI_B)
PI_IN = 3.1415925


class Chain:

    def __init__(self, eng, sem):
        self.eng, self.sem, self.n, self.at = eng, sem, 0, None

    def now(self):
        return self.n if self.at is None else self.n + self.at[0] * self.at[1]

    def link(self, ins):
        ins.then_inc(self.sem, 1)
        self.n += 1
        self.eng.wait_ge(self.sem, self.now())

    def each(self, i, per):
        self.at, self.first = (i, per), self.n

    def done(self, count):
        assert self.n - self.first == self.at[1], (self.n - self.first, self.at[1])
        self.n, self.at = self.first + self.at[1] * count, None


def program(nc, a):
    with ExitStack() as top:
        def sem(name):
            return top.enter_context(nc.semaphore(name))

        def area(stack, name, shape, dt=F32):
            return stack.enter_context(nc.sbuf_tensor(name, shape, dt))

        ps = top.enter_context(nc.psum_tensor("ps", [P, 8, 512], F32))
        NRM, SX, SY, SZ = 4, 5, 6, 7
        raw = area(top, "raw", [P, RING, D])
        cst = area(top, "cst", [P, NCC])
        gp = area(top, "gp", [P, NGC])
        with ExitStack() as s5:
            Wc = area(s5, "Wc", [P, GR, NC])
            Wsn = area(s5, "Wsn", [P, GR, NC])
            bb = area(s5, "bb", [P, 2, GR * GH])
            E = area(s5, "E", [P, 2, SG, P])
            ET = area(s5, "ET", [P, SG, P])
            vsb = area(s5, "vsb", [P, 512])
            z1 = area(s5, "z1", [P, 512])
            z2 = area(s5, "z2", [P, 512])
            z3 = area(s5, "z3", [P, 512])
            dec = area(s5, "dec", [P, SG, NC])
            lam = area(s5, "lam", [P, 3, GR])
            wt = area(s5, "wt", [P, LEVELS, 2, GR])
            T = area(s5, "T", [P, 2, ST * GH, GR // 2])
            S = area(s5, "S", [P, GR, NC])
            u = area(s5, "u", [P, GR, NC])
            bB = area(s5, "bB", [P, 2, GR * GH])
            d16 = area(s5, "d16", [GH, 2, D])
            tab = area(s5, "tab", [P, 26, GR])
            bC = area(s5, "bC", [P, 2, GR * GH])
            pwr = area(s5, "pwr", [P, ST + 1, GR])
            pwi = area(s5, "pwi", [P, ST + 1, GR])
            spi = area(s5, "spi", [P, ST + 1, GR])
            bt = area(s5, "bt", [P, W8])
            kst = area(s5, "kst", [P, 2, GH, GR // 2])
            blk = area(s5, "blk", [P, P])
            gch = area(s5, "gch", [P, GR])
            ssum = area(s5, "ssum", [P, 3, NC])
            G = area(s5, "G", [P, 2, SG, P])
            yg = area(s5, "yg", [P, 2, 512])
            vsw, zsw = yg[:, 0, :], yg[:, 1, :]
        main = top.enter_context(ExitStack())
        whi = area(main, "whi", [P, RING, D], FR)
        wlo = area(main, "wlo", [P, RING, D], FR)
        with ExitStack() as p0:
            X = {"P": tuple(area(p0, "P" + part, [P, 2, TOK], FR) for part in "hl")}
        h = area(main, "h", [P, KT, TOK])
        rcos = area(main, "rcos", [P, TOK])
        rsin = area(main, "rsin", [P, TOK])
        ev = area(main, "ev", [P, 2, TOK])
        sg = area(main, "sg", [P, TOK])
        sq = area(main, "sq", [P, TOK])
        acc = area(main, "acc", [P, TOK])
        std = area(main, "std", [P, TOK])
        rstd = area(main, "rstd", [P, TOK])
        cols = area(main, "cols", [P, 64])

        def pair(stack, name, tiles=KT):
            X[name] = (area(stack, name + "h", [P, tiles, TOK], FR), area(stack, name + "l", [P, tiles, TOK], FR))

        pair(main, "A")
        with ExitStack() as st:
            pair(st, "C")
            with ExitStack() as st2:
                pair(st2, "B")
                ple = area(st2, "ple", [P, KT, TOK])
            with ExitStack() as st2:
                yfm = area(st2, "yfm", [P, KT, ST, NC])
            with ExitStack() as st2:
                q1 = area(st2, "q1", [P, 8, TOK])
                k1 = area(st2, "k1", [P, 2, TOK + P])
                kv1 = area(st2, "kv1", [P, 4, TOK])
                v1 = area(st2, "v1", [P, NB, 256])
                rope1 = area(st2, "rope1", [P, 2, TOK])
                msk1 = area(st2, "msk1", [P, 3, 256])
                sm1 = area(st2, "sm1", [P, SLOTS, 2, 256])
                pt1 = area(st2, "pt1", [P, 2, 512])
            with ExitStack() as st2:
                q2 = area(st2, "q2", [P, 4, TOK])
                k2 = area(st2, "k2", [P, 4, TOK])
                v2 = area(st2, "v2", [P, NB, D])
                sgr = area(st2, "sgr", [P, KT, TOK])
                cu = area(st2, "cu", [P, TOK + 2])
                cy = area(st2, "cy", [P, TOK])
            with ExitStack() as st2:
                ybuf = area(st2, "ybuf", [P, KT, TOK])
        with ExitStack() as st2:
            for k in ("C",):
                area(st2, "pad_c", [P, 2 * KT * TOK])
            area(st2, "pad_b", [P, 3 * KT * TOK + SLOTS * TOK // 2 + 8])
            rmask = area(st2, "rmask", [P, RH, P])
            xi = area(st2, "xi", [P, 4, P])
        with ExitStack() as st:
            qn = area(st, "qn", [P, MH, TOK])
            kn = area(st, "kn", [P, MH, TOK])
            qr = area(st, "qr", [P, 4, TOK])
            kr = area(st, "kr", [P, TOK])
            v3 = area(st, "v3", [P, NB, D])
            cm = area(st, "cm", [P, TOK])
            sm3 = area(st, "sm3", [P, SLOTS, TOK])
            with ExitStack() as st2:
                pair(st2, "L", 5)
            with ExitStack() as st2:
                sg3 = area(st2, "sg3", [P, KT, TOK])
        ybuf3 = sg3
        ysc = nc.dram_tensor("ysc", [NSL, P, 512], F32, kind="Internal").ap()

        raw_in = [sem(f"raw_in{r}") for r in range(RING)]
        hi_ready = sem("hi_ready")
        lo_ready = sem("lo_ready")
        seg_done = sem("seg_done")
        evac = sem("evac")
        x_hi = sem("x_hi")
        x_lo = sem("x_lo")
        to_act = sem("to_act")
        to_dve = sem("to_dve")
        ssq_ready = sem("ssq_ready")
        sq_used = sem("sq_used")
        sq_made = sem("sq_made")
        nrm_ps = sem("nrm_ps")
        nrm_std = sem("nrm_std")
        acc_add = sem("acc_add")
        rope_ps = sem("rope_ps")
        rope_done = sem("rope_done")
        vt_ps = sem("vt_ps")
        vt_done = sem("vt_done")
        silu_done = sem("silu_done")
        dve_ch, act_ch, pool_ch = sem("dve_ch"), sem("act_ch"), sem("pool_ch")
        in_cst, in_lam, in_bc, in_x, in_d = sem("in_cst"), sem("in_lam"), sem("in_bc"), sem("in_x"), sem("in_d")
        in_h, in_p, in_pos = sem("in_h"), sem("in_p"), sem("in_pos")
        in_y = [sem(f"in_y{n}") for n in range(len(BACKS))]
        in_a1, in_rt, in_cm = sem("in_a1"), sem("in_rt"), sem("in_cm")
        fin, out_sem = sem("fin"), sem("out_sem")
        tabs, ang, sq_x, ss_x, ss_ps, std_x, u_ready = (sem(n) for n in ("tabs", "ang", "sq_x", "ss_x", "ss_ps", "std_x", "u_ready"))
        c_ready = sem("c_ready")
        u_gain, w_ready = sem("u_gain"), sem("w_ready")
        e_ready, e_used, et_ps, et_sb, v_ps, v_sb, vp, d_ready, z_ready, zp, s_ready = (
            sem(n) for n in ("e_ready", "e_used", "et_ps", "et_sb", "v_ps", "v_sb", "vp", "d_ready", "z_ready", "zp", "s_ready"))
        g_first = sem("g_first")
        k_out = sem("k_out")
        kst_ready, t_zero, g_ready, y_ps, yg_ready = (sem(n) for n in ("kst_ready", "t_zero", "g_ready", "y_ps", "yg_ready"))
        toep = [sem("toep0"), sem("toep1")]
        y_out = [sem("y_out0"), sem("y_out1")]
        sc_ps, sc_out, p_ready, pt_ps, pt_ready, o_ps, o_out = (sem(n) for n in ("sc_ps", "sc_out", "p_ready", "pt_ps", "pt_ready", "o_ps", "o_out"))
        rk_ps, rs_ps, rk_sb, rs_sb, rkv_ps, rpv, r_ps, r_out = (
            sem(n) for n in ("rk_ps", "rs_ps", "rk_sb", "rs_sb", "rkv_ps", "rpv", "r_ps", "r_out"))

        def C(name):
            return cst[:, CC[name]]

        def gain(name, m):
            return gp[:, GC[name].start + m:GC[name].start + m + 1]

        eps = C("eps")
        UG = GR // 4
        M8 = 20
        U1 = 8 * 2 * 2
        U3 = MH * NB
        MSCALE = float(MN + MR) ** -0.5
        LAT_K = {"qb": 3, "kvb": 2}

        p_raw = tab[:, M8 - 16:M8, :].rearrange("p (k a) c -> p k (a c)", k=2)
        squares = (sq, cy)

        def over(x, axis, n):
            x = x.unsqueeze(axis)
            shape = list(x.shape)
            shape[axis] = n
            return x.to_broadcast(shape)

        def by_group(x):
            return x.rearrange("p (g h) -> p g h", h=GH)

        def matrices(eng, ch, out, tr, pw, pi, first, x, z, gs, op):
            def pws(p):
                return over(p[:, first:first + ST, gs].rearrange("p r g -> p g r"), 3, GH)

            def mat(x):
                return over(x[:, gs, :], 2, ST)

            def cols4(x):
                return x.rearrange("p (g r h) -> p g r h", r=ST, h=GH)

            eng.tensor_tensor(cols4(out), pws(pw), mat(x), ALU.mult)
            ch.link(eng.tensor_tensor(cols4(tr), pws(pi), mat(z), ALU.mult))
            return eng.tensor_tensor(out, out, tr, op)

        def out_place(sl):
            return (G if sl // 2 % 2 == 0 else E)[:, sl % 2, :, :]

        def output_matrices(eng, ch, sl, scratch):
            gs = slice(sl * SG, (sl + 1) * SG)
            return matrices(eng, ch, out_place(sl).rearrange("p g n -> p (g n)"), scratch, pwr, pwi, 1, by_group(bC[:, 0, :]), by_group(bC[:, 1, :]), gs, ALU.subtract)

        finpre = cols[:, 0:KT]
        acc2 = cu[:, 2:]

        block = top.enter_context(nc.Block())

        @block.sync
        def _(sp):
            sp.dma_start(lam[:, :, :], a["lam"]).then_inc(in_lam, 16)
            sp.dma_start(cst[:, :], a["cst"]).then_inc(in_cst, 16)
            sp.dma_start(gp[:, :], a["gp"]).then_inc(in_cst, 16)
            sp.dma_start(bB[:, :, :], a["bc"][:, 0:2, :]).then_inc(in_bc, 16)
            sp.dma_start(u[:, :, :], a["xch"]).then_inc(in_x, 16)
            sp.dma_start(gch[:, :], a["gch"]).then_inc(in_d, 16)
            sp.dma_start(blk[:, :], a["blk"]).then_inc(in_d, 16)
            sp.dma_start(bC[:, :, :], a["bc"][:, 2:4, :]).then_inc(in_bc, 16)
            sp.dma_start(d16[:, :, :], a["d16"]).then_inc(in_d, 16)
            for r in range(RING):
                sp.dma_start(raw[:, r, :], a["w"][r, :, :]).then_inc(raw_in[r], 16)
            def toeplitz(half):
                sp.wait_ge(kst_ready, half + 1)
                sp.wait_ge(t_zero, 1)
                for t in range(ST):
                    sp.dma_start(T[GH * (ST - 1 - t):P, half, GH * t:GH * (t + 1), :], kst[0:GH * (t + 1), half, :, :]).then_inc(toep[half], 16)

            def change_over(dst, src, done):
                for b in range(2):
                    sp.dma_start(dst[64 * b:64 * b + 64, :], src[64 - 64 * b:128 - 64 * b, :]).then_inc(done, 16)

            for sl in range(NSL):
                sp.wait_ge(v_sb, sl + 1)
                if sl:
                    sp.wait_ge(z_ready, sl)
                change_over(vsw, vsb, vp)
                if sl == NSL // 2 + 1:
                    toeplitz(0)
                if sl == NSL - 1:
                    toeplitz(1)
                if sl == NSL - 2:
                    sp.wait_ge(e_ready, NSL)
                    sp.dma_start(p_raw, a["p"][0, :, :, :]).then_inc(in_p, 16)
                sp.wait_ge(z_ready, sl + 1)
                if sl:
                    sp.wait_ge(s_ready, sl)
                change_over(zsw, z2, zp)
            sp.wait_ge(s_ready, NSL)
            sp.dma_start(rcos[:, :].bitcast(I32), a["pos"].partition_broadcast(P)).then_inc(in_pos, 16)

            def back(n):
                first, many = BACKS[n]
                for sl in range(first, first + many):
                    sp.wait_ge(y_out[sl % 2], 16 * (sl // 2 + 1))
                for g in range(SG):
                    sp.dma_start(yfm[GH * g:GH * (g + 1), first:first + many, :, :].rearrange("p s t c -> p (s t) c"),
                                 ysc[first:first + many, :, g * NC:(g + 1) * NC].rearrange("s (t h) c -> h (s t) c", h=GH)).then_inc(in_y[n], 16)

            def next_strip(i, r):
                sp.wait_ge(lo_ready, RING * i + (r - RING + 1))
                sp.dma_start(raw[:, r, :], a["w"][RING * i + r, :, :]).then_inc(raw_in[r], 16)

            for r in range(RING):
                next_strip(1, r)
            for n in range(len(BACKS)):
                back(n)
            sp.wait_ge(y_ps, NSL)
            sp.dma_start(h[:, KT // 2:KT, :], a["xfm"][:, KT // 2:KT, :]).then_inc(in_h, 16)
            sp.wait_ge(seg_done, SEG0["glu"])
            sp.dma_start(h[:, 0:KT // 2, :], a["xfm"][:, 0:KT // 2, :]).then_inc(in_h, 16)
            sp.dma_start(rmask[:, :, :], a["rmask"]).then_inc(in_rt, 16)
            sp.dma_start(xi[:, :, :], a["xi"]).then_inc(in_rt, 16)
            with sp.Fori(2, NS // RING) as i:
                for r in range(RING):
                    next_strip(i, r)
            for m in range(KT):
                sp.wait_ge(fin, m + 1)
                sp.dma_start(a["out"][m, :, :], h[:, m, :]).then_inc(out_sem, 16)
            sp.wait_ge(out_sem, 16 * KT)

        @block.gpsimd
        def _(pool):
            ch = Chain(pool, pool_ch)
            nc.gpsimd.memset(T[:, :, :, :], 0.0).then_inc(t_zero, 1)
            pool.wait_ge(tabs, 2)
            turn_r, turn_i, s1, s2, s3 = (tab[:, k, :] for k in range(21, 26))
            ch.link(nc.gpsimd.tensor_scalar(turn_i, tab[:, 6, :], C("sgn"), None, ALU.mult))

            def square_turn(o_r, o_i, w_r, w_i):
                nc.gpsimd.tensor_tensor(s1, w_r, w_i, ALU.mult)
                nc.gpsimd.tensor_tensor(s2, w_r, w_r, ALU.mult)
                ch.link(nc.gpsimd.tensor_tensor(s3, w_i, w_i, ALU.mult))
                nc.gpsimd.tensor_tensor(o_r, s2, s3, ALU.subtract)
                ch.link(nc.gpsimd.tensor_tensor(o_i, s1, s1, ALU.add))

            square_turn(turn_r, turn_i, tab[:, 8, :], turn_i)
            square_turn(turn_r, turn_i, turn_r, turn_i)
            square_turn(wt[:, 0, 0, :], wt[:, 0, 1, :], turn_r, turn_i)
            for k in range(1, LEVELS):
                square_turn(wt[:, k, 0, :], wt[:, k, 1, :], wt[:, k - 1, 0, :], wt[:, k - 1, 1, :])
            pool.wait_ge(sq_x, 1)
            pool.wait_ge(in_d, 48)
            nc.gpsimd.tensor_tensor(u[:, 0:UG, :], u[:, 0:UG, :], over(gch[:, 0:UG], 2, NC), ALU.mult).then_inc(u_gain, 1)
            scratch = G[:, :, :, :].rearrange("p b g n -> p (b g n)")
            for q in range(QUARTERS):
                gs = slice(q * GQ, (q + 1) * GQ)
                nc.gpsimd.memset(Wc[:, gs, 0:1], 1.0)
                ch.link(nc.gpsimd.memset(Wsn[:, gs, 0:1], 0.0))
                for k in range(LEVELS):
                    m = 2 ** k
                    w_r, w_i = (over(wt[:, k, b, gs], 2, m) for b in range(2))
                    s1, s2, s3, s4 = (scratch[:, b * 512:b * 512 + GQ * m].rearrange("p (g c) -> p g c", c=m) for b in range(4))
                    nc.gpsimd.tensor_tensor(s1, Wc[:, gs, 0:m], w_r, ALU.mult)
                    nc.gpsimd.tensor_tensor(s2, Wsn[:, gs, 0:m], w_i, ALU.mult)
                    nc.gpsimd.tensor_tensor(s3, Wc[:, gs, 0:m], w_i, ALU.mult)
                    ch.link(nc.gpsimd.tensor_tensor(s4, Wsn[:, gs, 0:m], w_r, ALU.mult))
                    nc.gpsimd.tensor_tensor(Wc[:, gs, m:2 * m], s1, s2, ALU.subtract)
                    last = nc.gpsimd.tensor_tensor(Wsn[:, gs, m:2 * m], s3, s4, ALU.add)
                    if k < LEVELS - 1:
                        ch.link(last)
                last.then_inc(w_ready, 1)
                pool.wait_ge(w_ready, q + 1)
            def low_strip(i, r):
                pool.wait_ge(hi_ready, RING * i + r + 1)
                nc.gpsimd.tensor_tensor(wlo[:, r, :], raw[:, r, :], whi[:, r, :].bitcast(F32), ALU.subtract).then_inc(lo_ready, 1)

            pool.wait_ge(c_ready, 1)
            output_matrices(nc.gpsimd, ch, 0, bB[:, 0, :]).then_inc(g_first, 1)
            low_strip(0, 0)
            output_matrices(nc.gpsimd, ch, 1, bB[:, 1, :]).then_inc(g_first, 1)
            for k in range(2):
                pool.wait_ge(x_hi, XT["p0"] + k + 1)
                nc.gpsimd.tensor_tensor(X["P"][1][:, k, :], p_raw[:, k, :], X["P"][0][:, k, :].bitcast(F32), ALU.subtract).then_inc(x_lo, 1)
            for r in range(1, RING):
                low_strip(0, r)
            with pool.Fori(1, NS // RING) as i:
                for r in range(RING):
                    low_strip(i, r)

        @block.scalar
        def _(act):
            ch = Chain(act, act_ch)
            got = [0]
            nrm = [0]
            xs = [0]

            def split_strip(t, seg, slot=None, turn=None):
                if slot is None:
                    slot, turn = t % RING, t // RING + 1
                act.wait_ge(raw_in[slot], 16 * turn)
                if not isinstance(seg, int) or seg > 0:
                    act.wait_ge(seg_done, seg)
                nc.scalar.activation(whi[:, slot, :], raw[:, slot, :], ACT.Copy).then_inc(hi_ready, 1)

            def ahead(name, l):
                t = S0[name] + l + LEAD
                if t < NS:
                    split_strip(t, SEG0[name] + SEGS[name] * l)

            def ahead_loop(name, i, j):
                t = S0[name] + j + LEAD
                split_strip(None, SEG0[name] + SEGS[name] * j + SEGS[name] * RING * i, t % RING, t // RING + 1 + i)

            def answer(ins):
                ins.then_inc(to_dve, 1)

            def asked():
                got[0] += 1
                act.wait_ge(to_act, got[0])

            def high(dst, m, src, scale=None):
                if scale is None:
                    nc.scalar.activation(X[dst][0][:, m, :], src, ACT.Copy).then_inc(x_hi, 1)
                else:
                    nc.scalar.activation(X[dst][0][:, m, :], src, ACT.Copy, scale=scale).then_inc(x_hi, 1)
                xs[0] += 1

            def root(n):
                nrm[0] += 1
                act.wait_ge(nrm_ps, nrm[0])
                nc.scalar.activation(std[:, :], ps[:, NRM, :], ACT.Sqrt, bias=eps, scale=1.0 / n).then_inc(nrm_std, 1)

            act.wait_ge(in_lam, 16)
            nc.scalar.activation(tab[:, 0, :], lam[:, 2, :], ACT.Exp).then_inc(tabs, 1)
            act.wait_ge(ang, 1)
            act.wait_ge(in_cst, 32)
            nc.scalar.activation(tab[:, 5, :], tab[:, 1, :], ACT.Exp)
            nc.scalar.activation(tab[:, 6, :], tab[:, 4, :], ACT.Sin)
            ch.link(nc.scalar.activation(tab[:, 7, :], tab[:, 4, :], ACT.Abs))
            nc.scalar.activation(tab[:, 8, :], tab[:, 7, :], ACT.Sin, bias=C("halfpi"), scale=-1.0).then_inc(tabs, 1)
            act.wait_ge(in_x, 16)
            nc.scalar.activation(S[:, :, :], u[:, :, :], ACT.Square).then_inc(sq_x, 1)
            act.wait_ge(sq_x, 1)
            act.wait_ge(in_d, 48)
            for g in range(UG, GR):
                last = nc.scalar.activation(u[:, g, :], u[:, g, :], ACT.Copy, scale=gch[:, g:g + 1])
            last.then_inc(u_gain, 1)
            act.wait_ge(ss_x, 1)
            nc.scalar.activation(ssum[:, 1, :], ssum[:, 0, :], ACT.Sqrt, bias=eps, scale=1.0 / D).then_inc(std_x, 1)
            for sl in range(NSL):
                if sl:
                    act.wait_ge(v_ps, sl)
                for half in range(2):
                    act.wait_ge(et_ps, 2 * sl + half + 1)
                    nc.scalar.copy(ET[:, 4 * half:4 * half + 4, :], ps[:, 2 + half, :].rearrange("p (g n) -> p g n", g=4)).then_inc(et_sb, 1)
                if sl in (NSL // 2, NSL - 1):
                    b = int(sl == NSL - 1)
                    act.wait_ge(e_used, NSL // 2 * (b + 1))
                    nc.scalar.copy(kst[:, b, :, :].rearrange("p h g -> p g h"), by_group(ps[:, b, :])).then_inc(k_out, 1)
                act.wait_ge(v_ps, sl + 1)
                if sl:
                    act.wait_ge(z_ready, sl)
                nc.scalar.copy(vsb[:, :], ps[:, SX, :]).then_inc(v_sb, 1)
                nc.scalar.copy(dec[:, :, 1:NC], over(tab[:, M8, sl * SG:(sl + 1) * SG], 2, NC - 1)).then_inc(d_ready, 1)
                if sl == NSL - 1:
                    act.wait_ge(in_p, 16)
                    for k in range(2):
                        high("P", k, p_raw[:, k, :])
                if sl == NSL - 2:
                    act.wait_ge(s_ready, 2)
                    split_strip(0, 0)
            for sl in range(NSL):
                if sl == 0:
                    act.wait_ge(z_ready, NSL)
                if sl == 1:
                    act.wait_ge(s_ready, NSL)
                    for t in range(1, LEAD):
                        split_strip(t, 0)
                if sl == 2:
                    ahead("proj0", 0)
                act.wait_ge(y_ps, sl + 1)
                if sl >= 2:
                    act.wait_ge(y_out[sl % 2], 16 * (sl // 2))
                nc.scalar.activation(yg[:, sl % 2, :], ps[:, 2 + sl % 2, :], ACT.Gelu_apprx_tanh).then_inc(yg_ready, 1)
                act.wait_ge(yg_ready, sl + 1)
                act.dma_start(ysc[sl, :, :], yg[:, sl % 2, :]).then_inc(y_out[sl % 2], 16)
            asked()
            ch.link(nc.scalar.activation(rcos[:, :], rsin[:, :], ACT.Abs))
            nc.scalar.activation(rsin[:, :], rsin[:, :], ACT.Sin)
            answer(nc.scalar.activation(rcos[:, :], rcos[:, :], ACT.Sin, bias=C("halfpi"), scale=-1.0))
            for m in range(KT):
                act.wait_ge(in_y[[sl >= m for sl in LAST_BACK].index(True)], 16 * SG)
                nc.scalar.activation(X["A"][0][:, m, :].rearrange("p (c t) -> p c t", t=ST),
                                     yfm[:, m, :, :].rearrange("p t c -> p c t"), ACT.Copy).then_inc(x_hi, 1)
                xs[0] += 1
            ahead("proj0", 1)
            for m in range(KT):
                ahead("glu", 2 * m)
                ahead("glu", 2 * m + 1)
                o = OUT0["glu"] + 2 * m
                act.wait_ge(seg_done, SEG0["glu"] + 2 * m + 1)
                answer(nc.scalar.activation(sg[:, :], ps[:, o % RING, :], ACT.Sigmoid))
                asked()
                high("B", m, h[:, m, :], gain("mlp0", m))
                answer(nc.scalar.activation(sq[:, :], h[:, m, :], ACT.Square))

            def mlp(layer):
                root(D)
                for kind, c in (("up", 0), ("up", 1), ("down", 0), ("up", 2), ("down", 1), ("up", 3), ("down", 2), ("down", 3)):
                    name = f"{kind}{layer}_{c}"
                    if kind == "up":
                        dst = X["AC"[c % 2]][0]
                        with act.Fori(0, 8 // RING) as i:
                            for j in range(RING):
                                ahead_loop(name, i, j)
                                act.wait_ge(evac, OUT0[name] + RING * i + j + 1)
                                nc.scalar.activation(sg[:, :], ev[:, 0, :], ACT.Square)
                                nc.scalar.activation(dst[:, RING * i + j, :], ev[:, 0, :], ACT.Square).then_inc(x_hi, 1)
                        xs[0] += 8
                    elif c < CHUNKS - 1:
                        with act.Fori(0, 8 // RING) as i:
                            for j in range(RING):
                                ahead_loop(name, i, j)
                    else:
                        for m in range(KT):
                            ahead(name, m)
                            act.wait_ge(evac, OUT0[name] + m + 1)
                            high("B", m, h[:, m, :], gain(f"ple{layer}", m))
                            answer(nc.scalar.activation(sq[:, :], h[:, m, :], ACT.Square))

            def gate(layer):
                ahead(f"gate{layer}", 0)
                root(D)
                for m in range(KT):
                    act.wait_ge(evac, OUT0[f"gate{layer}"] + m + 1)
                    answer(nc.scalar.activation(sg[:, :], ev[:, 0, :], ACT.Sigmoid))
                    if m + 1 < KT:
                        ahead(f"gate{layer}", m + 1)
                    asked()
                    if layer == 0:
                        high("A", m, h[:, m, :], gain("kvn", m))
                        high("C", m, h[:, m, :], gain("mix1", m))
                    else:
                        high("C", m, h[:, m, :], finpre[:, m:m + 1])
                        nc.scalar.activation(cy[:, :], h[:, m, :], ACT.Square, scale=gain("fin", m))
                    answer(nc.scalar.activation(sq[:, :], h[:, m, :], ACT.Square))

            mlp(0)
            gate(0)
            act.wait_ge(seg_done, SEG0["kv"])
            act.wait_ge(x_lo, XT["kvq"] + 16)
            act.dma_start(rope1[:, :, :], a["rope1"]).then_inc(in_a1, 16)
            act.dma_start(msk1[:, :, :], a["msk1"]).then_inc(in_a1, 16)
            root(D)
            for l in range(NSTR["kv"]):
                ahead("kv", l)
            for l in range(2):
                ahead("q", l)
            for j in range(2):
                act.wait_ge(vt_ps, j + 1)
                nc.scalar.copy(v1[:, :, j * P:(j + 1) * P], ps[:, NRM, :].rearrange("p (n d) -> p n d", n=NB)).then_inc(vt_done, 1)

            act.dma_start(sq[:, :], a["p"][1, :, 0, :]).then_inc(in_p, 16)
            act.dma_start(acc[:, :], a["p"][1, :, 1, :]).then_inc(in_p, 16)

            def exp1(un):
                b, q0 = un // 2 % 2, 16 * (un % SLOTS)
                sink = gain("sink", un // 4 * 2 + b)
                asked()
                for n in range(2):
                    nc.scalar.activation(sm1[:, un % SLOTS, n, :], sm1[:, un % SLOTS, n, :], ACT.Exp, bias=cols[:, q0 + 4 + n:q0 + 5 + n],
                                         scale=float(HD) ** -0.5, accum_out=cols[:, q0 + 6 + n:q0 + 7 + n])
                answer(nc.scalar.activation(cols[:, q0 + 8:q0 + 10], cols[:, q0 + 4:q0 + 6], ACT.Exp, bias=sink))

            exp1(0)
            exp1(1)
            for un in range(U1):
                if un + 2 < U1:
                    exp1(un + 2)
                act.wait_ge(pt_ps, un + 1)
                nc.scalar.copy(pt1[:, un % 2, :], ps[:, 2 + un % 2, :]).then_inc(pt_ready, 1)
                if un % 4 == 1 and un > 4:
                    m = un // 4 - 1
                    act.wait_ge(o_ps, m + 1)
                    high("A", m, ps[:, SX + m % 2, :])
                if un % 4 == 2 and un // 4 + 2 < NSTR["q"]:
                    ahead("q", un // 4 + 2)
            act.wait_ge(o_ps, KT)
            high("A", KT - 1, ps[:, SX + (KT - 1) % 2, :])
            act.wait_ge(in_p, 48)
            for k in range(2):
                high("C", k, (sq, acc)[k][:, :])
            for m in range(KT):
                ahead("wo", m)
                act.wait_ge(evac, OUT0["wo"] + m + 1)
                high("B", m, h[:, m, :], gain("mlp1", m))
                answer(nc.scalar.activation(sq[:, :], h[:, m, :], ACT.Square))
            for l in range(2):
                ahead("proj1", l)
            mlp(1)
            gate(1)
            E0 = OUT0["even"]
            for l in range(2):
                ahead("even", l)
            root(D)
            nrm[0] += 1
            asked()
            nc.scalar.activation(std[:, :], sq[:, :], ACT.Sqrt, bias=eps, scale=1.0 / D).then_inc(nrm_std, 1)
            for l in range(2, 8):
                ahead("even", l)

            def value(n, dst, m, bank=SZ):
                act.wait_ge(vt_ps, n + 1)
                nc.scalar.copy(dst[:, :, m * P:(m + 1) * P], ps[:, bank, :].rearrange("p (n d) -> p n d", n=NB)).then_inc(vt_done, 1)

            for m in range(8):
                ahead("even", 8 + m)
                if m:
                    value(2 + m - 1, v2, m - 1)
            value(2 + 7, v2, 7)
            for m in range(8):
                ahead("even", 16 + m)
                act.wait_ge(evac, E0 + 16 + m + 1)
                nc.scalar.activation(sgr[:, m, :], ev[:, m % 2, :], ACT.Silu).then_inc(silu_done, 1)
            def head_squares(hh):
                act.wait_ge(r_ps, hh + 1)
                nc.scalar.activation(sq[:, :], ps[:, (SZ, SY)[hh % 2], :], ACT.Square).then_inc(ssq_ready, 1)

            for t in range(8):
                jp = t // 2
                ahead("even", 24 + 4 * t)
                if t % 2:
                    head_squares(2 * jp)
                ahead("even", 24 + 4 * t + 1)
                if t % 2:
                    root(P)
                    head_squares(2 * jp + 1)
                ahead("even", 24 + 4 * t + 2)
                asked()
                answer(nc.scalar.activation(cy[:, :], cu[:, 0:TOK], ACT.Identity, bias=gain("cb", t), scale=gain("cw", t)))
                if t % 2:
                    act.wait_ge(r_out, 2 * jp + 1)
                    root(P)
                ahead("even", 24 + 4 * t + 3)
                act.wait_ge(evac, E0 + 24 + 4 * t + 4)
                answer(nc.scalar.activation(sg[:, :], ev[:, 0, :], ACT.Silu))
                asked()
                high("A", t, cy[:, :])
            act.wait_ge(seg_done, SEG0["eout"])
            for hh in range(RH):
                act.wait_ge(r_out, hh + 1)
                high("C", hh, sgr[:, hh, :])

            def post(name):
                for m in range(KT):
                    for l in ((2 * m, 2 * m + 1) if name == "eout" else (m,)):
                        ahead(name, l)
                    act.wait_ge(evac, OUT0[name] + m + 1)
                    answer(nc.scalar.activation(sq[:, :], (ybuf if name == "eout" else ybuf3)[:, m, :], ACT.Square))
                root(D)

            post("eout")
            act.dma_start(cm[:, :], a["cm"]).then_inc(in_cm, 16)
            for m in range(KT):
                asked()
                high("A", m, h[:, m, :], gain("pre1", m))
                if m >= 2:
                    act.wait_ge(sq_used, m - 1)
                nc.scalar.activation(squares[m % 2][:, :], h[:, m, :], ACT.Square).then_inc(sq_made, 1)
            root(D)
            O0 = OUT0["odd"]
            ahead("odd", 0)
            for m in range(5):
                ahead("odd", 1 + m)
                act.wait_ge(evac, O0 + 1 + m + 1)
                high("L", m, kn[:, m, :], gain("qa", m) if m < 3 else gain("kva", m - 3))
                answer(nc.scalar.activation(sq[:, :], kn[:, m, :], ACT.Square))
                if m == 2:
                    root(QL)
            for l in range(NSTR["qb"]):
                ahead("qb", l)
            root(KL)
            for l in range(NSTR["kvb"]):
                ahead("kvb", l)
            for m in range(8):
                value(10 + m, v3, m, (SZ, NRM)[m % 2])

            def exp3(un):
                n, q0 = (un % NB + 1) * P, 8 * (un % SLOTS)
                asked()
                answer(nc.scalar.activation(sm3[:, un % SLOTS, 0:n], sm3[:, un % SLOTS, 0:n], ACT.Exp, bias=cols[:, q0 + 1:q0 + 2],
                                            scale=MSCALE, accum_out=cols[:, q0 + 2:q0 + 3]))

            def gates(m):
                act.wait_ge(evac, OUT0["mgate"] + m + 1)
                nc.scalar.activation(sg3[:, m, :], sg3[:, m, :], ACT.Silu).then_inc(silu_done, 1)

            exp3(0)
            exp3(1)
            for un in range(U3):
                n = (un % NB + 1) * P
                if un + 2 < U3:
                    exp3(un + 2)
                act.wait_ge(pt_ps, U1 + un + 1)
                nc.scalar.copy(ev[:, un % 2, 0:n], ps[:, 2 + un % 2, 0:n]).then_inc(pt_ready, 1)
                if un % NB == 0 and un:
                    gates(un // NB - 1)
                if un % NB == 1 and un > NB:
                    act.wait_ge(o_out, un // NB)
                    high("C", un // NB - 1, sg[:, :])
                if un % NB == 2:
                    ahead("mgate", un // NB)
            gates(MH - 1)
            act.wait_ge(o_out, MH)
            high("C", MH - 1, sg[:, :])
            post("oout")
            assert xs[0] == XT["oo"] + 8

        @block.tensor
        def _(pe):
            nrm = [0]
            def product(slot, k, bank, xh, xl, first, last):
                w = slice(k * P, (k + 1) * P)
                out = ps[:, bank, :]
                nc.tensor.matmul(out, whi[:, slot, w], xh, start=first, stop=False)
                nc.tensor.matmul(out, whi[:, slot, w], xl, start=False, stop=False)
                return nc.tensor.matmul(out, wlo[:, slot, w], xh, start=False, stop=last)

            def short_strip(name, l, per, k_tiles, x, xt, x0=0, bank0=None):
                slot = (S0[name] + l) % RING
                pe.wait_ge(lo_ready, S0[name] + l + 1)
                for q in range(per):
                    o = OUT0[name] + per * l + q
                    bank = o % RING if bank0 is None else bank0 + q
                    if o >= RING:
                        pe.wait_ge(evac, o - RING + 1)
                    for k in range(k_tiles):
                        pe.wait_ge(x_lo, xt + x0 + k + 1)
                        last = product(slot, q * k_tiles + k, bank, X[x][0][:, x0 + k, :], X[x][1][:, x0 + k, :], k == 0, k == k_tiles - 1)
                    last.then_inc(seg_done, 1)

            pe.wait_ge(in_d, 48)
            pe.wait_ge(in_cst, 32)
            def transpose_inputs(sl):
                pe.wait_ge(e_ready, sl + 1)
                for half in range(2):
                    if sl:
                        pe.wait_ge(et_sb, 2 * sl - 1 + half)
                    for g in range(4):
                        last = nc.tensor.transpose(ps[:, 2 + half, g * P:(g + 1) * P], E[:, sl % 2, 4 * half + g, :], C("ident"))
                    last.then_inc(et_ps, 1)

            pe.wait_ge(sq_x, 1)
            for k in range(GR // SG):
                last = nc.tensor.matmul(ps[:, NRM, :], blk[:, :], S[:, k * SG:(k + 1) * SG, :].rearrange("p g c -> p (g c)"),
                                        start=(k == 0), stop=(k == GR // SG - 1))
            last.then_inc(ss_ps, 1)
            transpose_inputs(0)
            for sl in range(NSL):
                pe.wait_ge(c_ready, 1)
                for g in range(SG):
                    gg = sl * SG + g
                    last = nc.tensor.matmul(ps[:, gg // 32, gg % 32 * GH:(gg % 32 + 1) * GH], E[:, sl % 2, g, :], bC[:, 0, gg * GH:(gg + 1) * GH],
                                            start=True, stop=True)
                last.then_inc(e_used, 1)
                pe.wait_ge(et_sb, 2 * sl + 2)
                pe.wait_ge(u_ready, 1)
                if sl:
                    pe.wait_ge(v_sb, sl)
                for g in range(SG):
                    last = nc.tensor.matmul(ps[:, SX, g * NC:(g + 1) * NC], ET[:, g, :], u[:, sl * SG + g, :], start=True, stop=True)
                last.then_inc(v_ps, 1)
                if sl + 1 < NSL:
                    transpose_inputs(sl + 1)
            for sl in range(NSL):
                if sl % (NSL // 2) == 0:
                    pe.wait_ge(toep[2 * sl // NSL], 16 * ST)
                if sl < 2:
                    pe.wait_ge(g_first, sl + 1)
                else:
                    pe.wait_ge(g_ready, sl - 1)
                pe.wait_ge(s_ready, sl + 1)
                if sl >= 2:
                    pe.wait_ge(yg_ready, sl - 1)
                for g in range(SG):
                    gg = sl * SG + g
                    nc.tensor.matmul(ps[:, 2 + sl % 2, g * NC:(g + 1) * NC], T[:, gg // (GR // 2), :, gg % (GR // 2)], u[:, gg, :],
                                     start=True, stop=False)
                    last = nc.tensor.matmul(ps[:, 2 + sl % 2, g * NC:(g + 1) * NC], out_place(sl)[:, g, :], S[:, gg, :],
                                            start=False, stop=True)
                last.then_inc(y_ps, 1)
                if sl == 0:
                    pe.wait_ge(v_sb, NSL)
                    short_strip("proj0", 0, 4, 2, "P", XT["p0"], bank0=NRM)
            def strip(name, l, j, x, xt, step=1, each=None):
                slot, bank = (S0[name] + j) % RING, (OUT0[name] + j) % RING
                pe.wait_ge(lo_ready, S0[name] + l + 1)
                pe.wait_ge(evac, OUT0[name] + l - RING + 1)
                for k in range(KT):
                    if j == 0:
                        pe.wait_ge(x_lo, xt + step * k + 1)
                    last = product(slot, k, bank, X[x][0][:, k, :], X[x][1][:, k, :], k == 0, k == KT - 1)
                    if each is not None:
                        each(k)
                last.then_inc(seg_done, 1)

            def strip_part(name, l, part, x):
                slot = (S0[name] + l) % RING
                if part == 0:
                    pe.wait_ge(lo_ready, S0[name] + l + 1)
                    pe.wait_ge(evac, OUT0[name] + l)
                for k in (2 * part, 2 * part + 1):
                    last = product(slot, k, NRM, X[x][0][:, k, :], X[x][1][:, k, :], k == 0, k == KT - 1)
                if part == 3:
                    last.then_inc(seg_done, 1)

            def add_squares(k):
                pe.wait_ge(sq_made, k + 1)
                last = nc.tensor.matmul(ps[:, NRM, :], C("ones"), squares[k % 2][:, :], start=(k == 0), stop=(k == KT - 1))
                last.then_inc(sq_used if k < KT - 1 else nrm_ps, 1)

            def strips(name, x, xt, step=1, n=8, between=None):
                if between is None:
                    with pe.Fori(0, n // RING) as i:
                        for j in range(RING):
                            strip(name, RING * i + j, j, x, xt, step)
                else:
                    for l in range(n):
                        strip(name, l, l, x, xt, step)
                        if l == 0:
                            between()

            def norm(src=None, bank=NRM):
                nrm[0] += 1
                pe.wait_ge(ssq_ready, nrm[0])
                nc.tensor.matmul(ps[:, bank, :], C("ones"), acc[:, :] if src is None else src, start=True, stop=True).then_inc(nrm_ps, 1)

            def mlp(layer):
                for kind, c in (("up", 0), ("up", 1), ("down", 0), ("up", 2), ("down", 1), ("up", 3), ("down", 2), ("down", 3)):
                    if kind == "up":
                        strips(f"up{layer}_{c}", "B", XT[f"mlp{layer}"], between=None if c else norm)
                    else:
                        strips(f"down{layer}_{c}", "AC"[c % 2], XT[f"hid{layer}_{c}"])
                strips(f"gate{layer}", "B", XT[f"gate{layer}"], between=norm)

            def partners(n, perm, src, bank):
                nc.tensor.matmul(ps[:, bank, :], C(perm), src, start=True, stop=True).then_inc(rope_ps, 1)

            def transposes(src, bank, n=NB):
                for k in range(n):
                    last = nc.tensor.transpose(ps[:, bank, k * P:(k + 1) * P], src[:, k * P:(k + 1) * P], C("ident"))
                return last

            pe.wait_ge(yg_ready, NSL)
            short_strip("proj0", 1, 4, 2, "P", XT["p0"])
            strips("glu", "A", XT["y"], n=16)
            mlp(0)
            strips("kv", "A", XT["kvq"], 2, n=NSTR["kv"], between=norm)
            strip("q", 0, 0, "C", XT["kvq"] + 1, 2)
            pe.wait_ge(evac, OUT0["q"] + 1)
            partners(0, "perm1", kv1[:, 0, :], SX)
            partners(1, "perm1", kv1[:, 1, :], SY)
            for j in range(2):
                if j:
                    pe.wait_ge(vt_done, j)
                transposes(kv1[:, 2 + j, :], NRM).then_inc(vt_ps, 1)
            partners(2, "perm1", q1[:, 0, :], SZ)
            pe.wait_ge(vt_done, 2)
            for part in range(4):
                strip_part("q", 1, part, "C")

            def scores1(un):
                m, b, r = un // 4, un // 2 % 2, slice(64 * (un // 2 % 2), 64 * (un // 2 % 2) + 64)
                pe.wait_ge(rope_done, 3 + m)
                if un >= 2:
                    pe.wait_ge(sc_out, un - 1)
                for k in range(2):
                    n = un % 2 * 2 + k
                    last = nc.tensor.matmul(ps[:, un % 2, k * 256:(k + 1) * 256], q1[r, m, n * P:(n + 1) * P],
                                            k1[r, m // 4, n * P:(n + 2) * P], start=True, stop=True)
                last.then_inc(sc_ps, 1)

            def values1(un):
                m, b = un // 4, un // 2 % 2
                r = slice(64 * b, 64 * b + 64)
                pe.wait_ge(pt_ready, un + 1)
                if un == 0:
                    pe.wait_ge(vt_done, 2)
                if un % 4 == 0 and m >= 2:
                    pe.wait_ge(x_lo, XT["o"] + m - 1)
                for k in range(2):
                    n = un % 2 * 2 + k
                    for kb in range(2):
                        if n + kb == 0:
                            continue
                        v = v1[:, n + kb - 1, m // 4 * P + 64 * b:m // 4 * P + 64 * b + 64]
                        last = nc.tensor.matmul(ps[r, SX + m % 2, n * P:(n + 1) * P], v, pt1[:, un % 2, (2 * k + kb) * P:(2 * k + kb + 1) * P],
                                                start=(kb == 0 or n == 0), stop=(kb == 1))
                if un % 4 == 3:
                    last.then_inc(o_ps, 1)

            for un in range(3):
                scores1(un)
            for un in range(U1):
                m = un // 4
                if m + 2 < KT:
                    strip_part("q", m + 2, un % 4, "C")
                if un % 4 == 0 and m + 1 < KT:
                    pe.wait_ge(rope_done, 3 + m)
                    pe.wait_ge(evac, OUT0["q"] + m + 2)
                    partners(3 + m, "perm1", q1[:, m + 1, :], SZ)
                if un + 3 < U1:
                    scores1(un + 3)
                pe.wait_ge(p_ready, un + 1)
                if un >= 2:
                    pe.wait_ge(pt_ready, un - 1)
                for k in range(4):
                    last = nc.tensor.transpose(ps[:, 2 + un % 2, k * P:(k + 1) * P], sm1[:, un % SLOTS, k // 2, k % 2 * P:(k % 2 + 1) * P], C("ident"))
                last.then_inc(pt_ps, 1)
                if un:
                    values1(un - 1)
            values1(U1 - 1)
            strips("wo", "A", XT["o"])
            for l in range(2):
                short_strip("proj1", l, 4, 2, "C", XT["p1"])
            mlp(1)
            def even(l):
                strip("even", l, l, "C", XT["even"])

            for l in range(8):
                even(l)
                if l == 1:
                    norm()
                    norm(acc2, SX)
            for m in range(8):
                even(8 + m)
                if m >= 2:
                    pe.wait_ge(rope_done, 10 + m - 1)
                partners(10 + m, "perm2", (q2 if m < 4 else k2)[:, m % 4, :], SX + m % 2)
                if m:
                    pe.wait_ge(evac, OUT0["even"] + 8 + m)
                    if m > 1:
                        pe.wait_ge(vt_done, 2 + m - 1)
                    transposes(ev[:, (m - 1) % 2, :], SZ).then_inc(vt_ps, 1)
            pe.wait_ge(evac, OUT0["even"] + 16)
            pe.wait_ge(vt_done, 2 + 7)
            transposes(ev[:, 1, :], SZ).then_inc(vt_ps, 1)
            with pe.Fori(0, 8 // RING) as i:
                for j in range(RING):
                    strip("even", 16 + RING * i + j, 16 + j, "C", XT["even"])
            pe.wait_ge(rope_done, 18)
            pe.wait_ge(vt_done, 10)

            def ret_scores(jp):
                if jp:
                    pe.wait_ge(rpv, jp)
                    pe.wait_ge(r_out, 2 * jp)
                transposes(k2[:, jp, :], SX).then_inc(rk_ps, 1)
                for b in range(2):
                    r = slice(64 * b, 64 * b + 64)
                    for n in range(NB):
                        cc = slice(n * P, (n + 1) * P)
                        last = nc.tensor.matmul(ps[:, (SZ, SY)[b], cc], k2[r, jp, cc], q2[r, jp, cc], start=True, stop=True)
                    last.then_inc(rs_ps, 1)

            def ret_keys_values(jp):
                pe.wait_ge(rk_sb, jp + 1)
                for n in range(NB - 1):
                    for b in range(2):
                        hh = 2 * jp + b
                        last = nc.tensor.matmul(ps[64 * b:64 * b + 64, SX, n * P:(n + 1) * P], k2[:, jp, n * P + 64 * b:n * P + 64 * b + 64],
                                                v2[:, n, hh * P:(hh + 1) * P], start=True, stop=True)
                last.then_inc(rkv_ps, 1)

            def ret_out(jp, b):
                hh, r = 2 * jp + b, slice(64 * b, 64 * b + 64)
                pe.wait_ge(rs_sb, hh + 1)
                pe.wait_ge(rpv, jp + 1)
                for n in range(NB):
                    cc = slice(n * P, (n + 1) * P)
                    last = nc.tensor.matmul(ps[:, (SZ, SY)[b], cc], v2[:, n, hh * P:(hh + 1) * P], ev[:, 1, cc], start=True, stop=(n == 0))
                    if n:
                        last = nc.tensor.matmul(ps[:, (SZ, SY)[b], cc], acc[r, cc], q2[r, jp, cc], start=False, stop=True)
                last.then_inc(r_ps, 1)

            for l in range(32):
                even(24 + l)
                jp = l // 8
                if l % 8 == 0:
                    ret_scores(jp)
                elif l % 8 == 2:
                    ret_keys_values(jp)
                elif l % 8 == 3:
                    ret_out(jp, 0)
                elif l % 8 == 4:
                    norm(sq[:, :])
                    ret_out(jp, 1)
                elif l % 8 == 5:
                    norm(sq[:, :])
            with pe.Fori(0, 2) as i:
                for j in range(8):
                    slot, bank = (S0["eout"] + j) % RING, (OUT0["eout"] + j // 2) % RING
                    pe.wait_ge(lo_ready, S0["eout"] + j + 1 + 8 * i)
                    if j % 2 == 0:
                        pe.wait_ge(evac, OUT0["eout"] + j // 2 - RING + 1 + 4 * i)
                    x, xt = ("A", XT["conv"]) if j % 2 == 0 else ("C", XT["ret"])
                    for k in range(KT):
                        if j < 2:
                            pe.wait_ge(x_lo, xt + k + 1)
                        last = product(slot, k, bank, X[x][0][:, k, :], X[x][1][:, k, :], j % 2 == 0 and k == 0, j % 2 == 1 and k == KT - 1)
                    last.then_inc(seg_done, 1)
            norm()
            for l in range(NSTR["odd"]):
                strip("odd", l, l, "A", XT["odd"], each=None if l else add_squares)
                if l == 1:
                    pe.wait_ge(evac, OUT0["odd"] + 1)
                    partners(18, "perm2", kr[:, :], SX)
                if l == 4:
                    norm()
            for l in range(NSTR["qb"]):
                short_strip("qb", l, 2, 3, "L", XT["lat"])
            norm()
            for l in range(NSTR["kvb"]):
                short_strip("kvb", l, 4, 2, "L", XT["lat"], 3)
                pe.wait_ge(evac, OUT0["kvb"])
                if l >= 2:
                    pe.wait_ge(rope_done, 18 + l)
                partners(19 + l, "perm2", qr[:, l, :], SX + l % 2)
            for m in range(8):
                pe.wait_ge(evac, OUT0["kvb"] + 8 + m + 1)
                if m >= 2:
                    pe.wait_ge(vt_done, 10 + m - 1)
                else:
                    pe.wait_ge(vt_done, 10)
                transposes(sm3[:, m % SLOTS, :], (SZ, NRM)[m % 2]).then_inc(vt_ps, 1)
            pe.wait_ge(evac, OUT0["mgate"])

            def scores3(un):
                hh, n = un // NB, un % NB
                r = slice(64 * (hh % 2), 64 * (hh % 2) + 64)
                pe.wait_ge(rope_done, 19 + hh // 2 + 1)
                if un >= 2:
                    pe.wait_ge(sc_out, U1 + un - 1)
                keys, qs = (n + 1) * P, slice(n * P, (n + 1) * P)
                nc.tensor.matmul(ps[:, un % 2, 0:keys], qn[:, hh, qs], kn[:, hh, 0:keys], start=True, stop=False)
                nc.tensor.matmul(ps[:, un % 2, 0:keys], qr[r, hh // 2, qs], kr[r, 0:keys], start=False, stop=True).then_inc(sc_ps, 1)

            def values3(un):
                hh, n = un // NB, un % NB
                pe.wait_ge(pt_ready, U1 + un + 1)
                if n == 0 and hh >= 2:
                    pe.wait_ge(o_out, hh - 1)
                for kb in range(n + 1):
                    last = nc.tensor.matmul(ps[:, SX + hh % 2, n * P:(n + 1) * P], v3[:, kb, hh * P:(hh + 1) * P], ev[:, un % 2, kb * P:(kb + 1) * P],
                                            start=(kb == 0), stop=(kb == n))
                if n == NB - 1:
                    last.then_inc(o_ps, 1)

            for un in range(3):
                scores3(un)
            pe.wait_ge(vt_done, 18)
            for un in range(U3):
                strip_part("mgate", un // 4, un % 4, "A")
                if un + 3 < U3:
                    scores3(un + 3)
                pe.wait_ge(p_ready, U1 + un + 1)
                if un >= 2:
                    pe.wait_ge(pt_ready, U1 + un - 1)
                transposes(sm3[:, un % SLOTS, :], 2 + un % 2, un % NB + 1).then_inc(pt_ps, 1)
                if un:
                    values3(un - 1)
            values3(U3 - 1)
            strips("oout", "C", XT["oo"])
            norm()

        @block.vector
        def _(dve):
            ch = Chain(dve, dve_ch)
            V = nc.vector
            asks, given, nrm = [0], [0], [0]
            xs = [XT["y"]]

            def t(k):
                return tab[:, k, :]

            dt, lr, th, y, r, mag, sn, cs, ar, ai, den, inv, nr, cr, ci, sci, nsci, t1, t2, m8 = (
                t(k) for k in (0, 1, 2, 3, 4, 5, 6, 8, 9, 10, 11, 12, 13, 14, 15, 16, 17, 18, 19, M8))
            lre, lim = lam[:, 0, :], lam[:, 1, :]
            dve.wait_ge(in_lam, 16)
            dve.wait_ge(tabs, 1)
            V.tensor_tensor(lr, lre, dt, ALU.mult)
            ch.link(V.tensor_tensor(th, lim, dt, ALU.mult))

            def reduce_angle(x, k):
                ch.link(V.tensor_scalar(k, x, 1.0 / TWO_PI, ROUND, ALU.mult, ALU.add))
                ch.link(V.tensor_scalar(k, k, ROUND, None, ALU.subtract))
                for part in (PI_A, PI_B, PI_C):
                    ch.link(V.scalar_tensor_tensor(x, k, -part, x, ALU.mult, ALU.add))

            reduce_angle(th, y)
            V.tensor_scalar(r, th, -PI_IN, PI_IN, ALU.max, ALU.min).then_inc(ang, 1)
            dve.wait_ge(tabs, 2)
            dve.wait_ge(in_cst, 32)
            V.tensor_tensor(ar, mag, cs, ALU.mult)
            V.tensor_tensor(ai, mag, sn, ALU.mult)
            V.tensor_tensor(t1, lre, lre, ALU.mult)
            ch.link(V.tensor_tensor(t2, lim, lim, ALU.mult))
            V.tensor_tensor(den, t1, t2, ALU.add)
            ch.link(V.tensor_scalar(nr, ar, 1.0, None, ALU.subtract))
            V.reciprocal(inv, den)
            V.tensor_tensor(t1, nr, lre, ALU.mult)
            ch.link(V.tensor_tensor(t2, ai, lim, ALU.mult))
            ch.link(V.tensor_tensor(cr, t1, t2, ALU.add))
            V.tensor_tensor(cr, cr, inv, ALU.mult)
            V.tensor_tensor(t1, ai, lre, ALU.mult)
            ch.link(V.tensor_tensor(t2, nr, lim, ALU.mult))
            ch.link(V.tensor_tensor(ci, t1, t2, ALU.subtract))
            ch.link(V.tensor_tensor(ci, ci, inv, ALU.mult))
            V.tensor_scalar(sci, ci, C("nsgn"), None, ALU.mult)
            V.tensor_scalar(nsci, ci, C("sgn"), None, ALU.mult)

            def cmul(o_r, o_i, a_r, a_i, b_r, b_i, s1, s2):
                V.tensor_tensor(s1, a_r, b_r, ALU.mult)
                ch.link(V.tensor_tensor(s2, a_i, b_i, ALU.mult))
                ch.link(V.tensor_tensor(o_r, s1, s2, ALU.subtract))
                V.tensor_tensor(s1, a_r, b_i, ALU.mult)
                ch.link(V.tensor_tensor(s2, a_i, b_r, ALU.mult))
                ch.link(V.tensor_tensor(o_i, s1, s2, ALU.add))

            V.memset(pwr[:, 0, :], 1.0)
            V.memset(pwi[:, 0, :], 0.0)
            V.tensor_copy(pwr[:, 1, :], ar)
            ch.link(V.tensor_copy(pwi[:, 1, :], ai))
            m = 1
            while m < ST:
                ab_r, ab_i = (over(pw[:, m, :], 1, m) for pw in (pwr, pwi))
                s1, s2 = (bt[:, k * 256:k * 256 + GR * m].rearrange("p (r g) -> p r g", r=m) for k in range(2))
                cmul(pwr[:, m + 1:2 * m + 1, :], pwi[:, m + 1:2 * m + 1, :], pwr[:, 1:m + 1, :], pwi[:, 1:m + 1, :], ab_r, ab_i, s1, s2)
                m *= 2
            ch.link(V.tensor_scalar(spi[:, :, :], pwi[:, :, :], C("nsgn"), None, ALU.mult))
            ch.link(V.tensor_tensor(m8, mag, mag, ALU.mult))
            ch.link(V.tensor_tensor(m8, m8, m8, ALU.mult))
            ch.link(V.tensor_tensor(m8, m8, m8, ALU.mult))
            dve.wait_ge(in_bc, 32)

            def per_group(x):
                return over(x, 2, GH)

            b1, b2 = by_group(bB[:, 0, :]), by_group(bB[:, 1, :])
            bb1, bb2, btg = by_group(bb[:, 0, :]), by_group(bb[:, 1, :]), by_group(bt[:, :])
            for o, x, z, s in ((bb1, b1, b2, sci), (bb2, b2, b1, nsci)):
                V.tensor_tensor(o, x, per_group(cr), ALU.mult)
                ch.link(V.tensor_tensor(btg, z, per_group(s), ALU.mult))
                ch.link(V.tensor_tensor(o, o, btg, ALU.add))
            V.memset(dec[:, :, 0:1], 0.0)
            V.tensor_scalar(bC[:, 0, :], bC[:, 0, :], C("sgn"), None, ALU.mult).then_inc(c_ready, 1)

            def gc(x):
                return x.rearrange("p (g c) -> p g c", g=SG)

            def scan(sl):
                gs = slice(sl * SG, (sl + 1) * SG)
                dve.wait_ge(v_sb, sl + 1)
                dve.wait_ge(w_ready, QUARTERS * sl // NSL + 1)
                V.tensor_tensor(gc(z1[:, :]), Wc[:, gs, :], gc(vsb[:, :]), ALU.mult)
                dve.wait_ge(vp, 32 * (sl + 1))
                ch.link(V.tensor_tensor(gc(z2[:, :]), Wsn[:, gs, :], gc(vsw), ALU.mult))
                ch.link(V.tensor_tensor(z1[:, :], z1[:, :], z2[:, :], ALU.add))
                dve.wait_ge(d_ready, sl + 1)
                V.tensor_tensor_scan(z2[:, :], dec[:, :, :].rearrange("p g c -> p (g c)"), z1[:, :], 0.0, ALU.mult, ALU.add).then_inc(z_ready, 1)

            def turn_back(sl):
                gs = slice(sl * SG, (sl + 1) * SG)
                dve.wait_ge(z_ready, sl + 1)
                V.tensor_tensor(gc(z1[:, :]), Wc[:, gs, :], gc(z2[:, :]), ALU.mult)
                dve.wait_ge(zp, 32 * (sl + 1))
                ch.link(V.tensor_tensor(gc(z3[:, :]), Wsn[:, gs, :], gc(zsw), ALU.mult))
                V.tensor_tensor(S[:, gs, 1:NC], gc(z1[:, :])[:, :, 0:NC - 1], gc(z3[:, :])[:, :, 0:NC - 1], ALU.subtract).then_inc(s_ready, 1)
                dve.wait_ge(s_ready, sl + 1)

            def inputs(sl):
                gs = slice(sl * SG, (sl + 1) * SG)
                if sl:
                    dve.wait_ge(e_ready, sl)
                if sl >= 2:
                    dve.wait_ge(et_ps, 2 * sl - 2)
                    dve.wait_ge(e_used, sl - 1)
                matrices(V, ch, E[:, sl % 2, :, :].rearrange("p g n -> p (g n)"), bt[:, :], pwr, spi, 0, bb1, bb2, gs, ALU.add).then_inc(e_ready, 1)

            def outputs(sl):
                if sl > 2:
                    dve.wait_ge(g_ready, sl - 2)
                if sl < 4:
                    dve.wait_ge(e_used, NSL + sl - 3)
                else:
                    dve.wait_ge(y_ps, sl - 3)
                output_matrices(V, ch, sl, bt[:, :]).then_inc(g_ready, 1)

            inputs(0)
            dve.wait_ge(ss_ps, 1)
            V.tensor_reduce(ssum[:, 0, :], ps[:, NRM, :].rearrange("p (g c) -> p c g", c=NC), AX_X, ALU.add).then_inc(ss_x, 1)
            V.memset(S[:, :, 0:1], 0.0)
            dve.wait_ge(std_x, 1)
            ch.link(V.reciprocal(ssum[:, 2, :], ssum[:, 1, :]))
            dve.wait_ge(u_gain, 2)
            V.tensor_tensor(u[:, :, :], u[:, :, :], over(ssum[:, 2, :], 1, GR), ALU.mult).then_inc(u_ready, 1)
            inputs(1)
            dve.wait_ge(in_d, 48)
            ch.link(V.tensor_tensor(d16[:, 0, :], d16[:, 0, :], d16[:, 1, :], ALU.mult))
            skip = d16[:, 0, :].rearrange("p (b h g) -> p b h g", b=2, h=GH)
            for sl in range(NSL):
                if sl in (NSL // 2, NSL - 1):
                    b = int(sl == NSL - 1)
                    dve.wait_ge(k_out, b + 1)
                    V.tensor_tensor(kst[0:GH, b, :, :], kst[0:GH, b, :, :], skip[:, b, :, :], ALU.add).then_inc(kst_ready, 1)
                scan(sl)
                if sl + 2 < NSL:
                    inputs(sl + 2)
                elif sl == NSL - 1:
                    outputs(2)
                turn_back(sl)
            def ask(ins):
                ins.then_inc(to_act, 1)
                asks[0] += 1

            def answered():
                given[0] += 1
                dve.wait_ge(to_dve, given[0])

            def out_ready(name, o, ends=1):
                dve.wait_ge(seg_done, SEG0[name] + ends * (o + 1))

            def bank(name, o):
                return ps[:, (OUT0[name] + o) % RING, :]

            def low(dst, m, src, g=None):
                xs[0] += 1
                dve.wait_ge(x_hi, xs[0])
                hi, lo = X[dst][0][:, m, :].bitcast(F32), X[dst][1][:, m, :]
                if g is None:
                    V.tensor_tensor(lo, src, hi, ALU.subtract).then_inc(x_lo, 1)
                else:
                    V.scalar_tensor_tensor(lo, src, g, hi, ALU.mult, ALU.subtract).then_inc(x_lo, 1)

            adds = [0]

            def start_sum():
                V.memset(acc[:, :], 0.0).then_inc(acc_add, 1)
                adds[0] += 1

            def add_square(last):
                dve.wait_ge(acc_add, adds[0])
                V.tensor_tensor(acc[:, :], acc[:, :], sq[:, :], ALU.add).then_inc(ssq_ready if last else acc_add, 1)
                adds[0] += not last

            def root(dst=rstd):
                nrm[0] += 1
                dve.wait_ge(nrm_std, nrm[0])
                ch.link(V.reciprocal(dst[:, :], std[:, :]))

            def scaled(name, o, dst, ends=1, at=None, by=None):
                out_ready(name, o, ends)
                V.tensor_tensor(dst, bank(name, o) if at is None else ps[:, at, :], (rstd if by is None else by)[:, :], ALU.mult).then_inc(evac, 1)

            def rotate(n, src, dst, part_bank, cos, sin, s1, s2):
                V.tensor_tensor(s1, src, cos, ALU.mult)
                dve.wait_ge(rope_ps, n + 1)
                ch.link(V.tensor_tensor(s2, part_bank, sin, ALU.mult))
                V.tensor_tensor(dst, s1, s2, ALU.add).then_inc(rope_done, 1)

            for sl in range(3, NSL):
                outputs(sl)
            dve.wait_ge(g_ready, NSL - 2)
            for m in range(4):
                out_ready("proj0", m)
                V.tensor_copy(ple[:, m, :], ps[:, NRM + m, :]).then_inc(evac, 1)
            dve.wait_ge(in_pos, 16)
            ch.link(V.tensor_copy(rsin[:, :], rcos[:, :].bitcast(I32)))
            ch.link(V.tensor_scalar(rsin[:, :], rsin[:, :], C("inv"), None, ALU.mult))
            reduce_angle(rsin[:, :], rcos[:, :])
            ask(V.tensor_scalar(rsin[:, :], rsin[:, :], -PI_IN, PI_IN, ALU.max, ALU.min))
            for m in range(4, 6):
                out_ready("proj0", m)
                V.tensor_copy(ple[:, m, :], bank("proj0", m)).then_inc(evac, 1)
            for m in range(KT):
                if m >= 6:
                    out_ready("proj0", m)
                    V.tensor_copy(ple[:, m, :], bank("proj0", m)).then_inc(evac, 1)
                xs[0] += 1
                dve.wait_ge(x_hi, xs[0])
                V.tensor_tensor(X["A"][1][:, m, :].rearrange("p (c t) -> p c t", t=ST), yfm[:, m, :, :].rearrange("p t c -> p c t"),
                                X["A"][0][:, m, :].bitcast(F32).rearrange("p (c t) -> p c t", t=ST), ALU.subtract).then_inc(x_lo, 1)
            answered()
            start_sum()
            for m in range(KT + 1):
                if m == 0:
                    dve.wait_ge(in_h, 32)
                if m:
                    low("B", m - 1, h[:, m - 1, :], gain("mlp0", m - 1))
                    answered()
                    add_square(m == KT)
                if m < KT:
                    answered()
                    out_ready("glu", 2 * m + 1)
                    V.tensor_tensor(ev[:, 0, :], bank("glu", 2 * m + 1), sg[:, :], ALU.mult).then_inc(evac, 2)
                if m < KT:
                    dve.wait_ge(evac, OUT0["glu"] + 2 * m + 2)
                    ask(V.tensor_tensor(h[:, m, :], h[:, m, :], ev[:, 0, :], ALU.add))
                    dve.wait_ge(to_act, asks[0])

            def mlp(layer):
                root()
                for kind, c in (("up", 0), ("up", 1), ("down", 0), ("up", 2), ("down", 1), ("up", 3), ("down", 2), ("down", 3)):
                    name = f"{kind}{layer}_{c}"
                    if kind == "up":
                        x = X["AC"[c % 2]]
                        with dve.Fori(0, 8 // RING) as i:
                            for j in range(RING):
                                o = RING * i + j
                                dve.wait_ge(seg_done, SEG0[name] + o + 1)
                                V.scalar_tensor_tensor(ev[:, 0, :], bank(name, j), 0.0, rstd[:, :], ALU.max, ALU.mult).then_inc(evac, 1)
                                dve.wait_ge(x_hi, xs[0] + o + 1)
                                V.tensor_tensor(x[1][:, o, :], sg[:, :], x[0][:, o, :].bitcast(F32), ALU.subtract).then_inc(x_lo, 1)
                        xs[0] += 8
                    elif c < CHUNKS - 1:
                        with dve.Fori(0, 8 // RING) as i:
                            for j in range(RING):
                                o = RING * i + j
                                dve.wait_ge(seg_done, SEG0[name] + o + 1)
                                V.tensor_tensor(h[:, o, :], bank(name, j), h[:, o, :], ALU.add).then_inc(evac, 1)
                    else:
                        dve.wait_ge(evac, OUT0[name])
                        start_sum()
                        for m in range(KT):
                            out_ready(name, m)
                            V.tensor_tensor(h[:, m, :], bank(name, m), h[:, m, :], ALU.add).then_inc(evac, 1)
                            dve.wait_ge(evac, OUT0[name] + m + 1)
                            low("B", m, h[:, m, :], gain(f"ple{layer}", m))
                            answered()
                            add_square(m == KT - 1)

            def gate(layer):
                name = f"gate{layer}"
                if layer == 1:
                    ch.link(V.tensor_tensor(finpre, gp[:, GC["fin"]], gp[:, GC["pre0"]], ALU.mult))
                root()
                start_sum()
                if layer == 1:
                    ch.link(V.memset(acc2, 0.0))

                def finish(m):
                    if layer == 0:
                        low("A", m, h[:, m, :], gain("kvn", m))
                        low("C", m, h[:, m, :], gain("mix1", m))
                        answered()
                        add_square(m == KT - 1)
                    else:
                        low("C", m, h[:, m, :], finpre[:, m:m + 1])
                        answered()
                        add_square(m == KT - 1)
                        last = V.tensor_tensor(acc2, acc2, cy[:, :], ALU.add)
                        if m < KT - 1:
                            ch.link(last)
                        else:
                            last.then_inc(ssq_ready, 1)

                for m in range(KT + 1):
                    if m < KT:
                        scaled(name, m, ev[:, 0, :])
                    if m:
                        finish(m - 1)
                    if m < KT:
                        answered()
                        ch.link(V.tensor_tensor(ev[:, 1, :], sg[:, :], ple[:, m, :], ALU.mult))
                        ask(V.tensor_tensor(h[:, m, :], h[:, m, :], ev[:, 1, :], ALU.add))
                        dve.wait_ge(to_act, asks[0])

            mlp(0)
            gate(0)
            root()
            dve.wait_ge(seg_done, SEG0["kv"])
            V.memset(k1[:, :, 0:P], 0.0)
            for o in range(4):
                scaled("kv", o, kv1[:, o, :])
            scaled("q", 0, q1[:, 0, :])
            dve.wait_ge(evac, OUT0["q"] + 1)
            dve.wait_ge(in_a1, 32)
            rc, rs = rope1[:, 0, :], rope1[:, 1, :]
            for j in range(2):
                rotate(j, kv1[:, j, :], k1[:, j, P:], ps[:, SX + j, :], rc, rs, ev[:, 0, :], ev[:, 1, :])
                dve.wait_ge(rope_done, j + 1)

            def rotate_q(m):
                rotate(2 + m, q1[:, m, :], q1[:, m, :], ps[:, SZ, :], rc, rs, ev[:, 0, :], ev[:, 1, :])

            def masked_max(un):
                q0 = 16 * (un % SLOTS)
                mx, mm, ng = cols[:, q0:q0 + 2], cols[:, q0 + 2:q0 + 4], cols[:, q0 + 4:q0 + 6]
                msk = msk1[:, 0:2, :] if un % 2 == 0 else msk1[:, 1:3, :]
                dve.wait_ge(sc_ps, un + 1)
                V.tensor_tensor(sm1[:, un % SLOTS, :, :], ps[:, un % 2, :].rearrange("p (n k) -> p n k", n=2), msk, ALU.add).then_inc(sc_out, 1)
                dve.wait_ge(sc_out, un + 1)
                ch.link(V.tensor_reduce(mx, sm1[:, un % SLOTS, :, :], AX_X, ALU.max))
                ch.link(V.tensor_scalar(mm, mx, float(HD) ** -0.5, gain("sink", un // 4 * 2 + un // 2 % 2), ALU.mult, ALU.max))
                ask(V.tensor_scalar(ng, mm, -1.0, None, ALU.mult))

            def normed(un):
                q0 = 16 * (un % SLOTS)
                rsum, es, dn, rc_ = (cols[:, q0 + k:q0 + k + 2] for k in (6, 8, 10, 12))
                answered()
                ch.link(V.tensor_tensor(dn, rsum, es, ALU.add))
                ch.link(V.reciprocal(rc_, dn))
                V.tensor_scalar(sm1[:, un % SLOTS, 0, :], sm1[:, un % SLOTS, 0, :], rc_[:, 0:1], None, ALU.mult)
                V.tensor_scalar(sm1[:, un % SLOTS, 1, :], sm1[:, un % SLOTS, 1, :], rc_[:, 1:2], None, ALU.mult).then_inc(p_ready, 1)

            rotate_q(0)
            scaled("q", 1, q1[:, 1, :], at=NRM)
            masked_max(0)
            masked_max(1)
            for un in range(U1):
                if un % 4 == 1 and un // 4 + 1 < KT:
                    dve.wait_ge(rope_done, 3 + un // 4)
                    rotate_q(un // 4 + 1)
                if un + 2 < U1:
                    if un + 2 >= SLOTS:
                        dve.wait_ge(pt_ps, un + 3 - SLOTS)
                    masked_max(un + 2)
                normed(un)
                if un % 4 == 2 and un > 4:
                    low("A", un // 4 - 1, ps[:, SX + (un // 4 - 1) % 2, :])
                if un % 4 == 3 and un // 4 + 2 < KT:
                    scaled("q", un // 4 + 2, q1[:, un // 4 + 2, :], at=NRM)
            low("A", KT - 1, ps[:, SX + (KT - 1) % 2, :])
            dve.wait_ge(in_p, 48)
            for k in range(2):
                low("C", k, (sq, acc)[k][:, :])
            dve.wait_ge(x_lo, xs[0])
            start_sum()
            for m in range(KT):
                out_ready("wo", m)
                V.tensor_tensor(h[:, m, :], bank("wo", m), h[:, m, :], ALU.add).then_inc(evac, 1)
                dve.wait_ge(evac, OUT0["wo"] + m + 1)
                low("B", m, h[:, m, :], gain("mlp1", m))
                answered()
                add_square(m == KT - 1)
            for o in range(8):
                out_ready("proj1", o)
                V.tensor_copy(ple[:, o, :], bank("proj1", o)).then_inc(evac, 1)
            mlp(1)
            gate(1)
            root()
            nrm[0] += 1
            dve.wait_ge(nrm_ps, nrm[0])
            ch.link(V.tensor_tensor(sq[:, :], ps[:, SX, :], rstd[:, :], ALU.mult))
            V.tensor_copy(sgr[:, KT - 1, :], rstd[:, :])
            ask(V.tensor_tensor(sq[:, :], sq[:, :], rstd[:, :], ALU.mult))
            dve.wait_ge(nrm_std, nrm[0])
            ch.link(V.reciprocal(sq[:, :], std[:, :]))
            ch.link(V.tensor_tensor(rstd[:, :], rstd[:, :], sq[:, :], ALU.mult))
            for o in range(8):
                scaled("even", o, (q2 if o < 4 else k2)[:, o % 4, :])
            for m in range(KT):
                last = V.scalar_tensor_tensor(h[:, m, :], h[:, m, :], gain("fin", m), sgr[:, KT - 1, :], ALU.mult, ALU.mult)
            ch.link(last)
            V.memset(cu[:, 0:2], 0.0)
            for m in range(8):
                if m >= 2:
                    dve.wait_ge(vt_ps, 2 + m - 1)
                scaled("even", 8 + m, ev[:, m % 2, :])
                qk = (q2 if m < 4 else k2)[:, m % 4, :]
                if m == 0:
                    dve.wait_ge(evac, OUT0["even"] + 8)
                rotate(10 + m, qk, qk, ps[:, SX + m % 2, :], rcos[:, :], rsin[:, :], acc[:, :], cy[:, :])
                dve.wait_ge(rope_done, 10 + m + 1)
            for m in range(8):
                if m < 2:
                    dve.wait_ge(vt_ps, 2 + 7 + m)
                else:
                    dve.wait_ge(silu_done, m - 1)
                scaled("even", 16 + m, ev[:, m % 2, :])
            dve.wait_ge(silu_done, 8)
            E0 = OUT0["even"]
            dve.wait_ge(in_rt, 32)

            def by_chunk(x):
                return x.rearrange("p (n k) -> p n k", n=NB)

            def masked_scores(jp, b):
                hh = 2 * jp + b
                if hh:
                    dve.wait_ge(r_ps, hh)
                V.tensor_tensor(by_chunk(ev[:, 1, :]), by_chunk(ps[:, (SZ, SY)[b], :]), over(rmask[:, hh, :], 1, NB), ALU.mult).then_inc(rs_sb, 1)

            def decayed(jp):
                dve.wait_ge(rk_ps, jp + 1)
                dve.wait_ge(rs_ps, 2 * jp + 2)
                for b in range(2):
                    cc = slice(64 * b, 64 * b + 64)
                    last = V.tensor_scalar(by_chunk(k2[:, jp, :])[:, :, cc], by_chunk(ps[:, SX, :])[:, :, cc],
                                           cst[:, CC["zeta"].start + 2 * jp + b:CC["zeta"].start + 2 * jp + b + 1], None, ALU.mult)
                last.then_inc(rk_sb, 1)
                V.tensor_tensor(by_chunk(q2[:, jp, :]), by_chunk(q2[:, jp, :]), over(xi[:, jp, :], 1, NB), ALU.mult)
                masked_scores(jp, 0)

            def states(jp):
                dve.wait_ge(rkv_ps, jp + 1)
                ch.link(V.tensor_copy(acc[:, P:2 * P], ps[:, SX, 0:P]))
                gam = cst[:, CC["gam"].start + jp:CC["gam"].start + jp + 1]
                for n in range(2, NB):
                    last = V.scalar_tensor_tensor(acc[:, n * P:(n + 1) * P], acc[:, (n - 1) * P:n * P], gam,
                                                  ps[:, SX, (n - 1) * P:n * P], ALU.mult, ALU.add)
                    if n < NB - 1:
                        ch.link(last)
                last.then_inc(rpv, 1)

            def head_out(jp, b):
                hh = 2 * jp + b
                nrm[0] += 1
                dve.wait_ge(nrm_std, nrm[0])
                ch.link(V.reciprocal(std[:, :], std[:, :]))
                ch.link(V.tensor_tensor(std[:, :], ps[:, (SZ, SY)[b], :], std[:, :], ALU.mult))
                V.scalar_tensor_tensor(sgr[:, hh, :], std[:, :], gain("gn", hh), sgr[:, hh, :], ALU.mult, ALU.mult).then_inc(r_out, 1)

            for k in range(8):
                o, jp = 24 + 4 * k, k // 2
                scaled("even", o, cu[:, 2:])
                scaled("even", o + 1, ev[:, 0, :])
                dve.wait_ge(evac, E0 + o + 2)
                ask(V.tensor_tensor(cu[:, 2:], cu[:, 2:], ev[:, 0, :], ALU.mult))
                if k % 2 == 0:
                    decayed(jp)
                else:
                    head_out(jp, 0)
                dve.wait_ge(to_act, asks[0])
                scaled("even", o + 2, ev[:, 0, :])
                answered()
                ch.link(V.scalar_tensor_tensor(cy[:, :], cu[:, 1:TOK + 1], gain("cw", 8 + k), cy[:, :], ALU.mult, ALU.add))
                ch.link(V.scalar_tensor_tensor(cy[:, :], cu[:, 2:TOK + 2], gain("cw", 16 + k), cy[:, :], ALU.mult, ALU.add))
                ch.link(V.tensor_tensor(cy[:, :], cy[:, :], ev[:, 0, :], ALU.mult))
                if k % 2 == 0:
                    states(jp)
                else:
                    head_out(jp, 1)
                scaled("even", o + 3, ev[:, 0, :])
                answered()
                ask(V.tensor_tensor(cy[:, :], cy[:, :], sg[:, :], ALU.mult))
                dve.wait_ge(to_act, asks[0])
                low("A", k, cy[:, :])
                if k % 2 == 0:
                    masked_scores(jp, 1)
            dve.wait_ge(r_out, RH)
            for hh in range(RH):
                low("C", hh, sgr[:, hh, :])

            def post(name, buf, g, ends):
                start_sum()
                for m in range(KT):
                    out_ready(name, m, ends)
                    V.tensor_copy(buf[:, m, :], bank(name, m)).then_inc(evac, 1)
                    answered()
                    add_square(m == KT - 1)
                root()
                for m in range(KT + 1):
                    if m < KT:
                        if m >= 2 and name == "eout":
                            dve.wait_ge(to_act, asks[0] - 1)
                        elif m >= 2:
                            dve.wait_ge(fin, m - 1)
                        ch.link(V.scalar_tensor_tensor(ev[:, m % 2, :], buf[:, m, :], gain(g, m), rstd[:, :], ALU.mult, ALU.mult))
                        last = V.tensor_tensor(h[:, m, :], h[:, m, :], ev[:, m % 2, :], ALU.add)
                        if name == "eout":
                            ask(last)
                        else:
                            last.then_inc(fin, 1)
                    if m and name == "eout":
                        dve.wait_ge(to_act, asks[0] - (m < KT))
                        low("A", m - 1, h[:, m - 1, :], gain("pre1", m - 1))

            post("eout", ybuf, "post0", 2)
            root()
            scaled("odd", 0, kr[:, :])
            start_sum()
            for m in range(5):
                scaled("odd", 1 + m, kn[:, m, :])
                answered()
                add_square(m in (2, 4))
                low("L", m, kn[:, m, :], gain("qa", m) if m < 3 else gain("kva", m - 3))
                if m == 1:
                    rotate(18, kr[:, :], kr[:, :], ps[:, SX, :], rcos[:, :], rsin[:, :], ev[:, 0, :], ev[:, 1, :])
                if m == 2:
                    dve.wait_ge(nrm_ps, nrm[0] + 1)
                    start_sum()
            dve.wait_ge(rope_done, 19)
            root(sg)
            for o in range(12):
                scaled("qb", o, qn[:, o, :] if o < 8 else qr[:, o - 8, :], by=sg)
            root(sq)
            dve.wait_ge(x_lo, xs[0])
            for l in range(NSTR["kvb"]):
                for q in range(4):
                    o = 4 * l + q
                    if o < 8:
                        scaled("kvb", o, kn[:, o, :], by=sq)
                    else:
                        if o >= 8 + SLOTS:
                            dve.wait_ge(vt_ps, 10 + o - 8 - SLOTS + 1)
                        scaled("kvb", o, sm3[:, o % SLOTS, :], by=sq)
                rotate(19 + l, qr[:, l, :], qr[:, l, :], ps[:, SX + l % 2, :], rcos[:, :], rsin[:, :], ev[:, 0, :], ev[:, 1, :])
                dve.wait_ge(rope_done, 20 + l)
            dve.wait_ge(evac, OUT0["mgate"])
            dve.wait_ge(vt_ps, 18)
            dve.wait_ge(in_cm, 16)

            def masked_max3(un):
                n, q0 = (un % NB + 1) * P, 8 * (un % SLOTS)
                dve.wait_ge(sc_ps, U1 + un + 1)
                V.tensor_tensor(sm3[:, un % SLOTS, 0:n], ps[:, un % 2, 0:n], cm[:, TOK - n:TOK], ALU.add).then_inc(sc_out, 1)
                dve.wait_ge(sc_out, U1 + un + 1)
                ch.link(V.tensor_reduce(cols[:, q0:q0 + 1], sm3[:, un % SLOTS, 0:n], AX_X, ALU.max))
                ask(V.tensor_scalar(cols[:, q0 + 1:q0 + 2], cols[:, q0:q0 + 1], -MSCALE, None, ALU.mult))

            def normed3(un):
                n, q0 = (un % NB + 1) * P, 8 * (un % SLOTS)
                answered()
                ch.link(V.reciprocal(cols[:, q0 + 3:q0 + 4], cols[:, q0 + 2:q0 + 3]))
                V.tensor_scalar(sm3[:, un % SLOTS, 0:n], sm3[:, un % SLOTS, 0:n], cols[:, q0 + 3:q0 + 4], None, ALU.mult).then_inc(p_ready, 1)

            def gated(hh):
                dve.wait_ge(o_ps, KT + hh + 1)
                dve.wait_ge(silu_done, 8 + hh + 1)
                V.tensor_tensor(sg[:, :], ps[:, SX + hh % 2, :], sg3[:, hh, :], ALU.mult).then_inc(o_out, 1)

            masked_max3(0)
            masked_max3(1)
            for un in range(U3):
                if un + 2 < U3:
                    if un + 2 >= SLOTS:
                        dve.wait_ge(pt_ps, U1 + un + 3 - SLOTS)
                    masked_max3(un + 2)
                normed3(un)
                if un % NB == 1 and un > NB:
                    gated(un // NB - 1)
                if un % NB == 2 and un > NB:
                    low("C", un // NB - 1, sg[:, :])
                if un % NB == NB - 1:
                    scaled("mgate", un // NB, sg3[:, un // NB, :], at=NRM)
            gated(MH - 1)
            dve.wait_ge(o_out, MH)
            low("C", MH - 1, sg[:, :])
            post("oout", ybuf3, "post1", 1)
            assert xs[0] == XT["oo"] + 8
        return nc


def constants():
    f = np.float32
    cst = np.zeros((P, NCC), f)
    cst[:, CC["ident"]] = np.eye(P)
    cst[:, CC["ones"]] = 1.0
    m1, m2 = (np.zeros((P, P), f) for _ in range(2))
    for b in (0, 64):
        for d in range(8):
            m1[b + d + 8, b + d], m1[b + d, b + d + 8] = -1.0, 1.0
        for d in range(32):
            m2[b + d + 32, b + d], m2[b + d, b + d + 32] = -1.0, 1.0
    cst[:, CC["perm1"]], cst[:, CC["perm2"]] = m1, m2
    cst[:, CC["eps"]] = EPS
    cst[:, CC["halfpi"]] = np.pi / 2
    cst[:, CC["sgn"]] = np.where(np.arange(P) < 64, 1.0, -1.0)[:, None]
    cst[:, CC["nsgn"]] = -cst[:, CC["sgn"]]
    inv = (f(10000.0) ** (-np.arange(0, MR, 2, dtype=f) / f(MR))).astype(f)
    cst[:, CC["inv"]] = inv[np.arange(P) % 32][:, None]
    lg = np.log1p(-np.exp2(-5.0 - np.arange(RH)))
    k = np.arange(P)
    cst[:, CC["zeta"]] = np.exp(lg[None, :] * (P - 1.0 - k[:, None])) * RDK ** -0.5
    for j in range(4):
        cst[:, CC["gam"].start + j] = np.exp(lg[2 * j + (k >= 64)] * P)
    rel = k[None, :] - k[:, None]
    rmask = np.where(rel[:, None, :] >= 0, np.exp(lg[None, :, None] * np.maximum(rel, 0)[:, None, :]), 0.0) * RDK ** -0.5
    xi = np.stack([np.exp(lg[2 * j + (k >= 64)][:, None] * (k[None, :] + 1.0)) for j in range(4)], 1)
    inv1 = (f(500000.0) ** (-np.arange(0, 16, 2, dtype=f) / f(16))).astype(f)
    ang = (np.arange(TOK, dtype=f)[None, :] * inv1[:, None]).astype(f)
    rope1 = np.zeros((P, 2, TOK), f)
    rope1[:, 0] = 1.0
    for b in (0, 64):
        for q in (0, 8):
            rope1[b + q:b + q + 8, 0], rope1[b + q:b + q + 8, 1] = np.cos(ang), np.sin(ang)
    kj, qi = np.arange(256)[None, :], k[:, None] + P
    band = (kj <= qi) & (qi - kj < WIN)
    gen, first = np.where(band, 0.0, NEG), np.where(band & (kj >= P), 0.0, NEG)
    cm = np.zeros((P, TOK), f)
    cm[:, TOK - P:] = np.where(k[None, :] <= k[:, None], 0.0, NEG)
    blk = (k[:, None] // GH == k[None, :] // GH).astype(f)
    diag = np.tile(np.repeat(np.eye(GH, dtype=f), GR // 2, 1), (1, 2))
    return {"cst": cst, "rmask": rmask.astype(f), "xi": xi.astype(f), "rope1": rope1, "msk1": np.stack([first, gen, gen], 1).astype(f),
            "cm": cm, "blk": blk}, diag


def strips_of(w, k_tiles=KT):
    K, M = w.shape
    per = KT // k_tiles
    b = w.reshape(k_tiles, P, M // P // per, per, P).transpose(2, 1, 3, 0, 4).reshape(M // P // per, P, per * k_tiles * P)
    return b if b.shape[2] == D else np.concatenate([b, np.zeros(b.shape[:2] + (D - b.shape[2],), w.dtype)], 2)


def layouts(v):
    consts, diag = constants()
    heads = [(2 * j + b) * GQA + g for j in range(2) for g in range(GQA) for b in range(2)]
    hc = (np.array(heads)[:, None] * HD + np.arange(HD)[None, :]).ravel()
    w = {"proj0": strips_of(v["w_ple_proj"][0], 2), "proj1": strips_of(v["w_ple_proj"][1], 2)}
    glu = strips_of(v["ssm_w_glu"][0])
    w["glu"] = np.stack([glu[8:], glu[:8]], 1).reshape(16, P, D)
    for i in range(2):
        for c in range(CHUNKS):
            w[f"up{i}_{c}"] = strips_of(v["w_up"][i][:, c * D:(c + 1) * D])
            w[f"down{i}_{c}"] = strips_of(v["w_down"][i][c * D:(c + 1) * D])
        w[f"gate{i}"] = strips_of(v["w_ple_gate"][i])
    w["kv"] = np.concatenate([strips_of(v["w_k"]), strips_of(v["w_v"])])
    w["q"] = strips_of(v["w_q"][0][:, hc])
    w["wo"] = strips_of(v["w_o"][0][hc])
    ein = strips_of(v["even_w_in_2"][0])
    w["even"] = np.concatenate([ein[:24], np.stack([ein[32:40], ein[40:48], ein[24:32], ein[48:56]], 1).reshape(32, P, D)])
    eo = v["even_w_out_2"][0]
    w["eout"] = np.stack([strips_of(eo[D:]), strips_of(eo[:D])], 1).reshape(16, P, D)
    oi = v["odd_w_in_2"][0]
    kr = oi[:, QL + KL:QL + KL + MR]
    w["odd"] = np.concatenate([strips_of(np.concatenate([kr, kr], 1)), strips_of(oi[:, :QL + KL])])
    w["mgate"] = strips_of(oi[:, QL + KL + MR:])
    qb = v["w_qb_2"][0].reshape(QL, MH, MN + MR)
    qb = np.concatenate([qb[:, :, :MN].reshape(QL, -1), qb[:, :, MN:].reshape(QL, -1)], 1)
    w["qb"] = strips_of(qb, 3)
    kvb = v["w_kvb_2"][0].reshape(KL, MH, 2 * P)
    w["kvb"] = strips_of(np.concatenate([kvb[:, :, :P].reshape(KL, -1), kvb[:, :, P:].reshape(KL, -1)], 1), 2)
    w["oout"] = strips_of(v["odd_w_out_2"][0])

    def cols(x):
        return x.reshape(-1, P).T

    g = {"mix1": v["norm_mix"][1], "kvn": v["kv_norm"], "mlp0": v["norm_mlp"][0], "mlp1": v["norm_mlp"][1], "ple0": v["norm_ple"][0],
         "ple1": v["norm_ple"][1], "fin": v["norm_final"], "pre0": v["pre_norm_2"][0], "pre1": v["pre_norm_2"][1],
         "post0": v["post_norm_2"][0], "post1": v["post_norm_2"][1], "gn": v["ret_gn_2"][0], "qa": v["q_a_norm_2"][0],
         "kva": v["kv_a_norm_2"][0], "cw": v["even_conv_w_2"][0].reshape(-1), "cb": v["even_conv_b_2"][0]}
    gpack = np.concatenate([cols(g[n]) if n != "sink" else np.broadcast_to(v["attn_sinks"][0][heads][None, :], (P, 16)) for n in GC], 1)
    x = v["x"][0]
    xt = x.reshape(NC, ST, GR, GH)[:, ::-1]
    dup = lambda z: np.concatenate([z, z], 0)
    lam = np.stack([dup(v["ssm_lambda_re"][0].T), dup(v["ssm_lambda_im"][0].T),
                    np.broadcast_to(v["ssm_log_dt"][0][None, :], (P, GR))], 1)
    br, bi = (v[n][0].transpose(1, 0, 2).reshape(NST, -1) for n in ("ssm_b_re", "ssm_b_im"))
    cr, ci = (v[n][0].transpose(2, 0, 1).reshape(NST, -1) for n in ("ssm_c_re", "ssm_c_im"))
    bcp = np.stack([np.concatenate(z, 0) for z in ((br, bi), (bi, br), (cr, ci), (ci, cr))], 1)
    d16 = np.stack([np.broadcast_to(v["ssm_d"][0].reshape(2, GR // 2, GH).transpose(0, 2, 1).reshape(1, D), (GH, D)), diag], 1)
    return consts | {
        "w": np.concatenate([w[n] for n, _, _ in PHASES]), "gp": gpack, "lam": lam, "bc": bcp, "d16": d16,
        "gch": np.tile(v["norm_mix"][0].reshape(GR, GH).T, (ST, 1)),
        "xch": xt.transpose(1, 3, 2, 0).reshape(P, GR, NC),
        "xfm": x.T.reshape(KT, P, TOK).transpose(1, 0, 2),
        "p": v["p"][:, 0].transpose(0, 2, 1).reshape(2, 2, P, TOK).transpose(0, 2, 1, 3),
        "pos": v["positions_2"][0],
    }


def kernel(**inputs):
    import concourse.bacc as bacc
    from concourse.bass_utils import run_bass_kernel_spmd as run

    arrays = {k: np.ascontiguousarray(x) for k, x in layouts({k: np.asarray(x) for k, x in inputs.items()}).items()}
    nc = bacc.Bacc("TRN2", target_bir_lowering=False, num_devices=1)
    a = {k: nc.dram_tensor("in_" + k, x.shape, mybir.dt.from_np(x.dtype), kind="ExternalInput").ap() for k, x in arrays.items()}
    a["out"] = nc.dram_tensor("out", (KT, P, TOK), F32, kind="ExternalOutput").ap()
    program(nc, a)
    arrays = {"in_" + k: x for k, x in arrays.items()}
    got = run(nc, [arrays], core_ids=[0]).results[0]["out"]
    return np.ascontiguousarray(got.reshape(D, TOK).T)[None]
```
